# Optimizing a Trainium2 kernel written in Bass

```python
import math
import jax
import jax.numpy as jnp
from jax import lax
import numpy as np

D_MODEL = 1024
BATCH = 1
SEQ = 256
DEPTH = 2

N_MEM = 256
N_AB_LAYERS = (DEPTH + 1) // 2
N_C_LAYERS = DEPTH // 2

MIX_HALF = D_MODEL // 2
HG_DK = 128
HG_DV = 128
HG_HEADS = MIX_HALF // HG_DK
HG_WIDTH = HG_HEADS * HG_DK
HG_CHUNK = 64
HG_MASK_LOG = -1e30
HG_EXP_CLIP = 60.0

RW_N = 64
RW_HEADS = MIX_HALF // RW_N
RW_WIDTH = RW_HEADS * RW_N
RW_DECAY_LORA = 32
RW_A_LORA = 32
RW_GATE_LORA = 96
RW_GN_EPS = 64e-5

HG_COLS = 4 * HG_WIDTH
RW_COLS = 3 * RW_WIDTH + RW_DECAY_LORA + RW_A_LORA + RW_GATE_LORA
AB_IN = HG_COLS + RW_COLS

S5_GROUP = 16
S5_GROUPS = D_MODEL // S5_GROUP
S5_STATE = 64
S5_DT_MIN = 1e-3
S5_DT_MAX = 1e-1

XA_HEADS = 4
XA_HEAD_DIM = D_MODEL // XA_HEADS

D_FF = 256 * ((8 * D_MODEL // 3 + 255) // 256)
N_EXPERTS = 8
TOP_K = 2
NORM_EPS = 1e-6

kernel_name = 'hybrid_hgrn2_rwkv7_s5_moe_trunk'

def rmsnorm(x, g, eps=NORM_EPS):
    xf = x.astype(jnp.float32)
    y = xf * lax.rsqrt(jnp.mean(xf * xf, axis=-1, keepdims=True) + eps)
    return (y * g.astype(jnp.float32)).astype(x.dtype)

def token_shift(t):
    return jnp.pad(t, ((0, 0), (1, 0), (0, 0)))[:, :-1]

def swiglu(t, w13, w2):
    gate, up = jnp.split(t @ w13, 2, axis=-1)
    return (jax.nn.silu(gate) * up) @ w2

def hgrn2_lower_bounds(logits):
    p = jax.nn.softmax(logits.astype(jnp.float32), axis=0)
    return jnp.cumsum(p, axis=0) - p[0:1]

def hgrn2_chunkwise(q, log_f, k, i):
    bsz, seq, heads, dk = q.shape
    dv = i.shape[-1]
    n_chunks = seq // HG_CHUNK

    def to_chunks(t):
        return t.reshape(bsz, n_chunks, HG_CHUNK, heads, t.shape[-1]).transpose(1, 0, 3, 2, 4)

    qc, lc, kc, ic = to_chunks(q), to_chunks(log_f), to_chunks(k), to_chunks(i)
    cum = jnp.cumsum(lc, axis=3)
    causal = jnp.tril(jnp.ones((HG_CHUNK, HG_CHUNK), dtype=bool))[:, :, None]

    def step(state, inp):
        q_c, l_c, k_c, i_c = inp
        diff = l_c[:, :, :, None, :] - l_c[:, :, None, :, :]
        decay = jnp.exp(jnp.where(causal, diff, HG_MASK_LOG))
        attn = jnp.einsum('bhtd,bhsd,bhtsd->bhts', q_c, k_c, decay)
        o = jnp.matmul(attn, i_c) + jnp.einsum('bhtd,bhdv->bhtv', q_c * jnp.exp(l_c), state)
        l_end = l_c[:, :, -1:, :]
        k_dec = k_c * jnp.exp(l_end - l_c)
        state = state * jnp.exp(l_end[:, :, 0, :, None]) + jnp.einsum('bhsd,bhsv->bhdv', k_dec, i_c)
        return state, o

    state0 = jnp.zeros((bsz, heads, dk, dv), jnp.float32)
    _, o = lax.scan(step, state0, (qc, cum, kc, ic))
    return o.transpose(1, 0, 3, 2, 4).reshape(bsz, seq, heads, dv)

def hgrn2_mix(p, lb, onorm_g):
    bsz, seq, _ = p.shape
    q, f_raw, i, g = jnp.split(p, 4, axis=-1)
    lb = lb.reshape(HG_HEADS, HG_DK)
    q = jax.nn.silu(q.reshape(bsz, seq, HG_HEADS, HG_DK))
    f_raw = f_raw.reshape(bsz, seq, HG_HEADS, HG_DK)
    log_f = jax.nn.log_sigmoid(f_raw) + jnp.log1p(lb * jnp.exp(jnp.minimum(-f_raw, HG_EXP_CLIP)))
    k = (1.0 - lb) * jax.nn.sigmoid(-f_raw)
    o = hgrn2_chunkwise(q, log_f, k, i.reshape(bsz, seq, HG_HEADS, HG_DV))
    o = rmsnorm(o, onorm_g)
    return o.reshape(bsz, seq, HG_WIDTH) * jax.nn.silu(g)

def rwkv7_scan(r, decay, k, v, kk, a):
    bsz, _, heads, n = r.shape

    def step(state, inp):
        r_t, d_t, k_t, v_t, kk_t, a_t = inp
        sa = jnp.einsum('bhvk,bhk->bhv', state, -kk_t)
        state = (state * d_t[:, :, None, :]
                 + sa[..., None] * (kk_t * a_t)[:, :, None, :]
                 + v_t[..., None] * k_t[:, :, None, :])
        return state, jnp.einsum('bhvk,bhk->bhv', state, r_t)

    xs = tuple(jnp.moveaxis(t, 1, 0) for t in (r, decay, k, v, kk, a))
    state0 = jnp.zeros((bsz, heads, n, n), jnp.float32)
    _, out = lax.scan(step, state0, xs)
    return jnp.moveaxis(out, 0, 1)

def rwkv7_mix(p, mu, w0, w2, a0, a2, g2, k_k, k_a, r_k, gn_g, gn_b):
    bsz, seq, _ = p.shape
    p = p + (token_shift(p) - p) * mu
    cuts = [RW_WIDTH, 2 * RW_WIDTH, 3 * RW_WIDTH, 3 * RW_WIDTH + RW_DECAY_LORA,
            3 * RW_WIDTH + RW_DECAY_LORA + RW_A_LORA]
    r, k, v, wd, ad, gd = jnp.split(p, cuts, axis=-1)
    w = -jax.nn.softplus(-(w0 + jnp.tanh(wd) @ w2)) - 0.5
    decay = jnp.exp(-jnp.exp(w))
    a = jax.nn.sigmoid(a0 + ad @ a2)
    g = jax.nn.sigmoid(gd) @ g2

    def heads(t):
        return t.reshape(bsz, seq, RW_HEADS, RW_N)

    kk = heads(k * k_k)
    kk = kk * lax.rsqrt(jnp.maximum(jnp.sum(kk * kk, axis=-1, keepdims=True), 1e-24))
    k = k * (1.0 + (a - 1.0) * k_a)
    r, k, v, a, decay = heads(r), heads(k), heads(v), heads(a), heads(decay)
    o = rwkv7_scan(r, decay, k, v, kk, a)
    mean = jnp.mean(o, axis=-1, keepdims=True)
    var = jnp.mean(jnp.square(o - mean), axis=-1, keepdims=True)
    o = ((o - mean) * lax.rsqrt(var + RW_GN_EPS)).reshape(bsz, seq, RW_WIDTH) * gn_g + gn_b
    bonus = jnp.sum(r * k * r_k, axis=-1, keepdims=True) * v
    return (o + bonus.reshape(bsz, seq, RW_WIDTH)) * g

def ab_mixer(h, w_in, w_out, lb, hg_onorm_g, rw_mu, rw_w0, rw_w2, rw_a0, rw_a2, rw_g2,
             rw_k_k, rw_k_a, rw_r_k, rw_gn_g, rw_gn_b):
    p = (h @ w_in).astype(jnp.float32)
    y_a = hgrn2_mix(p[..., :HG_COLS], lb, hg_onorm_g)
    y_b = rwkv7_mix(p[..., HG_COLS:], rw_mu, rw_w0, rw_w2, rw_a0, rw_a2, rw_g2,
                    rw_k_k, rw_k_a, rw_r_k, rw_gn_g, rw_gn_b)
    y = jnp.concatenate([y_a, y_b], axis=-1)
    return y.astype(h.dtype) @ w_out

def _complex_affine_combine(e1, e2):
    a1r, a1i, b1r, b1i = e1
    a2r, a2i, b2r, b2i = e2
    return (a2r * a1r - a2i * a1i,
            a2r * a1i + a2i * a1r,
            a2r * b1r - a2i * b1i + b2r,
            a2r * b1i + a2i * b1r + b2i)

def s5_mixer(h, w_in, a_re, a_im, log_dt, b_re, b_im, c_re, c_im, d, w_glu):
    bsz, seq, _ = h.shape
    u = (h @ w_in).astype(jnp.float32)
    ug = u.reshape(bsz, seq, S5_GROUPS, S5_GROUP)
    lam_re = jnp.minimum(a_re.astype(jnp.float32), -1e-4)
    lam_im = a_im.astype(jnp.float32)
    dt = jnp.exp(log_dt.astype(jnp.float32))[:, None]
    mag = jnp.exp(lam_re * dt)
    ab_re = mag * jnp.cos(lam_im * dt)
    ab_im = mag * jnp.sin(lam_im * dt)
    den = lam_re * lam_re + lam_im * lam_im
    coef_re = ((ab_re - 1.0) * lam_re + ab_im * lam_im) / den
    coef_im = (ab_im * lam_re - (ab_re - 1.0) * lam_im) / den
    bb_re = coef_re[..., None] * b_re - coef_im[..., None] * b_im
    bb_im = coef_re[..., None] * b_im + coef_im[..., None] * b_re
    bu_re = jnp.einsum('bsgm,gpm->bsgp', ug, bb_re)
    bu_im = jnp.einsum('bsgm,gpm->bsgp', ug, bb_im)
    a_seq_re = jnp.broadcast_to(ab_re, (1, seq, S5_GROUPS, S5_STATE))
    a_seq_im = jnp.broadcast_to(ab_im, (1, seq, S5_GROUPS, S5_STATE))
    _, _, x_re, x_im = lax.associative_scan(
        _complex_affine_combine, (a_seq_re, a_seq_im, bu_re, bu_im), axis=1)
    y = jnp.einsum('bsgp,gmp->bsgm', x_re, c_re) - jnp.einsum('bsgp,gmp->bsgm', x_im, c_im)
    y = y.reshape(bsz, seq, D_MODEL) + d * u
    z = jax.nn.gelu(y).astype(h.dtype) @ w_glu
    val, gate = jnp.split(z, 2, axis=-1)
    return val * jax.nn.sigmoid(gate)

def cross_attention(h, mem_n, wq, wkv, wo):
    bsz, seq, _ = h.shape
    q = (h @ wq).reshape(bsz, seq, XA_HEADS, XA_HEAD_DIM)
    k, v = jnp.split(mem_n @ wkv, 2, axis=-1)
    k = k.reshape(bsz, -1, XA_HEADS, XA_HEAD_DIM)
    v = v.reshape(bsz, -1, XA_HEADS, XA_HEAD_DIM)
    s = jnp.einsum('bshd,bmhd->bhsm', q, k).astype(jnp.float32) * (XA_HEAD_DIM ** -0.5)
    p = jax.nn.softmax(s, axis=-1).astype(v.dtype)
    o = jnp.einsum('bhsm,bmhd->bshd', p, v).reshape(bsz, seq, D_MODEL)
    return o @ wo

def moe_swiglu(h, router, w13, w2):
    bsz, seq, dm = h.shape
    t = h.reshape(-1, dm)
    logits = (t @ router).astype(jnp.float32)
    top_v, top_i = lax.top_k(logits, TOP_K)
    top_w = jax.nn.softmax(top_v, axis=-1)
    gates = jnp.einsum('nk,nke->ne', top_w, jax.nn.one_hot(top_i, N_EXPERTS, dtype=jnp.float32))
    out = jnp.zeros(t.shape, jnp.float32)
    for e in range(N_EXPERTS):
        out = out + gates[:, e:e + 1] * swiglu(t, w13[e], w2[e]).astype(jnp.float32)
    return out.astype(h.dtype).reshape(bsz, seq, dm)

def setup_inputs(seed: int = 0) -> dict:
    key = jax.random.key(seed)
    keys = jax.random.split(key, 48)
    counter = [0]

    def nxt():
        k = keys[counter[0]]
        counter[0] += 1
        return k

    def nrm(shape, scale):
        return jax.random.normal(nxt(), shape, jnp.float32) * scale

    def gain(shape):
        return 1.0 + nrm(shape, 0.02)

    def unif(shape, lo, hi):
        return jax.random.uniform(nxt(), shape, jnp.float32, lo, hi)

    D = D_MODEL
    NAB = N_AB_LAYERS
    NC = N_C_LAYERS
    G, P, M = S5_GROUPS, S5_STATE, S5_GROUP
    n_idx = jnp.arange(P, dtype=jnp.float32)
    return {
        'x': nrm((BATCH, SEQ, D), 1.0),
        'mem': nrm((BATCH, N_MEM, D), 1.0),
        'mix_norm_g': gain((DEPTH, D)),
        'xattn_norm_g': gain((DEPTH, D)),
        'ffn_norm_g': gain((DEPTH, D)),
        'mem_norm_g': gain((D,)),
        'final_norm_g': gain((D,)),
        'ab_w_in': nrm((NAB, D, AB_IN), D ** -0.5),
        'ab_w_out': nrm((NAB, D, D), D ** -0.5),
        'hg_lb_logits': nrm((NAB, HG_WIDTH), 0.1),
        'hg_onorm_g': gain((NAB, HG_DV)),
        'rw_mu': unif((NAB, RW_COLS), 0.0, 1.0),
        'rw_w0': unif((NAB, RW_WIDTH), -6.0, -1.0),
        'rw_w2': nrm((NAB, RW_DECAY_LORA, RW_WIDTH), RW_DECAY_LORA ** -0.5),
        'rw_a0': nrm((NAB, RW_WIDTH), 0.1),
        'rw_a2': nrm((NAB, RW_A_LORA, RW_WIDTH), RW_A_LORA ** -0.5),
        'rw_g2': nrm((NAB, RW_GATE_LORA, RW_WIDTH), RW_GATE_LORA ** -0.5),
        'rw_k_k': 0.85 + nrm((NAB, RW_WIDTH), 0.02),
        'rw_k_a': 1.0 + nrm((NAB, RW_WIDTH), 0.02),
        'rw_r_k': -0.04 + nrm((NAB, RW_HEADS, RW_N), 0.1),
        'rw_gn_g': gain((NAB, RW_WIDTH)),
        'rw_gn_b': nrm((NAB, RW_WIDTH), 0.02),
        'c_w_in': nrm((NC, D, D), D ** -0.5),
        's5_a_re': -0.5 + nrm((NC, G, P), 0.01),
        's5_a_im': math.pi * n_idx + nrm((NC, G, P), 0.01),
        's5_log_dt': unif((NC, G), math.log(S5_DT_MIN), math.log(S5_DT_MAX)),
        's5_b_re': nrm((NC, G, P, M), (2 * M) ** -0.5),
        's5_b_im': nrm((NC, G, P, M), (2 * M) ** -0.5),
        's5_c_re': nrm((NC, G, M, P), 0.5 ** 0.5),
        's5_c_im': nrm((NC, G, M, P), 0.5 ** 0.5),
        's5_d': nrm((NC, D), 1.0),
        'c_w_glu': nrm((NC, D, 2 * D), D ** -0.5),
        'xa_wq': nrm((DEPTH, D, D), D ** -0.5),
        'xa_wkv': nrm((DEPTH, D, 2 * D), D ** -0.5),
        'xa_wo': nrm((DEPTH, D, D), D ** -0.5),
        'ffn_w13': nrm((NAB, D, 2 * D_FF), D ** -0.5),
        'ffn_w2': nrm((NAB, D_FF, D), D_FF ** -0.5),
        'moe_router': nrm((NC, D, N_EXPERTS), D ** -0.5),
        'moe_w13': nrm((NC, N_EXPERTS, D, 2 * D_FF), D ** -0.5),
        'moe_w2': nrm((NC, N_EXPERTS, D_FF, D), D_FF ** -0.5),
    }

def reference(x, mem, mix_norm_g, xattn_norm_g, ffn_norm_g, mem_norm_g, final_norm_g,
              ab_w_in, ab_w_out, hg_lb_logits, hg_onorm_g, rw_mu, rw_w0, rw_w2, rw_a0,
              rw_a2, rw_g2, rw_k_k, rw_k_a, rw_r_k, rw_gn_g, rw_gn_b, c_w_in, s5_a_re,
              s5_a_im, s5_log_dt, s5_b_re, s5_b_im, s5_c_re, s5_c_im, s5_d, c_w_glu,
              xa_wq, xa_wkv, xa_wo, ffn_w13, ffn_w2, moe_router, moe_w13, moe_w2):
    mem_n = rmsnorm(mem, mem_norm_g)
    lb_table = hgrn2_lower_bounds(hg_lb_logits)
    for layer in range(DEPTH):
        j = layer // 2
        h = rmsnorm(x, mix_norm_g[layer])
        if layer % 2 == 0:
            x = x + ab_mixer(h, ab_w_in[j], ab_w_out[j], lb_table[j], hg_onorm_g[j],
                             rw_mu[j], rw_w0[j], rw_w2[j], rw_a0[j], rw_a2[j], rw_g2[j],
                             rw_k_k[j], rw_k_a[j], rw_r_k[j], rw_gn_g[j], rw_gn_b[j])
        else:
            x = x + s5_mixer(h, c_w_in[j], s5_a_re[j], s5_a_im[j], s5_log_dt[j], s5_b_re[j],
                             s5_b_im[j], s5_c_re[j], s5_c_im[j], s5_d[j], c_w_glu[j])
        x = x + cross_attention(rmsnorm(x, xattn_norm_g[layer]), mem_n,
                                xa_wq[layer], xa_wkv[layer], xa_wo[layer])
        h = rmsnorm(x, ffn_norm_g[layer])
        if layer % 2 == 0:
            x = x + swiglu(h, ffn_w13[j], ffn_w2[j])
        else:
            x = x + moe_swiglu(h, moe_router[j], moe_w13[j], moe_w2[j])
    return rmsnorm(x, final_norm_g)


_drawn_inputs = setup_inputs


def setup_inputs(seed=0):
    import zlib

    import numpy as np

    out = dict(_drawn_inputs(seed))
    spreads = {}
    factors = {'xattn_norm_g': 3.303,
     'mem_norm_g': 4.854,
     'final_norm_g': 2.73,
     'rw_k_a': 2.888,
     'rw_gn_g': 4.551,
     'rw_gn_b': 2.778,
     's5_a_re': 8.0}
    for name, (base, spread) in spreads.items():
        noise = np.random.default_rng([zlib.crc32(name.encode()), seed]).standard_normal(out[name].shape)
        drawn = base * np.exp(spread * noise) if base else spread * noise
        out[name] = jnp.asarray(drawn.astype(out[name].dtype))
    for name, factor in factors.items():
        out[name] = (out[name] * factor).astype(out[name].dtype)
    return out
```

```python
from contextlib import ExitStack

import numpy as np

import concourse.bass as bass
from concourse import mybir

F32 = mybir.dt.float32
ALU = mybir.AluOpType
ACT = mybir.ActivationFunctionType
AX = mybir.AxisListType

P = 128
T = 256
D = 1024
KT = D // P
C = 128
LEVELS = 7
RW_N = 64
EPS = 1e-6
GN_EPS = 64e-5
RING = 4
SLOT = 6144
DENSE = 4096
D_FF = 2816
STEP = 256
STEPS = D_FF // STEP
EXPERTS = 8
TAU = 8
BLOCKS = T // TAU
S5_M = 16
S5_P = 64
PAIRS = 32
PIECE = 4
PIECES = PAIRS // PIECE
XA_HEADS = 4
TWO_PI = 6.283185307179586
TWO_PI_HI = 6.28125
PI_BELOW = 3.1415925
ROUNDER = 12582912.0
FAR = 1048576.0
XA_SCALE = float(D // XA_HEADS) ** -0.5

ARENA = 13568

PARAM_COLS = {}
_n = 0
for _name, _w in (("mix0", 8), ("mix1", 8), ("xat0", 8), ("xat1", 8), ("ffn0", 8), ("ffn1", 8), ("memg", 8),
                  ("fin", 8), ("s5_d", 8), ("mu_r", 4), ("mu_k", 4), ("mu_v", 4), ("mu_wd", 1), ("mu_ad", 1),
                  ("mu_gd", 1), ("w0", 4), ("a0", 4), ("k_k", 4), ("k_a", 4), ("r_k", 4), ("gn_g", 4),
                  ("gn_b", 4), ("onorm", 1), ("lb", 4)):
    PARAM_COLS[_name] = (_n, _w)
    _n += _w
N_PARAM = _n
MU0, MU1 = PARAM_COLS["mu_r"][0], PARAM_COLS["mu_gd"][0] + 1

CONST_COLS = {"ident": 0, "lev": 1, "incl0": 8, "strict": 9, "incl1": 10, "head_ones": 11, "ones": 12, "mean": 14,
              "slots": 15}
N_CONST = 16


def shape_constants():
    s = np.arange(P)[:, None]
    t = np.arange(P)[None, :]
    out = np.zeros((N_CONST, P, P), np.float32)
    out[0] = s == t
    for i in range(LEVELS):
        h = 1 << i
        out[1 + i] = (s // (2 * h) == t // (2 * h)) & (s % (2 * h) < h) & (t % (2 * h) >= h)
    out[8] = out[10] = s <= t
    out[9] = s < t
    out[11] = s // RW_N == t // RW_N
    out[12] = out[13] = 1.0
    out[14] = 1.0 / D
    out[15] = t
    return np.ascontiguousarray(out.transpose(1, 0, 2).reshape(P, N_CONST * P))


def build_trunk(nc, A, out):
    ctx = ExitStack()
    with ctx:
        def sb(name, shape):
            return ctx.enter_context(nc.sbuf_tensor(name, shape, F32))

        sems = {}

        def S(name):
            if name not in sems:
                sems[name] = ctx.enter_context(nc.semaphore(name))
            return sems[name]

        x = sb("x", [P, KT, T])
        h = sb("h", [P, KT, T])
        sq = sb("sq", [P, KT, T])
        memn = sb("memn", [P, KT, T])
        kT = sb("kT", [P, KT, T])
        vN = sb("vN", [P, 2, D])
        con = sb("con", [P, N_CONST, P])
        par = sb("par", [P, N_PARAM])
        omu = sb("omu", [P, MU1 - MU0])
        lbs = sb("lbs", [P, 4, 4])
        rstd = sb("rstd", [P, T])
        nrm = sb("nrm", [P, T])
        small = sb("small", [P, 16])
        ring = sb("ring", [P, RING, SLOT])
        arena = sb("arena", [P, ARENA])
        ps = [ctx.enter_context(nc.psum_tensor(f"ps{i}", [P, 512], F32)) for i in range(8)]

        def pc(name, i=0, rows=P, n=1):
            c0 = PARAM_COLS[name][0] + i
            return par[0:rows, c0:c0 + n]

        def om(name, i=0, rows=P):
            c0 = PARAM_COLS[name][0] + i - MU0
            return omu[0:rows, c0:c0 + 1]

        def cc(name, n=1):
            c0 = CONST_COLS[name]
            return con[:, c0:c0 + n, :]

        ident = con[:, 0, :]
        head_ones = con[:, CONST_COLS["head_ones"], :]
        ones = con[:, CONST_COLS["ones"], :]
        mean_ones = con[:, CONST_COLS["mean"], :]
        ring_flat = ring[:, :, :].rearrange("p s w -> p (s w)")

        def ar(at, words):
            assert at + words <= ARENA
            return arena[:, at:at + words]

        def spare(at, words):
            assert at + words <= 2 * SLOT
            return ring_flat[:, 2 * SLOT + at:2 * SLOT + at + words]

        def tiles4(a):
            return a.rearrange("p (n t) -> p n t", t=T)

        def flat(a):
            return a.rearrange("p n t -> p (n t)")

        def stack(a, n=8):
            return a.rearrange("p (n t) -> p n t", n=n)

        hq, hL, hk, hg = (tiles4(ar(1024 * i, 1024)) for i in range(4))
        hi = ar(4096, 1024).rearrange("p (c v) -> p c v", c=2)
        rr, rk, rv, rg = (tiles4(ar(5120 + 1024 * i, 1024)) for i in range(4))
        lw, la, lg = (ar(9216 + 256 * i, 256) for i in range(3))
        vn = ar(9984, 1024).rearrange("p (c v) -> p c v", c=2)
        F = [ar(11008 + 1024 * i, 1024) for i in range(2)]
        M0 = ar(13056, 512).rearrange("p (n two v) -> p n two v", n=4, two=2)
        smallw = spare(0, 1536).rearrange("p (m n) -> p m n", m=3)
        ld, cL, ra, kk = (tiles4(spare(1536 + 1024 * i, 1024)) for i in range(4))
        AR = spare(5632, 2048).rearrange("p (n c two t) -> p n c two t", n=4, c=2, two=2)
        bt = tiles4(spare(7680, 1024))
        kt = tiles4(spare(8704, 1024))
        att = [spare(9728 + 512 * i, 512) for i in range(2)]
        R = stack(spare(10752, 512))
        U = stack(spare(11264, 512))
        bonus = tiles4(flat(sq[:, 0:4, :]))
        tA = tiles4(spare(9728, 1024))
        tB = tiles4(spare(10752, 1024))
        tC = tiles4(flat(sq[:, 4:8, :]))
        SC = spare(2560, 3072).rearrange("p (h m t) -> p h m t", h=8, m=3)
        Am = stack(spare(1536, 1024))
        X = stack(ar(5120, 1024))
        Y = stack(ar(6144, 1024))
        V = stack(spare(0, 1024))
        bkn = flat(sq[:, 4:8, :]).rearrange("p (two v) -> p two v", two=2)
        ro = tiles4(ar(7168, 1024))
        ho = hq

        qT = ar(0, 2048).rearrange("p (n t) -> p n t", t=T)
        prob = ar(2048, 2048).rearrange("p (h s m) -> p h s m", h=4, s=2)
        pT = ar(4096, 2048).rearrange("p (h m t) -> p h m t", h=4, m=2)
        smax = small[:, 0:8]
        ssum = small[:, 8:16]
        fg = [flat(sq[:, i:i + 1, :]) for i in range(2)]
        fh = [sq[:, 2 + 2 * i:4 + 2 * i, :] for i in range(2)]
        sa = ar(0, 96).rearrange("p (w g) -> p w g", w=3)
        sw = ar(96, 1024).rearrange("p (w g) -> p w g", g=PAIRS)
        sbc = ar(1120, 2048).rearrange("p (w g m) -> p w g m", w=4, g=PAIRS)
        sbb = ar(3168, 1024).rearrange("p (w g m) -> p w g m", w=2, g=PAIRS)
        spw = ar(4192, 576).rearrange("p (w k g) -> p w k g", w=2, k=TAU + 1)
        sCW = ar(4768, 1152).rearrange("p (g w k m) -> p g w k m", g=PIECE, w=2, k=TAU + 1)
        sW1T = ar(5920, 1024).rearrange("p (w g k m) -> p w g k m", w=2, g=PIECE, k=TAU)
        st = [ar(6944 + 576 * i, 576) for i in range(2)]
        sW1 = ar(8096, 1024).rearrange("p (g w c) -> p g w c", g=PIECE, w=2)
        sK = ar(9120, 2048).rearrange("p (g k m) -> p g k m", g=2 * PIECE, k=2 * TAU)[0:S5_M, :, :, :]
        s5rot = ar(ARENA - 128, 96).rearrange("p (w g) -> p w g", w=3)
        uT = ar(0, 2048).rearrange("p (n t) -> p n t", t=T)
        Ub = ar(2048, 2048).rearrange("p (g j) -> p g j", j=BLOCKS)
        Z = ar(4096, 2048).rearrange("p (w g) -> p w g", w=2)
        rot = ar(6144, 2048).rearrange("p (w g j) -> p w g j", w=2, g=PAIRS)
        rho = ar(8192, 1024).rearrange("p (g j) -> p g j", g=PAIRS)
        t2 = ar(9216, 2048).rearrange("p (w g) -> p w g", w=2)
        Xs = ar(11264, 2048).rearrange("p (w g j) -> p w g j", w=2, g=PAIRS)
        Yb = ar(9216, 2048).rearrange("p (g j) -> p g j", j=BLOCKS)
        yT = ar(4096, 2048).rearrange("p (n t) -> p n t", t=T)
        sg = [ar(9216 + 512 * i, 512) for i in range(2)]
        hN = ar(0, 2048).rearrange("p (c d) -> p c d", c=2)
        Gs = ar(2048, 256).rearrange("p (c s) -> p c s", c=2)
        Gg = ar(2304, 256).rearrange("p (c s) -> p c s", c=2)
        GT = ar(2560, 256)
        hc = ar(2816, 1024).rearrange("p (k c) -> p k c", k=KT)
        sil = [ar(3840 + 256 * i, 256) for i in range(2)]
        hid = [ar(4352 + 256 * i, 256) for i in range(2)]
        hidT = [ar(4864 + 256 * i, 256).rearrange("p (j c) -> p j c", j=2) for i in range(2)]
        yc = ar(5376, 1024)
        router = ar(6400, 64).rearrange("p (k e) -> p k e", k=KT)
        lgt = ar(6464, 16).rearrange("p (c e) -> p c e", c=2)
        cmpA = ar(6480, 128).rearrange("p (c e f) -> p c e f", c=2, e=EXPERTS)
        cmpB = ar(6608, 128).rearrange("p (c e f) -> p c e f", c=2, e=EXPERTS)
        sel = ar(6736, 16).rearrange("p (c e) -> p c e", c=2)
        gw = ar(6752, 16).rearrange("p (c e) -> p c e", c=2)
        gm = ar(6768, 4)
        PG = ar(6776, 40).rearrange("p (c w e) -> p c w e", c=2, w=2)
        pick = ar(6816, 4).rearrange("p (c w) -> p c w", c=2)
        cnt = ar(6820, 9)
        flag = ctx.enter_context(nc.sbuf_tensor("flag", [1, 1], mybir.dt.int32))
        dW1 = nc.dram_tensor("s5_w1", [2, P, 4096], F32, kind="Internal").ap()
        dW2 = nc.dram_tensor("s5_w2", [2, P, 4096], F32, kind="Internal").ap()
        dK = nc.dram_tensor("s5_k", [S5_M, 2 * PAIRS, 2 * TAU * S5_M], F32, kind="Internal").ap()
        dU = nc.dram_tensor("s5_u", [D, T], F32, kind="Internal").ap()
        dY = nc.dram_tensor("s5_y", [D, T], F32, kind="Internal").ap()

        bank_count = [[0, 0] for _ in range(8)]
        uses = {}

        def use_bank(name, bank, reads=1):
            fills, before = bank_count[bank]
            uses[name] = (bank, fills + 1, before, before + reads)
            bank_count[bank] = [fills + 1, before + reads]

        def bank(name):
            return ps[uses[name][0]]

        def wait_bank_free(pe, name):
            b, _, before, _ = uses[name]
            if before:
                pe.wait_ge(S(f"bank{b}_read"), before)

        def filled(name):
            return S(f"bank{uses[name][0]}_filled")

        def is_filled(name):
            return S(f"bank{uses[name][0]}_filled"), uses[name][1]

        def read(name):
            return S(f"bank{uses[name][0]}_read")

        def was_read(name):
            return S(f"bank{uses[name][0]}_read"), uses[name][3]

        use_bank("norm_mix0", 6)
        use_bank("norm_mem", 7)
        use_bank("wd_ad", 0, 2)
        use_bank("gd", 1)
        turn = [2]

        def next_bank(name):
            use_bank(name, turn[0] % 6)
            turn[0] += 1

        for name in ("r", "k", "z", "a", "rg", "v", "kk", "q", "f", "i", "g", "bonus", "vn", "kv_0", "kv_1"):
            for half in range(2):
                next_bank(f"{name}{half}")
        order = []
        fillers = [("kv", 2), ("kv", 3)]
        levels = [("level", i) for i in range(LEVELS + 2)]
        for c in range(2):
            order.append(("scores", c))
            for l in range(LEVELS):
                order.append(("invert", c, l))
                if levels:
                    order.append(levels.pop(0))
                if l == 3 and c == 0:
                    order.append(fillers.pop(0))
            order.append(("solve", c))
            if c == 0:
                order.append(fillers.pop(0))
        assert not levels and not fillers
        for step in order:
            if step[0] == "scores":
                for head in range(8):
                    use_bank(f"sc{step[1]}_{head}", head % 4)
                if step[1] == 0:
                    for m in range(2):
                        use_bank(f"bkn{m}", 4 + m)
            elif step[0] == "invert":
                c, l = step[1:]
                for g in range(2):
                    use_bank(f"V{c}_{l}_{g}", g)
                for g in range(2):
                    if l < LEVELS - 1:
                        use_bank(f"dX{c}_{l}_{g}", 2)
                    use_bank(f"dY{c}_{l}_{g}", 3)
            elif step[0] == "level":
                for b in range(2 if step[1] <= LEVELS else 1):
                    use_bank(f"att{step[1]}_{b}", 4 + b)
                if step[1] == LEVELS + 1:
                    for b in range(2):
                        use_bank(f"ho{b}", 6 + b)
            elif step[0] == "kv":
                for half in range(2):
                    use_bank(f"kv_{step[1]}{half}", 4 + half)
            elif step[0] == "solve":
                c = step[1]
                use_bank(f"R{c}", 0)
                use_bank(f"U{c}", 1)
                if c == 0:
                    use_bank("M0", 2)
                use_bank(f"ro{c}", 3)
        for b in range(2):
            use_bank(f"hsum{b}", 4 + b)
        for what in ("mean", "var"):
            for b in range(2):
                use_bank(f"{what}{b}", 0 + b)

        def xattn_uses(l):
            use_bank(f"norm_xat{l}", 7)
            for c in range(2):
                for half in range(2):
                    use_bank(f"q{l}_{c}{half}", 2 * c + half)
            for head in range(4):
                use_bank(f"s{l}_{head}", 4 + head % 2)
            for head in range(4):
                use_bank(f"pt{l}_{head}", head)
                use_bank(f"pv{l}_{head}", 6 + head % 2)
            for c in range(2):
                for half in range(2):
                    use_bank(f"xo{l}_{c}{half}", 2 * c + half)

        for c in range(2):
            for half in range(2):
                use_bank(f"out_{c}{half}", 2 + 2 * c + half)
        xattn_uses(0)
        use_bank("norm_ffn0", 7)
        ffn_bank = [0]
        for s_ in range(STEPS):
            for j in range(2):
                use_bank(f"f{s_}_{j}", ffn_bank[0] % 3)
                ffn_bank[0] += 1
        for p_ in range(PIECES):
            for w_ in ("re", "im", "k0", "k1"):
                use_bank(f"{w_}_{p_}", 3)
        for b in range(4):
            use_bank(f"fo{b}", 4 + b)
        use_bank("norm_mix1", 0)
        for c in range(2):
            for half in range(2):
                use_bank(f"u_{c}{half}", 1 + 2 * c + half)
        for c in range(4):
            for half in range(2):
                use_bank(f"kv1_{c}{half}", (5 + 2 * c + half) % 4)
        for w_ in range(2):
            for half in range(2):
                use_bank(f"Z{w_}{half}", 4 + 2 * w_ + half)
        for par_ in range(2):
            for half in range(2):
                use_bank(f"Y{par_}{half}", 2 * par_ + half)
        for c in range(4):
            use_bank(f"val{c}", 4 + (2 * c) % 4)
            use_bank(f"gate{c}", 4 + (2 * c + 1) % 4)
        xattn_uses(1)
        use_bank("norm_ffn1", 0)
        use_bank("logits", 1)
        for m in range(4):
            use_bank(f"hN{m}", 2 + m)
        use_bank("places", 6)

        use_bank("norm_fin", 0)
        x_writes, squares_before = {}, {}
        for i, name in enumerate(("norm_xat0", "norm_ffn0", "norm_mix1", "norm_xat1", "norm_ffn1", "norm_fin")):
            x_writes[name] = 4 * i
            squares_before[name] = 2 + 4 * i

        stream = []
        slot_uses = [0] * RING
        in_slot = [None, None, ("yb_ready", 1), ("yb_ready", 1)]
        place = {}

        def chunk(name, slot, src, last_bank=None, freed=None):
            stream.append((name, slot, src, in_slot[slot]))
            place[name] = (slot, slot_uses[slot])
            slot_uses[slot] += 1
            in_slot[slot] = freed or ("bank", last_bank)

        first = [("w_lora", "gd"), ("w_r", "r1"), ("w_k", "k1"), ("w_v", "v1"), ("w_q", "q1"), ("w_f", "f1"),
                 ("w_i", "i1"), ("w_g", "g1"), ("kv0_0", "kv_01"), ("kv0_1", "kv_11"), ("kv0_2", "kv_21"),
                 ("kv0_3", "kv_31"), ("wout0", "out_01"), ("wout1", "out_11"), ("wq0_0", "q0_01"),
                 ("wq0_1", "q0_11"), ("wo0_0", "xo0_01"), ("wo0_1", "xo0_11")]
        for n, (name, last) in enumerate(first):
            chunk(name, n % (2 if n < 14 else 4), A["dense"][n - 1] if n else A["lora"], last)
        turn_slot = len(first)
        n_dense = len(first) - 1
        for i in range(STEPS):
            chunk(f"ffn{i}", turn_slot % RING, A["ffn"][i], freed=("ffn_steps", i + 1) if i < STEPS - 1 else ("bank", "fo3"))
            turn_slot += 1
        second = [("cw0", "u_01"), ("cw1", "u_11"), ("kv1_0", "kv1_01"), ("kv1_1", "kv1_11"), ("s5_W1_0", None),
                  ("s5_W1_1", "Z11"), ("kv1_2", "kv1_21"), ("kv1_3", "kv1_31"), ("s5_T_0", None), ("s5_T_1", None),
                  ("s5_W2_0", None), ("s5_W2_1", None), ("glu0", "gate0"), ("glu1", "gate1"), ("glu2", "gate2"),
                  ("glu3", "gate3"), ("wq1_0", "q1_01"), ("wq1_1", "q1_11"), ("wo1_0", "xo1_01"), ("wo1_1", "xo1_11")]
        for name, last in second:
            if name.startswith("s5_"):
                i = int(name[-1])
                src = {"W1": dW1[i], "T_": i, "W2": dW2[i]}[name[3:5]]
                freed = ("bank", "Z10") if name == "s5_W1_0" else ("bank", "Z11") if name == "s5_W1_1" else ("bank", "Y11")
                chunk(name, turn_slot % RING, src, freed=freed)
            else:
                chunk(name, turn_slot % RING, A["dense"][n_dense], last)
                n_dense += 1
            turn_slot += 1
        first_use = list(slot_uses)
        per_expert = [len(range(i, STEPS, RING)) for i in range(RING)]

        def weights(name, words=DENSE):
            return ring[:, place[name][0], 0:words].rearrange("p (k n) -> p k n", k=KT)

        def arrived(name):
            slot, use = place[name]
            return S(f"slot{slot}_filled"), 16 * (use + 1)

        def freed_by(what):
            return is_filled(what[1]) if what[0] == "bank" else (S(what[0]), what[1])

        block = ctx.enter_context(nc.Block())

        @block.sync
        def _(sp):
            for name, slot, src, freed in stream:
                if freed:
                    sp.wait_ge(*freed_by(freed))
                if name.startswith("s5_"):
                    sp.wait_ge(S("s5_stored"), 16 * 3 * PIECES)
                if name.startswith("s5_T"):
                    for kappa in range(TAU):
                        row, sigma = S5_M * kappa, TAU - 1 - kappa
                        sp.dma_start(ring[row:row + S5_M, slot, 0:DENSE].rearrange("p (g c) -> p g c", g=PAIRS),
                                     dK[:, PAIRS * src:PAIRS * (src + 1), (TAU - sigma) * S5_M:(2 * TAU - sigma) * S5_M])\
                          .then_inc(S("s5_T_filled"), 16)
                    sp.wait_ge(S("s5_T_filled"), 16 * TAU * (src + 1))
                    sp.sem_inc(S(f"slot{slot}_filled"), 16)
                    continue
                sp.dma_start(ring[:, slot, 0:src.shape[-1]], src).then_inc(S(f"slot{slot}_filled"), 16)

            def expert_steps(e, i):
                for step in range(STEPS):
                    slot = step % RING
                    if step < RING:
                        before = max(range(slot, STEPS, RING)) + 1
                    else:
                        before = STEPS + step - RING + 1
                    sp.wait_ge(S("moe_steps"), i * STEPS + before)
                    sp.dma_start(ring[:, slot, :], A["moe"][bass.ds(e, 1), step, :, :].rearrange("o p w -> p (o w)"))\
                      .then_inc(S(f"slot{slot}_filled"), 16)

            for slot in range(RING):
                if in_slot[slot]:
                    sp.wait_ge(*freed_by(in_slot[slot]))
            with sp.Fori(0, EXPERTS) as e:
                expert_steps(e, e)
            sp.wait_ge(S("flag_ready"), 1)
            busiest = sp.value_load(flag[0:1, 0:1], min_val=0, max_val=T)
            with sp.If(busiest > P):
                with sp.Fori(0, EXPERTS) as e:
                    expert_steps(e, e + EXPERTS)
            sp.wait_ge(S("final_ready"), KT)
            sp.dma_start(out, h[:, :, :]).then_inc(S("stored"), 16)
            sp.wait_ge(S("stored"), 16)

        @block.gpsimd
        def _(pool):
            for p in range(PIECES):
                pool.wait_ge(S("s5_cw"), p + 1)
                pool.wait_ge(*is_filled(f"k1_{p}"))
                cols = slice((p % 4) * 1024, (p % 4 + 1) * 1024)
                pool.dma_start(dW2[p // 4][:, cols].rearrange("p (g w c) -> p g w c", g=PIECE, w=2),
                               sCW[:, :, :, 1:TAU + 1, :].rearrange("p g w k m -> p g w (k m)")).then_inc(S("s5_stored"), 16)
                pool.wait_ge(*was_read(f"im_{p}"))
                pool.wait_ge(*was_read(f"k1_{p}"))
                pool.dma_start(dW1[p // 4][:, cols], ar(8096, 1024)).then_inc(S("s5_stored"), 16)
                pool.dma_start(dK[:, 8 * p:8 * p + 8, :], sK.rearrange("p g k m -> p g (k m)")).then_inc(S("s5_stored"), 16)

        @block.scalar
        def _(act):
            act.dma_start(x[:, :, :], A["x"]).then_inc(S("x_loaded"), 16)
            act.dma_start(con[:, :, :].rearrange("p n c -> p (n c)"), A["con"]).then_inc(S("con_loaded"), 16)
            act.dma_start(par[:, :], A["par"]).then_inc(S("par_loaded"), 16)
            act.dma_start(memn[:, :, :], A["mem"]).then_inc(S("mem_loaded"), 16)
            act.dma_start(spare(0, 1536), A["smallw"]).then_inc(S("smallw_loaded"), 16)

            linked = [0]

            def link(ins):
                linked[0] += 1
                ins.then_inc(S("act_link"), 1)
                act.wait_ge(S("act_link"), linked[0])

            def squares(src):
                act.activation(sq[:, :, :], src[:, :, :], ACT.Square).then_inc(S("squares"), 1)

            def root(name):
                act.wait_ge(*is_filled(name))
                act.activation(nrm[:, :], bank(name)[:, 0:T], ACT.Sqrt, bias=EPS).then_inc(read(name), 1)

            def copy_bank(name, dst):
                act.wait_ge(*is_filled(name))
                act.activation(dst, bank(name)[:, :], ACT.Copy).then_inc(read(name), 1)

            act.wait_ge(S("x_loaded"), 16)
            squares(x)
            root("norm_mix0")
            act.wait_ge(S("mem_loaded"), 16)
            squares(memn)
            act.wait_ge(S("norm_scaled"), 1)
            root("norm_mem")
            act.wait_ge(S("lb_shifted"), 1)
            act.activation(lbs[:, 1, :], lbs[:, 0, :], ACT.Exp).then_inc(S("lb_exp"), 1)

            act.wait_ge(S("omu_ready"), 1)
            act.wait_ge(*is_filled("wd_ad"))
            act.activation(lw[0:32, :], bank("wd_ad")[0:32, 0:T], ACT.Copy, scale=om("mu_wd", 0, 32)).then_inc(S("own_part"), 1)
            act.activation(la[0:32, :], bank("wd_ad")[0:32, T:2 * T], ACT.Copy, scale=om("mu_ad", 0, 32)).then_inc(S("own_part"), 1)
            act.wait_ge(*is_filled("gd"))
            act.activation(lg[0:96, :], bank("gd")[0:96, 0:T], ACT.Copy, scale=om("mu_gd", 0, 96)).then_inc(S("own_part"), 1)

            def own_part(name, dst):
                for half in range(2):
                    act.wait_ge(*is_filled(f"{name}{half}"))
                    for i in range(2):
                        act.activation(dst[:, 2 * half + i, :], bank(f"{name}{half}")[:, i * T:(i + 1) * T], ACT.Copy,
                                       scale=om("mu_" + name, 2 * half + i)).then_inc(S("own_part"), 1)

            own_part("r", rr)
            act.wait_ge(*was_read("wd_ad"))
            act.wait_ge(*was_read("gd"))
            act.activation(lw[0:32, :], lw[0:32, :], ACT.Tanh).then_inc(S("low_rank_in"), 1)
            act.activation(lg[0:96, :], lg[0:96, :], ACT.Sigmoid).then_inc(S("low_rank_in"), 1)
            own_part("k", rk)
            for name, bias, dst in (("z", "w0", ld), ("a", "a0", ra)):
                for half in range(2):
                    act.wait_ge(*is_filled(f"{name}{half}"))
                    for i in range(2):
                        last = act.activation(dst[:, 2 * half + i, :], bank(f"{name}{half}")[:, i * T:(i + 1) * T],
                                              ACT.Sigmoid, bias=pc(bias, 2 * half + i))
                    last.then_inc(read(f"{name}{half}"), 1)
            for half in range(2):
                copy_bank(f"rg{half}", flat(rg[:, 2 * half:2 * half + 2, :]))
            own_part("v", rv)
            act.wait_ge(*was_read("k1"))
            for n in range(4):
                last = act.activation(kk[:, n, :], rk[:, n, :], ACT.Copy, scale=pc("k_k", n))
            link(last)
            act.activation(tC, kk, ACT.Square).then_inc(S("kk_squared"), 1)
            act.wait_ge(*was_read("kk0"))
            act.wait_ge(*was_read("kk1"))
            act.activation(tC, tC, ACT.Sqrt).then_inc(S("kk_root"), 1)
            for half in range(2):
                act.wait_ge(*is_filled(f"q{half}"))
                act.activation(flat(hq[:, 2 * half:2 * half + 2, :]), bank(f"q{half}")[:, :], ACT.Sigmoid).then_inc(S("q_sigmoid"), 1)
            for half in range(2):
                act.wait_ge(*is_filled(f"f{half}"))
                act.activation(F[0][:, half * 512:(half + 1) * 512], bank(f"f{half}")[:, :], ACT.Abs)
                act.activation(flat(hk[:, 2 * half:2 * half + 2, :]), bank(f"f{half}")[:, :], ACT.Sigmoid, scale=-1.0).then_inc(S("f_sigmoid"), 1)
            for half in range(2):
                copy_bank(f"i{half}", hi[:, half, :])
            for half in range(2):
                act.wait_ge(*is_filled(f"g{half}"))
                act.activation(flat(hg[:, 2 * half:2 * half + 2, :]), bank(f"g{half}")[:, :], ACT.Sigmoid).then_inc(S("g_sigmoid"), 1)
            act.wait_ge(*was_read("f0"))
            act.wait_ge(*was_read("f1"))
            act.activation(F[0], F[0], ACT.Exp, scale=-1.0)
            link(act.activation(F[1], F[1], ACT.Exp))
            act.wait_ge(S("decays_in"), 1)
            act.activation(small[:, 0:4], small[:, 0:4], ACT.Exp)
            act.activation(tA, cL, ACT.Exp, scale=-1.0)
            act.activation(tB, ld, ACT.Exp).then_inc(S("decays_out"), 1)
            act.activation(cL, cL, ACT.Exp).then_inc(S("decays_out"), 1)
            act.activation(F[0], F[0], ACT.Ln, bias=1.0)
            act.wait_ge(S("lb_ready"), 1)
            for n in range(4):
                last = act.activation(F[1][:, n * T:(n + 1) * T], F[1][:, n * T:(n + 1) * T], ACT.Ln, bias=1.0, scale=lbs[:, 2, n:n + 1])
            last.then_inc(S("f_logs"), 1)
            for c in range(2):
                copy_bank(f"vn{c}", vn[:, c, :])
            for half in range(2):
                copy_bank(f"kv_0{half}", flat(kT[:, 2 * half:2 * half + 2, :]))
            for half in range(2):
                copy_bank(f"kv_1{half}", flat(kT[:, 4 + 2 * half:6 + 2 * half, :]))

            def level(i):
                if i > LEVELS + 1:
                    return
                act.wait_ge(S("distances"), i)
                act.activation(F[i % 2], F[i % 2], ACT.Exp).then_inc(S("level_decays"), 1)

            for step in order:
                if step[0] == "scores":
                    c = step[1]
                    if c == 1:
                        act.wait_ge(*is_filled(f"V0_{LEVELS - 1}_1"))
                    for head in range(8):
                        act.wait_ge(*is_filled(f"sc{c}_{head}"))
                        act.activation(Am[:, head, :], bank(f"sc{c}_{head}")[:, 0:P], ACT.Copy).then_inc(S("A_copied"), 1)
                    if c == 0:
                        for m in range(2):
                            copy_bank(f"bkn{m}", bkn[:, m, :])
                elif step[0] == "level":
                    level(step[1] + 1)
                elif step[0] == "kv":
                    for half in range(2):
                        copy_bank(f"kv_{step[1]}{half}", vN[:, half, (step[1] - 2) * 512:(step[1] - 1) * 512])
                elif step[0] == "solve":
                    c = step[1]
                    copy_bank(f"R{c}", flat(R))
                    copy_bank(f"U{c}", flat(U))
                    act.wait_ge(*is_filled(f"ro{c}"))
                    act.activation(ro[:, :, c * C:(c + 1) * C], stack(bank(f"ro{c}")[:, :], 4), ACT.Copy).then_inc(read(f"ro{c}"), 1)
            for b in range(2):
                copy_bank(f"ho{b}", flat(ho[:, 2 * b:2 * b + 2, :]))
            act.wait_ge(*was_read("ho0"))
            act.wait_ge(*was_read("ho1"))
            act.activation(F[0], flat(ho), ACT.Square).then_inc(S("ho_squared"), 1)
            for b in range(2):
                act.wait_ge(*is_filled(f"hsum{b}"))
                act.activation(F[1][:, b * 512:(b + 1) * 512], bank(f"hsum{b}")[:, :], ACT.Sqrt, bias=EPS, scale=1.0 / P).then_inc(read(f"hsum{b}"), 1)
            for b in range(2):
                act.wait_ge(*was_read(f"mean{b}"))
            act.activation(tA, ro, ACT.Square).then_inc(S("ro_squared"), 1)
            for b in range(2):
                act.wait_ge(*is_filled(f"var{b}"))
                act.activation(flat(tB[:, 2 * b:2 * b + 2, :]), bank(f"var{b}")[:, :], ACT.Sqrt, bias=GN_EPS, scale=1.0 / RW_N).then_inc(read(f"var{b}"), 1)

            norms = [2]

            def norm_of_x(name):
                for b in range(4):
                    act.wait_ge(S("x_written"), x_writes[name] + b + 1)
                    act.activation(sq[:, 2 * b:2 * b + 2, :], x[:, 2 * b:2 * b + 2, :], ACT.Square).then_inc(S("squares"), 1)
                act.wait_ge(S("norm_scaled"), KT * (norms[0] - 1) + 1)
                norms[0] += 1
                root(name)

            def cross_attention(l):
                norm_of_x(f"norm_xat{l}")
                for c in range(2):
                    for half in range(2):
                        copy_bank(f"q{l}_{c}{half}", flat(qT[:, 4 * c + 2 * half:4 * c + 2 * half + 2, :]))
                for head in range(4):
                    act.wait_ge(S("score_max"), 4 * l + head + 1)
                    for b in range(2):
                        last = act.activation(prob[:, head, b, :], bank(f"s{l}_{head}")[:, b * T:(b + 1) * T], ACT.Exp, scale=XA_SCALE,
                                              bias=smax[:, 2 * head + b:2 * head + b + 1], accum_out=ssum[:, 2 * head + b:2 * head + b + 1])
                    last.then_inc(read(f"s{l}_{head}"), 1)
                for head in range(4):
                    copy_bank(f"pt{l}_{head}", pT[:, head, :, :].rearrange("p m t -> p (m t)"))
                    copy_bank(f"pv{l}_{head}", flat(h[:, 2 * head:2 * head + 2, :]))

            cross_attention(0)
            norm_of_x("norm_ffn0")

            act.dma_start(ar(0, 96), A["s5a"]).then_inc(S("s5_a_loaded"), 16)
            act.dma_start(ar(1120, 2048), A["s5bc"]).then_inc(S("s5_bc_loaded"), 16)

            def s5_base():
                act.wait_ge(S("s5_a_loaded"), 16)
                act.activation(sw[:, 0, :], sa[:, 2, :], ACT.Exp).then_inc(S("s5_dt"), 1)
                act.wait_ge(S("s5_angles"), 1)
                act.activation(sw[:, 3, :], sw[:, 1, :], ACT.Exp)
                act.activation(s5rot[:, 2, :], sw[:, 1, :], ACT.Exp, scale=float(TAU))
                act.activation(sw[:, 4, :], sw[:, 5, :], ACT.Sin)
                act.activation(sw[:, 6, :], sw[:, 7, :], ACT.Sin).then_inc(S("s5_sines"), 1)

            def s5_piece(p):
                if p:
                    act.wait_ge(S("s5_stored"), 48 * p)
                for w, name in enumerate(("re", "im")):
                    act.wait_ge(*is_filled(f"{name}_{p}"))
                    act.activation(sW1[:, :, w, :], stack(bank(f"{name}_{p}")[:, :], PIECE), ACT.Copy).then_inc(read(f"{name}_{p}"), 1)
                if p == 0:
                    act.wait_ge(S("s5_zeros"), 1)
                for par_ in range(2):
                    name = f"k{par_}_{p}"
                    act.wait_ge(*is_filled(name))
                    act.activation(sK.rearrange("p (g two) k m -> p g two (k m)", two=2)[:, :, par_, P:2 * P],
                                   stack(bank(name)[0:S5_M, :], PIECE), ACT.Copy).then_inc(read(name), 1)

            for step in range(STEPS):
                for j in range(2):
                    name = f"f{step}_{j}"
                    act.wait_ge(*is_filled(name))
                    if 2 * step + j >= 2:
                        act.wait_ge(S("hidden"), 2 * step + j - 1)
                    act.activation(fg[j], bank(name)[:, 0:T], ACT.Silu).then_inc(S("gated"), 1)
                if step == 0:
                    s5_base()
                if 3 <= step and step - 3 < PIECES:
                    s5_piece(step - 3)

            act.wait_ge(*is_filled("fo3"))
            norm_of_x("norm_mix1")
            for c in range(2):
                for half in range(2):
                    copy_bank(f"u_{c}{half}", flat(uT[:, 4 * c + 2 * half:4 * c + 2 * half + 2, :]))
            act.wait_ge(*was_read("u_11"))
            by_channel = lambda a: a.rearrange("(n p) t -> p n t", p=P)
            by_group = lambda a: a.rearrange("(g m) (s j) -> m g s j", m=S5_M, j=BLOCKS)
            act.dma_start(by_channel(dU), uT).then_inc(S("u_stored"), 16)
            act.wait_ge(S("u_stored"), 16)
            for kappa in range(TAU):
                act.dma_start(Ub[S5_M * kappa:S5_M * (kappa + 1), :, :], by_group(dU)[:, :, TAU - 1 - kappa, :]).then_inc(S("u_blocks"), 16)
            for c in range(2):
                for half in range(2):
                    copy_bank(f"kv1_{c}{half}", flat(kT[:, 4 * c + 2 * half:4 * c + 2 * half + 2, :]))
            for w in range(2):
                for half in range(2):
                    copy_bank(f"Z{w}{half}", Z[:, w, half * 512:(half + 1) * 512])
            for c in range(2):
                for half in range(2):
                    copy_bank(f"kv1_{c + 2}{half}", vN[:, half, c * 512:(c + 1) * 512])
            act.wait_ge(S("states"), 1)
            for half in range(2):
                for par_ in range(2):
                    name = f"Y{par_}{half}"
                    act.wait_ge(*is_filled(name))
                    act.activation(Yb.rearrange("p (g two) j -> p g two j", two=2)[:, 16 * half:16 * half + 16, par_, :],
                                   bank(name)[:, :].rearrange("p (g j) -> p g j", j=BLOCKS), ACT.Copy).then_inc(read(name), 1)
            for par_ in range(2):
                act.wait_ge(*was_read(f"Y{par_}1"))
            for tau in range(TAU):
                act.dma_start(by_group(dY)[:, :, tau, :], Yb[S5_M * tau:S5_M * (tau + 1), :, :]).then_inc(S("y_stored"), 16)
            act.wait_ge(S("y_stored"), 16 * TAU)
            act.dma_start(yT, by_channel(dY)).then_inc(S("y_loaded"), 16)
            for n in range(KT):
                act.wait_ge(S("y_skipped"), n + 1)
                act.activation(h[:, n, :], yT[:, n, :], ACT.Gelu_apprx_tanh).then_inc(S("gelu"), 1)
            for c in range(4):
                act.wait_ge(*is_filled(f"gate{c}"))
                if c >= 2:
                    act.wait_ge(S("x_written"), x_writes["norm_xat1"] + c - 1)
                act.activation(sg[c % 2], bank(f"gate{c}")[:, :], ACT.Sigmoid).then_inc(read(f"gate{c}"), 1)
            cross_attention(1)

            norm_of_x("norm_ffn1")
            act.dma_start(ar(6400, 64), A["router"]).then_inc(S("router_loaded"), 16)
            act.wait_ge(S("logits_less_max"), 1)
            act.activation(gw, lgt, ACT.Exp).then_inc(S("gate_exp"), 1)
            for m in range(4):
                copy_bank(f"hN{m}", hN[:, m // 2, (m % 2) * 512:(m % 2 + 1) * 512])

            def expert(i):
                for b in range(2):
                    act.wait_ge(S("gathered"), 2 * i + b + 1)
                    act.activation(hc[:, 4 * b:4 * b + 4, :].rearrange("p k c -> p (k c)"), ps[6 + b][:, :], ACT.Copy).then_inc(S("gather_copied"), 1)
                act.wait_ge(S("gates_turned"), i + 1)
                act.activation(GT, ps[3][:, 0:T], ACT.Copy).then_inc(S("gates_copied"), 1)
                for step in range(STEPS + 1):
                    if step < STEPS:
                        act.wait_ge(S("up_done"), i * STEPS + step + 1)
                        act.wait_ge(S("moe_hidden"), (i + 1) * STEPS + step - 1)
                        act.activation(sil[step % 2], ps[step % 2][:, 0:STEP], ACT.Silu).then_inc(S("moe_gated"), 1)
                    if step:
                        act.wait_ge(S("hidden_turned"), (i + 1) * STEPS + step)
                        act.activation(hidT[(step - 1) % 2].rearrange("p j c -> p (j c)"), ps[2][:, 0:T], ACT.Copy).then_inc(S("hidden_copied"), 1)
                act.wait_ge(S("moe_steps"), (i + 2) * STEPS)
                for b in range(2):
                    act.activation(yc[:, b * 512:(b + 1) * 512], ps[4 + b][:, :], ACT.Copy).then_inc(S("y_copied"), 1)

            with act.Fori(0, EXPERTS) as e:
                expert(e)
            act.wait_ge(S("flag_ready"), 1)
            busiest = act.value_load(flag[0:1, 0:1], min_val=0, max_val=T)
            with act.If(busiest > P):
                with act.Fori(0, EXPERTS) as e:
                    expert(e + EXPERTS)
            norm_of_x("norm_fin")

        @block.tensor
        def _(pe):
            def norm_sum(name, n):
                pe.wait_ge(S("squares"), n)
                for k in range(KT):
                    last = pe.matmul(bank(name)[:, 0:T], mean_ones, sq[:, k, :], start=(k == 0), stop=(k == KT - 1))
                last.then_inc(filled(name), 1)

            def project(w, names, rhs):
                pe.wait_ge(*arrived(w))
                for half in range(2):
                    name = f"{names}{half}"
                    wait_bank_free(pe, name)
                    for i in range(2):
                        n = 2 * half + i
                        for k in range(KT):
                            last = pe.matmul(bank(name)[:, i * T:(i + 1) * T], weights(w)[:, k, n * P:(n + 1) * P],
                                             rhs[:, k, :], start=(k == 0), stop=(k == KT - 1))
                    last.then_inc(filled(name), 1)

            def project_tokens(w, names, lhs):
                pe.wait_ge(*arrived(w))
                for half in range(2):
                    name = f"{names}{half}"
                    wait_bank_free(pe, name)
                    for k in range(KT):
                        last = pe.matmul(bank(name)[:, :], lhs[:, k, half * P:(half + 1) * P], weights(w)[:, k, :],
                                         start=(k == 0), stop=(k == KT - 1))
                    last.then_inc(filled(name), 1)

            def low_rank(names, m, rows, rhs):
                for half in range(2):
                    name = f"{names}{half}"
                    wait_bank_free(pe, name)
                    for i in range(2):
                        n = 2 * half + i
                        last = pe.matmul(bank(name)[:, i * T:(i + 1) * T], smallw[0:rows, m, n * P:(n + 1) * P], rhs[0:rows, :],
                                         start=True, stop=True)
                    last.then_inc(filled(name), 1)

            def head_sums(names, src, matrix=head_ones):
                for half in range(2):
                    name = f"{names}{half}"
                    wait_bank_free(pe, name)
                    for i in range(2):
                        last = pe.matmul(bank(name)[:, i * T:(i + 1) * T], matrix, src[:, 2 * half + i, :], start=True, stop=True)
                    last.then_inc(filled(name), 1)

            pe.sem_inc(S("moe_steps"), STEPS)
            pe.sem_inc(S("y_copied"), 2)
            pe.sem_inc(S("moe_added"), 4)
            pe.sem_inc(S("moe_hidden"), STEPS)
            pe.sem_inc(S("hidden_copied"), STEPS)
            pe.sem_inc(S("hidden_turned"), STEPS)
            pe.wait_ge(S("con_loaded"), 16)
            norm_sum("norm_mix0", 1)
            norm_sum("norm_mem", 2)
            pe.wait_ge(S("norm_scaled"), KT)
            w = ring[:, place["w_lora"][0], 0:KT * 160].rearrange("p (k n) -> p k n", k=KT)
            pe.wait_ge(*arrived("w_lora"))
            for name, i, c0, c1 in (("wd_ad", 0, 0, 32), ("wd_ad", 1, 32, 64), ("gd", 0, 64, 160)):
                for k in range(KT):
                    last = pe.matmul(bank(name)[0:c1 - c0, i * T:(i + 1) * T], w[:, k, c0:c1], h[:, k, :], start=(k == 0), stop=(k == KT - 1))
                if (name, i) != ("wd_ad", 0):
                    last.then_inc(filled(name), 1)
            project("w_r", "r", h)
            project("w_k", "k", h)
            pe.wait_ge(S("smallw_loaded"), 16)
            pe.wait_ge(S("low_rank_in"), 1)
            low_rank("z", 0, 32, lw)
            low_rank("a", 1, 32, la)
            pe.wait_ge(S("low_rank_in"), 2)
            low_rank("rg", 2, 96, lg)
            project("w_v", "v", h)
            pe.wait_ge(S("kk_squared"), 1)
            head_sums("kk", tC)
            project("w_q", "q", h)
            project("w_f", "f", h)
            project_tokens("w_i", "i", h)
            project("w_g", "g", h)
            pe.wait_ge(S("bonus_in"), 4)
            head_sums("bonus", tC)
            for c in range(2):
                wait_bank_free(pe, f"vn{c}")
                pe.wait_ge(*was_read("v1"))
                for n in range(4):
                    last = pe.transpose(bank(f"vn{c}")[:, n * P:(n + 1) * P], rv[:, n, c * C:(c + 1) * C], ident)
                last.then_inc(filled(f"vn{c}"), 1)
            pe.wait_ge(S("norm_scaled"), 2 * KT)
            project("kv0_0", "kv_0", memn)
            project("kv0_1", "kv_1", memn)

            def head_rows(head):
                return slice(RW_N * (head % 2), RW_N * (head % 2) + RW_N)

            def scores(c):
                for head in range(8):
                    n, rows, name = head // 2, head_rows(head), f"sc{c}_{head}"
                    if head == 0:
                        pe.wait_ge(S("tildes"), 1)
                    wait_bank_free(pe, name)
                    pb = bank(name)
                    pe.matmul(pb[:, 0:P], AR[rows, n, c, 0, :], bt[rows, n, c * C:(c + 1) * C], start=True, stop=True)
                    pe.matmul(pb[:, P:2 * P], bt[rows, n, c * C:(c + 1) * C], AR[rows, n, c, 1, :], start=True, stop=True)
                    pe.matmul(pb[:, 2 * P:4 * P], kt[rows, n, c * C:(c + 1) * C], AR[rows, n, c, :, :].rearrange("p two t -> p (two t)"),
                              start=True, stop=True).then_inc(filled(name), 1)
                if c == 0:
                    for m, src in ((0, bt), (1, kt)):
                        name = f"bkn{m}"
                        wait_bank_free(pe, name)
                        for n in range(4):
                            last = pe.transpose(bank(name)[:, n * P:(n + 1) * P], src[:, n, 0:C], ident)
                        last.then_inc(filled(name), 1)

            def invert(c, l):
                if l == 0:
                    pe.wait_ge(S("A_copied"), 8 * (c + 1))
                    pe.wait_ge(S("XY_ready"), c + 1)
                for g in range(2):
                    name = f"V{c}_{l}_{g}"
                    wait_bank_free(pe, name)
                    if l:
                        pe.wait_ge(*was_read(f"dY{c}_{l - 1}_{g}"))
                    for i in range(4):
                        last = pe.matmul(bank(name)[:, i * P:(i + 1) * P], Am[:, 4 * g + i, :], Y[:, 4 * g + i, :], start=True, stop=True)
                    last.then_inc(filled(name), 1)
                for g in range(2):
                    pe.wait_ge(*was_read(f"V{c}_{l}_{g}"))
                    if l < LEVELS - 1:
                        name = f"dX{c}_{l}_{g}"
                        wait_bank_free(pe, name)
                        for i in range(4):
                            last = pe.matmul(bank(name)[:, i * P:(i + 1) * P], V[:, 4 * g + i, :], X[:, 4 * g + i, :], start=True, stop=True)
                        last.then_inc(filled(name), 1)
                    name = f"dY{c}_{l}_{g}"
                    wait_bank_free(pe, name)
                    for i in range(4):
                        last = pe.matmul(bank(name)[:, i * P:(i + 1) * P], X[:, 4 * g + i, :], V[:, 4 * g + i, :], start=True, stop=True)
                    last.then_inc(filled(name), 1)

            def head_cols(head):
                return slice(RW_N * head, RW_N * head + RW_N)

            def solve(c):
                name = f"R{c}"
                wait_bank_free(pe, name)
                pe.wait_ge(*was_read(f"sc{c}_7"))
                for c_ in range(2):
                    pe.wait_ge(*was_read(f"vn{c_}"))
                if c == 1:
                    pe.wait_ge(*was_read("M0"))
                for n in range(4):
                    if c == 1:
                        pe.matmul(bank(name)[:, n * P:(n + 1) * P], AR[:, n, c, 0, :], M0[:, n, :, :].rearrange("p two v -> p (two v)"),
                                  start=True, stop=False, skip_group_check=True)
                    for head in (2 * n, 2 * n + 1):
                        last = pe.matmul(bank(name)[:, head_cols(head)], SC[:, head, 1, :], vn[:, c, head_cols(head)],
                                         start=(c == 0), stop=True, skip_group_check=True)
                last.then_inc(filled(name), 1)
                for g in range(2):
                    pe.wait_ge(*was_read(f"dY{c}_{LEVELS - 1}_{g}"))
                pe.wait_ge(*was_read(name))
                name = f"U{c}"
                wait_bank_free(pe, name)
                for head in range(8):
                    last = pe.matmul(bank(name)[:, head_cols(head)], Y[:, head, :], flat(R)[:, head_cols(head)], start=True, stop=True)
                last.then_inc(filled(name), 1)
                pe.wait_ge(*was_read(name))
                if c == 0:
                    wait_bank_free(pe, "M0")
                    for m in range(2):
                        pe.wait_ge(*was_read(f"bkn{m}"))
                    for head in range(8):
                        pb = bank("M0")[head_rows(head), head_cols(head // 2)]
                        pe.matmul(pb, bkn[:, 0, head_cols(head)], flat(U)[:, head_cols(head)], start=True, stop=False)
                        last = pe.matmul(pb, bkn[:, 1, head_cols(head)], vn[:, 0, head_cols(head)], start=False, stop=True)
                    last.then_inc(filled("M0"), 1)
                name = f"ro{c}"
                wait_bank_free(pe, name)
                for n in range(4):
                    if c == 1:
                        pe.matmul(bank(name)[:, n * P:(n + 1) * P], M0[:, n, :, :].rearrange("p two v -> p (two v)"), AR[:, n, c, 1, :],
                                  start=True, stop=False, skip_group_check=True)
                    for head in (2 * n, 2 * n + 1):
                        pb = bank(name)[head_rows(head), n * P:(n + 1) * P]
                        pe.matmul(pb, flat(U)[:, head_cols(head)], SC[:, head, 0, :], start=(c == 0), stop=False, skip_group_check=True)
                        last = pe.matmul(pb, vn[:, c, head_cols(head)], SC[:, head, 2, :], start=False, stop=True, skip_group_check=True)
                last.then_inc(filled(name), 1)

            def level(i):
                if i == 0:
                    for b in range(2):
                        wait_bank_free(pe, f"ho{b}")
                if i <= LEVELS:
                    for b in range(2):
                        name = f"att{i}_{b}"
                        wait_bank_free(pe, name)
                        if i == 0:
                            for half in range(2):
                                pe.wait_ge(*was_read(f"q{half}"))
                                pe.wait_ge(*was_read(f"f{half}"))
                            left, right = hk, hq
                        else:
                            pe.wait_ge(S("level_ready"), i)
                            left = right = tiles4(F[i % 2])
                        for j in range(4):
                            head, c = 2 * b + j // 2, j % 2
                            last = pe.matmul(bank(name)[:, j * P:(j + 1) * P], left[:, head, c * C:(c + 1) * C],
                                             right[:, head, c * C:(c + 1) * C], start=True, stop=True)
                        last.then_inc(filled(name), 1)
                    for b in range(2):
                        name = f"att{i}_{b}"
                        pe.wait_ge(*was_read(name))
                        if i == 0:
                            for half in range(2):
                                pe.wait_ge(*was_read(f"i{half}"))
                        for j in range(4):
                            head, c = 2 * b + j // 2, j % 2
                            last = pe.matmul(ps[6 + b][:, j * P:(j + 1) * P], hi[:, c, head * P:(head + 1) * P],
                                             att[b][:, j * P:(j + 1) * P], start=(i == 0 and j == 0), stop=False, skip_group_check=True)
                        last.then_inc(S("att_used"), 1)
                else:
                    name = f"att{i}_0"
                    wait_bank_free(pe, name)
                    pe.wait_ge(S("level_ready"), i)
                    f = tiles4(F[i % 2])
                    for head in range(4):
                        last = pe.matmul(bank(name)[:, head * P:(head + 1) * P], f[:, head, 0:C], f[:, head, C:T], start=True, stop=True)
                    last.then_inc(filled(name), 1)
                    pe.wait_ge(*was_read(name))
                    for head in range(4):
                        b, j = head // 2, 2 * (head % 2) + 1
                        last = pe.matmul(ps[6 + b][:, j * P:(j + 1) * P], hi[:, 0, head * P:(head + 1) * P],
                                         att[0][:, head * P:(head + 1) * P], start=False, stop=True, skip_group_check=True)
                        if head % 2:
                            last.then_inc(filled(f"ho{b}"), 1)

            for step in order:
                if step[0] == "scores":
                    scores(step[1])
                elif step[0] == "invert":
                    invert(*step[1:])
                elif step[0] == "level":
                    level(step[1])
                elif step[0] == "kv":
                    project_tokens(f"kv0_{step[1]}", f"kv_{step[1]}", memn)
                elif step[0] == "solve":
                    solve(step[1])
            pe.wait_ge(S("ho_squared"), 1)
            head_sums("hsum", tiles4(F[0]), ones)
            for c in range(2):
                pe.wait_ge(*was_read(f"ro{c}"))
            head_sums("mean", ro)
            pe.wait_ge(S("ro_squared"), 1)
            head_sums("var", tA)

            pe.wait_ge(S("ya_ready"), 1)
            pe.wait_ge(S("yb_ready"), 1)
            project("wout0", "out_0", h)
            project("wout1", "out_1", h)
            norm_done = [2]

            def sum_squares(name):
                wait_bank_free(pe, name)
                n = squares_before[name]
                for b in range(4):
                    pe.wait_ge(S("squares"), n + b + 1)
                    for k in (2 * b, 2 * b + 1):
                        last = pe.matmul(bank(name)[:, 0:T], mean_ones, sq[:, k, :], start=(k == 0), stop=(k == KT - 1))
                last.then_inc(filled(name), 1)
                norm_done[0] += 1
                pe.wait_ge(S("norm_scaled"), KT * norm_done[0])

            def cross_attention(l):
                sum_squares(f"norm_xat{l}")
                for c in range(2):
                    project(f"wq{l}_{c}", f"q{l}_{c}", h)
                if l == 1:
                    for c in range(4):
                        pe.wait_ge(*was_read(f"kv1_{c}1"))
                for head in range(4):
                    name = f"s{l}_{head}"
                    wait_bank_free(pe, name)
                    pe.wait_ge(*was_read(f"q{l}_{head // 2}{head % 2}"))
                    for b in range(2):
                        for k in (2 * head, 2 * head + 1):
                            last = pe.matmul(bank(name)[:, b * T:(b + 1) * T], qT[:, k, b * P:(b + 1) * P], kT[:, k, :],
                                             start=(k == 2 * head), stop=(k == 2 * head + 1))
                    last.then_inc(filled(name), 1)
                for head in range(4):
                    name = f"pt{l}_{head}"
                    wait_bank_free(pe, name)
                    pe.wait_ge(S("prob_normed"), 4 * l + head + 1)
                    for m in range(2):
                        for b in range(2):
                            last = pe.transpose(bank(name)[:, m * T + b * P:m * T + (b + 1) * P], prob[:, head, b, m * P:(m + 1) * P], ident)
                    last.then_inc(filled(name), 1)
                    pe.wait_ge(*was_read(name))
                    name = f"pv{l}_{head}"
                    wait_bank_free(pe, name)
                    for i in range(2):
                        for m in range(2):
                            last = pe.matmul(bank(name)[:, i * T:(i + 1) * T], vN[:, m, (2 * head + i) * P:(2 * head + i + 1) * P],
                                             pT[:, head, m, :], start=(m == 0), stop=(m == 1))
                    last.then_inc(filled(name), 1)
                for head in range(4):
                    pe.wait_ge(*was_read(f"pv{l}_{head}"))
                for c in range(2):
                    project(f"wo{l}_{c}", f"xo{l}_{c}", h)

            cross_attention(0)

            sum_squares("norm_ffn0")

            def step_up(step):
                pe.wait_ge(*arrived(f"ffn{step}"))
                w = weights(f"ffn{step}")
                for j in range(2):
                    name = f"f{step}_{j}"
                    wait_bank_free(pe, name)
                    for i in range(2):
                        c0 = i * STEP + j * P
                        for k in range(KT):
                            last = pe.matmul(bank(name)[:, i * T:(i + 1) * T], w[:, k, c0:c0 + P], h[:, k, :], start=(k == 0), stop=(k == KT - 1))
                    last.then_inc(filled(name), 1)

            def step_down(step):
                w = ring[:, place[f"ffn{step}"][0], DENSE:SLOT].rearrange("p (j n) -> p j n", j=2)
                pe.wait_ge(S("hidden"), 2 * step + 2)
                for n in range(KT):
                    if step == 0 and n % 2 == 0:
                        wait_bank_free(pe, f"fo{n // 2}")
                    for j in range(2):
                        last = pe.matmul(ps[4 + n // 2][:, (n % 2) * T:(n % 2 + 1) * T], w[:, j, n * P:(n + 1) * P], fh[step % 2][:, j, :],
                                         start=(step == 0 and j == 0 and n % 2 == 0), stop=(step == STEPS - 1 and j == 1), skip_group_check=True)
                    if step == STEPS - 1 and n % 2:
                        last.then_inc(filled(f"fo{n // 2}"), 1)
                if step < STEPS - 1:
                    last.then_inc(S("ffn_steps"), 1)

            def s5_piece(p):
                pe.wait_ge(S("s5_w1t"), p + 1)
                for w, name in enumerate(("re", "im")):
                    name = f"{name}_{p}"
                    wait_bank_free(pe, name)
                    for g in range(PIECE):
                        last = pe.transpose(bank(name)[:, g * P:(g + 1) * P], sW1T[:, w, g, :, :].rearrange("p k m -> p (k m)"), ident)
                    last.then_inc(filled(name), 1)
                pe.wait_ge(S("s5_cw"), p + 1)
                for par_ in range(2):
                    name = f"k{par_}_{p}"
                    wait_bank_free(pe, name)
                    rows = slice(S5_P * par_, S5_P * (par_ + 1))
                    for g in range(PIECE):
                        for w in range(2):
                            last = pe.matmul(bank(name)[0:S5_M, g * P:(g + 1) * P], sbb[rows, w, PIECE * p + g, :],
                                             sCW[rows, g, w, 0:TAU, :].rearrange("p k m -> p (k m)"), start=(w == 0), stop=(w == 1))
                    last.then_inc(filled(name), 1)

            for step in range(STEPS):
                step_up(step)
                if step:
                    step_down(step - 1)
                if 3 <= step and step - 3 < PIECES:
                    s5_piece(step - 3)
            step_down(STEPS - 1)

            sum_squares("norm_mix1")
            project("cw0", "u_0", h)
            project("cw1", "u_1", h)
            project("kv1_0", "kv1_0", memn)
            project("kv1_1", "kv1_1", memn)
            pe.wait_ge(S("u_blocks"), 16 * TAU)
            table = lambda name: ring[:, place[name][0], 0:DENSE]
            for half in range(2):
                pe.wait_ge(*arrived(f"s5_W1_{half}"))
                for w in range(2):
                    wait_bank_free(pe, f"Z{w}{half}")
                w1 = table(f"s5_W1_{half}").rearrange("p (g w c) -> p g w c", g=PAIRS // 2, w=2)
                for w in range(2):
                    for g in range(PAIRS // 2):
                        for par_ in range(2):
                            rows = slice(S5_P * par_, S5_P * (par_ + 1))
                            last = pe.matmul(bank(f"Z{w}{half}")[rows, g * BLOCKS:(g + 1) * BLOCKS], w1[:, g, w, rows],
                                             Ub[:, PAIRS * half + 2 * g + par_, :], start=True, stop=True)
                    last.then_inc(filled(f"Z{w}{half}"), 1)
            project_tokens("kv1_2", "kv1_2", memn)
            project_tokens("kv1_3", "kv1_3", memn)
            pe.wait_ge(S("states"), 1)
            for half in range(2):
                pe.wait_ge(*arrived(f"s5_T_{half}"))
                pe.wait_ge(*arrived(f"s5_W2_{half}"))
                for par_ in range(2):
                    wait_bank_free(pe, f"Y{par_}{half}")
                tt = table(f"s5_T_{half}").rearrange("p (g c) -> p g c", g=PAIRS)
                w2 = table(f"s5_W2_{half}").rearrange("p (g w c) -> p g w c", g=PAIRS // 2, w=2)
                for par_ in range(2):
                    rows = slice(S5_P * par_, S5_P * (par_ + 1))
                    for g in range(PAIRS // 2):
                        pb = bank(f"Y{par_}{half}")[:, g * BLOCKS:(g + 1) * BLOCKS]
                        pe.matmul(pb, tt[:, 2 * g + par_, :], Ub[:, PAIRS * half + 2 * g + par_, :], start=True, stop=False)
                        for w in range(2):
                            last = pe.matmul(pb, w2[rows, g, w, :], Xs[rows, w, 16 * half + g, :], start=False, stop=(w == 1))
                    last.then_inc(filled(f"Y{par_}{half}"), 1)
            pe.wait_ge(S("gelu"), KT)
            for c in range(4):
                pe.wait_ge(*arrived(f"glu{c}"))
                for i, name in enumerate((f"val{c}", f"gate{c}")):
                    wait_bank_free(pe, name)
                    for j in range(2):
                        c0 = i * 256 + j * P
                        for k in range(KT):
                            last = pe.matmul(bank(name)[:, j * T:(j + 1) * T], weights(f"glu{c}")[:, k, c0:c0 + P], h[:, k, :],
                                             start=(k == 0), stop=(k == KT - 1))
                    last.then_inc(filled(name), 1)
            cross_attention(1)

            sum_squares("norm_ffn1")
            pe.wait_ge(S("router_loaded"), 16)
            wait_bank_free(pe, "logits")
            for b in range(2):
                for k in range(KT):
                    last = pe.matmul(bank("logits")[:, b * EXPERTS:(b + 1) * EXPERTS], h[:, k, b * P:(b + 1) * P], router[:, k, :],
                                     start=(k == 0), stop=(k == KT - 1))
            last.then_inc(filled("logits"), 1)
            for m in range(4):
                name = f"hN{m}"
                wait_bank_free(pe, name)
                for i in range(4):
                    k = 4 * (m % 2) + i
                    last = pe.transpose(bank(name)[:, i * P:(i + 1) * P], h[:, k, (m // 2) * P:(m // 2 + 1) * P], ident)
                last.then_inc(filled(name), 1)
            pe.wait_ge(S("selected"), 1)
            wait_bank_free(pe, "places")
            strict = con[:, CONST_COLS["strict"], :]
            pb = bank("places")
            pe.matmul(pb[:, 0:8], strict, sel[:, 0, :], start=True, stop=True)
            pe.matmul(pb[:, 8:16], strict, sel[:, 1, :], start=True, stop=False)
            pe.matmul(pb[:, 8:16], ones, sel[:, 0, :], start=False, stop=True)
            pe.matmul(pb[:, 16:24], ones, sel[:, 0, :], start=True, stop=False)
            pe.matmul(pb[:, 16:24], ones, sel[:, 1, :], start=False, stop=True).then_inc(filled("places"), 1)
            for m in range(4):
                pe.wait_ge(*was_read(f"hN{m}"))

            def expert(i, rnd):
                pe.wait_ge(S("slots_ready"), i + 1 + rnd)
                pe.wait_ge(S("moe_added"), (i + 1) * 4)
                for b in range(2):
                    for k in range(4):
                        for c in range(2):
                            last = pe.matmul(ps[6 + b][:, k * P:(k + 1) * P], hN[:, c, (4 * b + k) * P:(4 * b + k + 1) * P], Gs[:, c, :],
                                             start=(c == 0), stop=(c == 1))
                    last.then_inc(S("gathered"), 1)
                for c in range(2):
                    last = pe.transpose(ps[3][:, c * P:(c + 1) * P], Gg[:, c, :], ident)
                last.then_inc(S("gates_turned"), 1)
                pe.wait_ge(S("gather_copied"), 2 * i + 2)

                def up(step):
                    slot = step % RING
                    use = first_use[slot] + step // RING
                    pe.wait_ge(S(f"slot{slot}_filled"), i * (16 * per_expert[slot]) + 16 * (use + 1))
                    pe.wait_ge(S("moe_hidden"), (i + 1) * STEPS + max(step - 1, 0))
                    w = ring[:, slot, 0:DENSE].rearrange("p (k n) -> p k n", k=KT)
                    for k in range(KT):
                        last = pe.matmul(ps[step % 2][:, :], hc[:, k, :], w[:, k, :], start=(k == 0), stop=(k == KT - 1))
                    last.then_inc(S("up_done"), 1)

                def turn(step):
                    pe.wait_ge(S("moe_hidden"), (i + 1) * STEPS + step + 1)
                    pe.wait_ge(S("hidden_copied"), (i + 1) * STEPS + step)
                    for j in range(2):
                        last = pe.transpose(ps[2][:, j * P:(j + 1) * P], hid[step % 2][:, j * P:(j + 1) * P], ident)
                    last.then_inc(S("hidden_turned"), 1)

                def down(step):
                    pe.wait_ge(S("hidden_copied"), (i + 1) * STEPS + step + 1)
                    if step == 0:
                        pe.wait_ge(S("y_copied"), 2 * i + 2)
                    w = ring[:, step % RING, DENSE:SLOT].rearrange("p (j n) -> p j n", j=2)
                    for j in range(2):
                        for b in range(2):
                            last = pe.matmul(ps[4 + b][:, :], hidT[step % 2][:, j, :], w[:, j, b * 512:(b + 1) * 512],
                                             start=(step == 0 and j == 0), stop=(step == STEPS - 1 and j == 1), skip_group_check=True)
                    last.then_inc(S("moe_steps"), 1)

                for step in range(STEPS):
                    up(step)
                    if step >= 2:
                        down(step - 2)
                    if step >= 1:
                        turn(step - 1)
                down(STEPS - 2)
                turn(STEPS - 1)
                down(STEPS - 1)
                pe.wait_ge(S("y_copied"), 2 * i + 4)
                pe.wait_ge(S("gates_copied"), i + 1)
                for m in range(4):
                    pe.wait_ge(S("moe_added"), i * 4 + max(m - 1, 0) + 4)
                    for j in range(2):
                        n = 2 * m + j
                        last = pe.matmul(ps[6 + m % 2][:, j * T:(j + 1) * T], yc[:, n * P:(n + 1) * P], GT, start=True, stop=True)
                    last.then_inc(S("scattered"), 1)

            with pe.Fori(0, EXPERTS) as e:
                expert(e, 0)
            pe.wait_ge(S("flag_ready"), 1)
            busiest = pe.value_load(flag[0:1, 0:1], min_val=0, max_val=T)
            with pe.If(busiest > P):
                with pe.Fori(0, EXPERTS) as e:
                    expert(e + EXPERTS, 1)
            sum_squares("norm_fin")

        @block.vector
        def _(dve):
            linked = [0]

            def link(ins):
                linked[0] += 1
                ins.then_inc(S("dve_link"), 1)
                dve.wait_ge(S("dve_link"), linked[0])

            norms = [0]

            def normalise(name, src, gain, dst):
                dve.wait_ge(*was_read(name))
                if norms[0]:
                    dve.wait_ge(S("norm_scaled"), norms[0])
                norms[0] += KT
                link(dve.reciprocal(rstd[:, :], nrm[:, :]))
                for k in range(KT):
                    dve.scalar_tensor_tensor(out=dst[:, k, :], in0=src[:, k, :], scalar=pc(gain, k), in1=rstd[:, :],
                                             op0=ALU.mult, op1=ALU.mult).then_inc(S("norm_scaled"), 1)

            dve.wait_ge(S("par_loaded"), 16)
            dve.tensor_scalar(omu[:, :], par[:, MU0:MU1], -1.0, 1.0, ALU.mult, ALU.add).then_inc(S("omu_ready"), 1)
            lb = pc("lb", 0, P, 4)
            dve.tensor_tensor(lbs[:, 0, :], lb, lb, ALU.subtract).then_inc(S("lb_shifted"), 1)
            dve.wait_ge(S("x_loaded"), 16)
            normalise("norm_mix0", x, "mix0", h)
            dve.wait_ge(S("mem_loaded"), 16)
            normalise("norm_mem", memn, "memg", memn)
            dve.wait_ge(S("lb_exp"), 1)
            link(dve.reciprocal(lbs[:, 0, :], lbs[:, 1, :]))
            link(dve.tensor_tensor(lbs[:, 0, :], lbs[:, 0, :], lbs[:, 1, :], ALU.mult))
            link(dve.tensor_tensor(lbs[:, 2, :], lbs[:, 0, :], lbs[:, 0, :], ALU.subtract))
            dve.tensor_scalar(lbs[:, 3, :], lbs[:, 2, :], -1.0, 1.0, ALU.mult, ALU.add).then_inc(S("lb_ready"), 1)

            def shifted(dst, src, mu, own):
                dve.wait_ge(S("own_part"), own)
                return dve.scalar_tensor_tensor(out=dst[:, 1:T], in0=src[:, 0:T - 1], scalar=mu, in1=dst[:, 1:T],
                                                op0=ALU.mult, op1=ALU.add)

            shifted(lw[0:32, :], bank("wd_ad")[0:32, 0:T], pc("mu_wd", 0, 32), 2).then_inc(read("wd_ad"), 1)
            shifted(la[0:32, :], bank("wd_ad")[0:32, T:2 * T], pc("mu_ad", 0, 32), 2).then_inc(read("wd_ad"), 1)
            shifted(lg[0:96, :], bank("gd")[0:96, 0:T], pc("mu_gd", 0, 96), 3).then_inc(read("gd"), 1)

            def shift(name, dst, own):
                for half in range(2):
                    for i in range(2):
                        n = 2 * half + i
                        last = shifted(dst[:, n, :], bank(f"{name}{half}")[:, i * T:(i + 1) * T], pc("mu_" + name, n), own + 2 * half + 2)
                    last.then_inc(read(f"{name}{half}"), 1)

            shift("r", rr, 3)
            shift("k", rk, 7)
            for half in range(2):
                dve.wait_ge(*was_read(f"z{half}"))
            link(dve.tensor_scalar(ld, ld, -float(np.exp(-0.5)), None, ALU.mult))
            for n in range(4):
                for c in range(2):
                    last = dve.tensor_tensor_scan(cL[:, n, c * C:(c + 1) * C], ones, ld[:, n, c * C:(c + 1) * C], 0.0, ALU.mult, ALU.add)
            link(last)
            shift("v", rv, 11)
            for half in range(2):
                dve.wait_ge(*is_filled(f"kk{half}"))
                dve.tensor_scalar(flat(tC[:, 2 * half:2 * half + 2, :]), bank(f"kk{half}")[:, :], 1e-24, None, ALU.max).then_inc(read(f"kk{half}"), 1)
            dve.wait_ge(S("kk_root"), 1)
            link(dve.reciprocal(tC, tC))
            link(dve.tensor_tensor(kk, kk, tC, ALU.mult))
            for half in range(2):
                dve.wait_ge(*was_read(f"a{half}"))
            for n in range(4):
                last = dve.tensor_scalar(tC[:, n, :], ra[:, n, :], -1.0, pc("k_a", n), ALU.add, ALU.mult)
            link(last)
            link(dve.scalar_tensor_tensor(out=rk, in0=tC, scalar=1.0, in1=rk, op0=ALU.add, op1=ALU.mult))
            dve.tensor_tensor(ra, ra, kk, ALU.mult)
            for n in range(4):
                dve.scalar_tensor_tensor(out=tC[:, n, :], in0=rr[:, n, :], scalar=pc("r_k", n), in1=rk[:, n, :],
                                         op0=ALU.mult, op1=ALU.mult).then_inc(S("bonus_in"), 1)
            mid = small[:, 4:12].rearrange("p (n c) -> p n c", n=4)
            cL8 = flat(cL).rearrange("p (m t) -> p m t", t=C)
            link(dve.tensor_copy(small[:, 4:12], cL8[:, :, C // 2 - 1]))
            dve.tensor_copy(small[:, 0:4], mid[:, :, 1])
            link(dve.tensor_tensor(cL8, cL8, small[:, 4:12].rearrange("p (m o) -> p m o", o=1).broadcast_to([P, 8, C]), ALU.subtract))
            dve.tensor_tensor(ld, cL, ld, ALU.subtract).then_inc(S("decays_in"), 1)

            for half in range(2):
                dve.wait_ge(S("q_sigmoid"), half + 1)
                v = flat(hq[:, 2 * half:2 * half + 2, :])
                dve.tensor_tensor(v, v, bank(f"q{half}")[:, :], ALU.mult).then_inc(read(f"q{half}"), 1)
            for half in range(2):
                dve.wait_ge(S("f_sigmoid"), half + 1)
                for i in range(2):
                    n = 2 * half + i
                    dve.tensor_scalar(hk[:, n, :], hk[:, n, :], lbs[:, 3, n:n + 1], None, ALU.mult)
                pb = bank(f"f{half}")[:, :]
                sl = slice(half * 512, (half + 1) * 512)
                dve.tensor_scalar(flat(hL)[:, sl], pb, 0.0, None, ALU.min)
                dve.tensor_scalar(F[1][:, sl], pb, -1.0, 60.0, ALU.mult, ALU.min).then_inc(read(f"f{half}"), 1)
            for half in range(2):
                dve.wait_ge(S("g_sigmoid"), half + 1)
                v = flat(hg[:, 2 * half:2 * half + 2, :])
                dve.tensor_tensor(v, v, bank(f"g{half}")[:, :], ALU.mult).then_inc(read(f"g{half}"), 1)
            dve.wait_ge(S("decays_out"), 2)
            v4 = lambda a: a.rearrange("p n (c t) -> p n c t", c=2)
            for n in range(4):
                a, b = v4(kk)[:, n], v4(tB)[:, n]
                dve.scalar_tensor_tensor(out=AR[:, n, :, 0, :], in0=a, scalar=-1.0, in1=b, op0=ALU.mult, op1=ALU.mult)
                last = dve.tensor_tensor(AR[:, n, :, 1, :], v4(rr)[:, n], v4(cL)[:, n], ALU.mult)
            dve.tensor_tensor(bt, ra, tA, ALU.mult)
            dve.tensor_tensor(kt, rk, tA, ALU.mult)
            dve.tensor_tensor(small[:, 0:4], small[:, 0:4], cL[:, :, C - 1], ALU.mult).then_inc(S("tildes"), 1)
            for half in range(2):
                dve.wait_ge(*is_filled(f"bonus{half}"))
                dve.tensor_tensor(flat(bonus[:, 2 * half:2 * half + 2, :]), bank(f"bonus{half}")[:, :],
                                  flat(rv[:, 2 * half:2 * half + 2, :]), ALU.mult).then_inc(read(f"bonus{half}"), 1)
            dve.wait_ge(S("f_logs"), 1)
            link(dve.tensor_tensor(flat(hL), flat(hL), F[0], ALU.subtract))
            link(dve.tensor_tensor(F[0], flat(hL), F[1], ALU.add))
            for n in range(4):
                last = dve.tensor_tensor_scan(hL[:, n, :], flat(cc("ones", 2)),
                                              F[0][:, n * T:(n + 1) * T], 0.0, ALU.mult, ALU.add)
            link(last)

            def distances(i):
                if i == 0 or i > LEVELS + 1:
                    return
                w = 1 << (i - 1)
                L = flat(hL).rearrange("p (b u) -> p b u", u=2 * w)
                f = F[i % 2].rearrange("p (b u) -> p b u", u=2 * w)
                edge = L[:, :, w - 1:w].broadcast_to([P, 1024 // (2 * w), w])
                if i > 2:
                    dve.wait_ge(*is_filled(f"att{i - 2}_1"))
                dve.tensor_tensor(f[:, :, 0:w], edge, L[:, :, 0:w], ALU.subtract)
                dve.tensor_tensor(f[:, :, w:2 * w], L[:, :, w:2 * w], edge, ALU.subtract).then_inc(S("distances"), 1)

            def factors(i):
                if i == 0 or i > LEVELS + 1:
                    return
                w = 1 << (i - 1)
                f = F[i % 2].rearrange("p (b u) -> p b u", u=2 * w)
                dve.wait_ge(S("level_decays"), i)
                k = flat(hk).rearrange("p (b u) -> p b u", u=2 * w)
                q = flat(hq).rearrange("p (b u) -> p b u", u=2 * w)
                dve.tensor_tensor(f[:, :, 0:w], f[:, :, 0:w], k[:, :, 0:w], ALU.mult)
                dve.tensor_tensor(f[:, :, w:2 * w], f[:, :, w:2 * w], q[:, :, w:2 * w], ALU.mult).then_inc(S("level_ready"), 1)

            def level(i):
                distances(i + 1)
                for b in range(2 if i <= LEVELS else 1):
                    name = f"att{i}_{b}"
                    dve.wait_ge(*is_filled(name))
                    if i:
                        dve.wait_ge(S("att_used"), 2 * (i - 1) + b + 1)
                    if i <= LEVELS:
                        mask = con[:, i:i + 1, :].broadcast_to([P, 4, P])
                        dve.tensor_tensor(stack(att[b], 4), stack(bank(name)[:, :], 4), mask, ALU.mult).then_inc(read(name), 1)
                    else:
                        dve.tensor_copy(att[0], bank(name)[:, :]).then_inc(read(name), 1)
                factors(i + 1)

            def scores(c):
                if c == 0:
                    link(dve.memset(M0, 0.0))
                else:
                    dve.wait_ge(*is_filled("ro0"))
                for head in range(8):
                    name = f"sc{c}_{head}"
                    dve.wait_ge(*is_filled(name))
                    dve.wait_ge(S("A_copied"), 8 * c + head + 1)
                    dve.tensor_tensor(SC[:, head, :, :], bank(name)[:, P:4 * P].rearrange("p (m t) -> p m t", m=3),
                                      cc("incl0", 3), ALU.mult).then_inc(read(name), 1)
                one = con[:, 0:1, :].broadcast_to([P, 8, P])
                dve.tensor_copy(X, one)
                dve.tensor_copy(Y, one).then_inc(S("XY_ready"), 1)

            def invert(c, l):
                half = lambda a, g: a[:, 4 * g:4 * g + 4, :]
                mask = con[:, 1 + l:2 + l, :].broadcast_to([P, 4, P])
                for g in range(2):
                    name = f"V{c}_{l}_{g}"
                    dve.wait_ge(*is_filled(name))
                    if c or l:
                        before = f"dY{c}_{l - 1}_{g}" if l else f"dY{c - 1}_{LEVELS - 1}_{g}"
                        dve.wait_ge(*is_filled(before))
                    dve.tensor_tensor(half(V, g), stack(bank(name)[:, :], 4), mask, ALU.mult).then_inc(read(name), 1)
                for g in range(2):
                    dve.wait_ge(*is_filled(f"dY{c}_{l}_{g}"))
                    if l < LEVELS - 1:
                        dve.wait_ge(*is_filled(f"dX{c}_{l}_{g}"))
                        dve.tensor_tensor(half(X, g), half(X, g), stack(bank(f"dX{c}_{l}_{g}")[:, :], 4), ALU.add).then_inc(read(f"dX{c}_{l}_{g}"), 1)
                    dve.tensor_tensor(half(Y, g), half(Y, g), stack(bank(f"dY{c}_{l}_{g}")[:, :], 4), ALU.add).then_inc(read(f"dY{c}_{l}_{g}"), 1)

            for step in order:
                if step[0] == "scores":
                    scores(step[1])
                elif step[0] == "invert":
                    invert(*step[1:])
                elif step[0] == "level":
                    level(step[1])
                elif step == ("solve", 0):
                    dve.wait_ge(*is_filled("M0"))
                    for n in range(4):
                        for two in range(2):
                            rows = slice(RW_N * two, RW_N * two + RW_N)
                            last = dve.tensor_scalar(M0[rows, n, two, :], bank("M0")[rows, n * RW_N:(n + 1) * RW_N], small[rows, n:n + 1], None, ALU.mult)
                    last.then_inc(read("M0"), 1)
            for b in range(2):
                dve.wait_ge(*was_read(f"hsum{b}"))
            link(dve.reciprocal(F[1], F[1]))
            link(dve.scalar_tensor_tensor(out=flat(ho), in0=flat(ho), scalar=pc("onorm"), in1=F[1], op0=ALU.mult, op1=ALU.mult))
            for b in range(2):
                dve.wait_ge(*was_read(f"g{b}"))
            dve.tensor_tensor(h[:, 0:4, :], ho, hg, ALU.mult).then_inc(S("ya_ready"), 1)
            for b in range(2):
                name = f"mean{b}"
                dve.wait_ge(*is_filled(name))
                v = flat(ro[:, 2 * b:2 * b + 2, :])
                dve.scalar_tensor_tensor(out=v, in0=bank(name)[:, :], scalar=-1.0 / RW_N, in1=v, op0=ALU.mult, op1=ALU.add).then_inc(read(name), 1)
            for b in range(2):
                dve.wait_ge(*was_read(f"var{b}"))
            link(dve.reciprocal(tB, tB))
            link(dve.tensor_tensor(ro, ro, tB, ALU.mult))
            for n in range(4):
                last = dve.tensor_scalar(ro[:, n, :], ro[:, n, :], pc("gn_g", n), pc("gn_b", n), ALU.mult, ALU.add)
            link(last)
            for b in range(2):
                dve.wait_ge(*was_read(f"bonus{b}"))
                dve.wait_ge(*was_read(f"rg{b}"))
            link(dve.tensor_tensor(ro, ro, bonus, ALU.add))
            dve.tensor_tensor(h[:, 4:8, :], ro, rg, ALU.mult).then_inc(S("yb_ready"), 1)

            def add_to_x(name, b):
                dve.wait_ge(*is_filled(name))
                v = flat(x[:, 2 * b:2 * b + 2, :])
                dve.tensor_tensor(v, v, bank(name)[:, :], ALU.add).then_inc(S("x_written"), 1)
                x_written[0] += 1
                dve.wait_ge(S("x_written"), x_written[0])
                dve.sem_inc(read(name), 1)

            x_written = [0]

            def norm_of_x(name, gain, permuted=False):
                dve.wait_ge(*was_read(name))
                dve.wait_ge(S("norm_scaled"), norms[0])
                norms[0] += KT
                link(dve.reciprocal(rstd[:, :], nrm[:, :]))
                v = (lambda a: a.rearrange("p (j s) -> p s j", s=TAU)) if permuted else (lambda a: a)
                o = (lambda a: a.rearrange("p (s j) -> p s j", s=TAU)) if permuted else (lambda a: a)
                for k in range(KT):
                    dve.scalar_tensor_tensor(out=o(h[:, k, :]), in0=v(x[:, k, :]), scalar=pc(gain, k), in1=v(rstd[:, :]),
                                             op0=ALU.mult, op1=ALU.mult).then_inc(S("norm_scaled"), 1)

            def cross_attention(l):
                norm_of_x(f"norm_xat{l}", f"xat{l}")
                for head in range(4):
                    dve.wait_ge(*is_filled(f"s{l}_{head}"))
                    m = smax[:, 2 * head:2 * head + 2]
                    link(dve.tensor_reduce(m, bank(f"s{l}_{head}")[:, :].rearrange("p (b m) -> p b m", b=2), AX.X, ALU.max))
                    dve.tensor_scalar(m, m, -XA_SCALE, None, ALU.mult).then_inc(S("score_max"), 1)
                for head in range(4):
                    dve.wait_ge(*was_read(f"s{l}_{head}"))
                    m = ssum[:, 2 * head:2 * head + 2]
                    link(dve.reciprocal(m, m))
                    for b in range(2):
                        last = dve.tensor_scalar(prob[:, head, b, :], prob[:, head, b, :], ssum[:, 2 * head + b:2 * head + b + 1], None, ALU.mult)
                    last.then_inc(S("prob_normed"), 1)
                for c in range(2):
                    for half in range(2):
                        add_to_x(f"xo{l}_{c}{half}", 2 * c + half)

            for c in range(2):
                for half in range(2):
                    add_to_x(f"out_{c}{half}", 2 * c + half)
            cross_attention(0)
            norm_of_x("norm_ffn0", "ffn0")

            def w_(i):
                return sw[:, i, :]

            def tt(o, a, b, op):
                return dve.tensor_tensor(o, a, b, op)

            def ts(o, a, s1, s2, op0, op1=None):
                return dve.tensor_scalar(o, a, s1, s2, op0, op1) if op1 is not None else dve.tensor_scalar(o, a, s1, s2, op0)

            def product(o_re, o_im, a_re, a_im, b_re, b_im, work, conjugate=False):
                t0, t1, t2_, t3 = work
                tt(t0, a_re, b_re, ALU.mult)
                tt(t1, a_im, b_im, ALU.mult)
                tt(t2_, a_re, b_im, ALU.mult)
                link(tt(t3, a_im, b_re, ALU.mult))
                tt(o_re, t0, t1, ALU.add if conjugate else ALU.subtract)
                link(tt(o_im, t3, t2_, ALU.subtract if conjugate else ALU.add))

            def s5_angles():
                dve.wait_ge(S("s5_a_loaded"), 16)
                dve.wait_ge(S("s5_dt"), 1)
                link(ts(w_(9), sa[:, 0, :], -1e-4, None, ALU.min))
                tt(w_(1), w_(9), w_(0), ALU.mult)
                link(tt(w_(2), sa[:, 1, :], w_(0), ALU.mult))
                for dst, turn in ((5, 0.0), (7, 0.25)):
                    if turn:
                        link(ts(w_(8), w_(2), 1 / TWO_PI, turn, ALU.mult, ALU.add))
                    else:
                        link(ts(w_(8), w_(2), 1 / TWO_PI, None, ALU.mult))
                    link(ts(w_(8), w_(8), ROUNDER, None, ALU.add))
                    link(ts(w_(8), w_(8), ROUNDER, None, ALU.subtract))
                    link(dve.scalar_tensor_tensor(out=w_(dst), in0=w_(8), scalar=-TWO_PI_HI, in1=w_(2), op0=ALU.mult, op1=ALU.add))
                    link(dve.scalar_tensor_tensor(out=w_(dst), in0=w_(8), scalar=-(TWO_PI - TWO_PI_HI), in1=w_(dst), op0=ALU.mult, op1=ALU.add))
                    if turn:
                        link(ts(w_(dst), w_(dst), TWO_PI * turn, None, ALU.add))
                    link(ts(w_(dst), w_(dst), PI_BELOW, -PI_BELOW, ALU.min, ALU.max))
                dve.tensor_copy(w_(10), w_(2)).then_inc(S("s5_angles"), 1)

            def s5_base():
                dve.wait_ge(S("s5_sines"), 1)
                dve.wait_ge(S("s5_bc_loaded"), 16)
                pw = lambda w, k: spw[:, w, k, :]
                dve.memset(pw(0, 0), 1.0)
                dve.memset(pw(1, 0), 0.0)
                tt(pw(0, 1), w_(3), w_(6), ALU.mult)
                link(tt(pw(1, 1), w_(3), w_(4), ALU.mult))
                for k in range(2, TAU + 1):
                    product(pw(0, k), pw(1, k), pw(0, k - 1), pw(1, k - 1), pw(0, 1), pw(1, 1), [w_(12 + i) for i in range(4)])
                tt(w_(12), w_(9), w_(9), ALU.mult)
                tt(w_(13), sa[:, 1, :], sa[:, 1, :], ALU.mult)
                link(ts(w_(11), pw(0, 1), -1.0, None, ALU.add))
                link(tt(w_(12), w_(12), w_(13), ALU.add))
                link(dve.reciprocal(w_(10), w_(12)))
                product(w_(16), w_(17), w_(11), pw(1, 1), w_(9), sa[:, 1, :], [w_(12 + i) for i in range(4)], conjugate=True)
                tt(w_(16), w_(16), w_(10), ALU.mult)
                link(tt(w_(17), w_(17), w_(10), ALU.mult))
                wide = lambda v: v.rearrange("p (g o) -> p g o", o=1).broadcast_to([P, PAIRS, S5_M])
                q = [sCW_flat(i) for i in range(2)]
                c_re, c_im, b_re, b_im = wide(w_(16)), wide(w_(17)), sbc[:, 0, :, :], sbc[:, 1, :, :]
                g3 = lambda a: a.rearrange("p (g m) -> p g m", g=PAIRS)
                tt(g3(q[0]), c_re, b_re, ALU.mult)
                link(tt(g3(q[1]), c_im, b_im, ALU.mult))
                link(tt(sbb[:, 0, :, :], g3(q[0]), g3(q[1]), ALU.subtract))
                tt(g3(q[0]), c_re, b_im, ALU.mult)
                link(tt(g3(q[1]), c_im, b_re, ALU.mult))
                link(tt(sbb[:, 1, :, :], g3(q[0]), g3(q[1]), ALU.add))
                rc, rs = s5rot[:, 0, :], s5rot[:, 1, :]
                wk = [w_(12 + i) for i in range(4)]
                product(rc, rs, w_(6), w_(4), w_(6), w_(4), wk)
                product(rc, rs, rc, rs, rc, rs, wk)
                product(rc, rs, rc, rs, rc, rs, wk)
                tt(w_(12), rc, rc, ALU.mult)
                link(tt(w_(13), rs, rs, ALU.mult))
                link(tt(w_(12), w_(12), w_(13), ALU.add))
                link(ts(w_(12), w_(12), -0.5, 1.5, ALU.mult, ALU.add))
                tt(rc, rc, w_(12), ALU.mult)
                link(tt(rs, rs, w_(12), ALU.mult))
                dve.memset(ar(9120, 2048)[0:S5_M, :], 0.0).then_inc(S("s5_zeros"), 1)

            def sCW_flat(i):
                return ar(4768 + 576 * i, 512)

            def s5_piece(p):
                pairs = slice(PIECE * p, PIECE * (p + 1))
                if p:
                    dve.wait_ge(S("s5_stored"), 48 * p)
                    dve.wait_ge(*is_filled(f"k1_{p - 1}"))
                def power(w, n, m):
                    a = spw[:, w, 0:n, pairs].rearrange("p k g -> p g k")
                    return a.unsqueeze(3).broadcast_to([P, PIECE, n, m])
                def channel(a, n):
                    return a.unsqueeze(2).broadcast_to([P, PIECE, n, S5_M])
                v = [st[i].rearrange("p (g k m) -> p g k m", g=PIECE, k=TAU + 1) for i in range(2)]
                c_re, c_im = channel(sbc[:, 2, pairs, :], TAU + 1), channel(sbc[:, 3, pairs, :], TAU + 1)
                p_re, p_im = power(0, TAU + 1, S5_M), power(1, TAU + 1, S5_M)
                tt(v[0], c_re, p_re, ALU.mult)
                link(tt(v[1], c_im, p_im, ALU.mult))
                link(tt(sCW[:, :, 0, :, :], v[0], v[1], ALU.subtract))
                tt(v[0], c_re, p_im, ALU.mult)
                link(tt(v[1], c_im, p_re, ALU.mult))
                dve.scalar_tensor_tensor(out=sCW[:, :, 1, :, :], in0=v[0], scalar=-1.0, in1=v[1], op0=ALU.mult, op1=ALU.subtract)\
                   .then_inc(S("s5_cw"), 1)
                dve.wait_ge(S("s5_cw"), p + 1)
                v = [st[i][:, 0:512].rearrange("p (g k m) -> p g k m", g=PIECE, k=TAU) for i in range(2)]
                b_re, b_im = channel(sbb[:, 0, pairs, :], TAU), channel(sbb[:, 1, pairs, :], TAU)
                p_re, p_im = power(0, TAU, S5_M), power(1, TAU, S5_M)
                tt(v[0], b_re, p_re, ALU.mult)
                link(tt(v[1], b_im, p_im, ALU.mult))
                link(tt(sW1T[:, 0, :, :, :], v[0], v[1], ALU.subtract))
                tt(v[0], b_re, p_im, ALU.mult)
                link(tt(v[1], b_im, p_re, ALU.mult))
                tt(sW1T[:, 1, :, :, :], v[0], v[1], ALU.add).then_inc(S("s5_w1t"), 1)
                dve.wait_ge(S("s5_w1t"), p + 1)

            for step in range(STEPS):
                for j in range(2):
                    name = f"f{step}_{j}"
                    dve.wait_ge(S("gated"), 2 * step + j + 1)
                    if step >= 2:
                        dve.wait_ge(S("ffn_steps"), step - 1)
                    dve.tensor_tensor(fh[step % 2][:, j, :], fg[j], bank(name)[:, T:2 * T], ALU.mult).then_inc(S("hidden"), 1)
                    dve.wait_ge(S("hidden"), 2 * step + j + 1)
                    dve.sem_inc(read(name), 1)
                if step == 0:
                    s5_angles()
                    s5_base()
                if 1 <= step and step - 1 < PIECES:
                    s5_piece(step - 1)
            for b in range(4):
                add_to_x(f"fo{b}", b)

            norm_of_x("norm_mix1", "mix1", permuted=True)
            dve.wait_ge(S("s5_stored"), 48 * PIECES)
            cos_, sin_ = rot[:, 0, :, :], rot[:, 1, :, :]
            dve.memset(cos_[:, :, 0:1], 1.0)
            link(dve.memset(sin_[:, :, 0:1], 0.0))
            e_re, e_im = ar(11264, 32), ar(11296, 32)
            link(dve.tensor_copy(ar(11264, 64), ar(ARENA - 128, 64)))
            n = 1
            while n < BLOCKS:
                bro = lambda v: v.rearrange("p (g o) -> p g o", o=1).broadcast_to([P, PAIRS, n])
                tmp = [ar(9216 + 512 * i, PAIRS * n).rearrange("p (g j) -> p g j", g=PAIRS) for i in range(4)]
                product(cos_[:, :, n:2 * n], sin_[:, :, n:2 * n], cos_[:, :, 0:n], sin_[:, :, 0:n], bro(e_re), bro(e_im), tmp)
                product(e_re, e_im, e_re, e_im, e_re, e_im, [ar(11328 + 32 * i, 32) for i in range(4)])
                n *= 2
            link(dve.tensor_copy(rho, s5rot[:, 2, :].rearrange("p (g o) -> p g o", o=1).broadcast_to([P, PAIRS, BLOCKS])))
            link(dve.memset(rho[:, :, 0:1], 0.0))
            for w in range(2):
                for half in range(2):
                    dve.wait_ge(*was_read(f"Z{w}{half}"))
            c1, s1 = cos_.rearrange("p g j -> p (g j)"), sin_.rearrange("p g j -> p (g j)")
            flat_x = Xs.rearrange("p w g j -> p w (g j)")
            tt(t2[:, 0, :], Z[:, 0, :], c1, ALU.mult)
            tt(t2[:, 1, :], Z[:, 1, :], c1, ALU.mult)
            tt(flat_x[:, 0, :], Z[:, 1, :], s1, ALU.mult)
            link(tt(flat_x[:, 1, :], Z[:, 0, :], s1, ALU.mult))
            tt(t2[:, 0, :], t2[:, 0, :], flat_x[:, 0, :], ALU.add)
            link(tt(t2[:, 1, :], t2[:, 1, :], flat_x[:, 1, :], ALU.subtract))
            r1 = rho.rearrange("p g j -> p (g j)")
            dve.tensor_tensor_scan(Z[:, 0, :], r1, t2[:, 0, :], 0.0, ALU.mult, ALU.add)
            link(dve.tensor_tensor_scan(Z[:, 1, :], r1, t2[:, 1, :], 0.0, ALU.mult, ALU.add))
            j3 = lambda a: a.rearrange("p (g j) -> p g j", j=BLOCKS)[:, :, 0:BLOCKS - 1]
            dve.memset(Xs[:, :, :, 0:1], 0.0)
            tt(t2[:, 0, :], Z[:, 0, :], c1, ALU.mult)
            link(tt(t2[:, 1, :], Z[:, 1, :], s1, ALU.mult))
            link(tt(Xs[:, 0, :, 1:BLOCKS], j3(t2[:, 0, :]), j3(t2[:, 1, :]), ALU.subtract))
            tt(t2[:, 0, :], Z[:, 0, :], s1, ALU.mult)
            link(tt(t2[:, 1, :], Z[:, 1, :], c1, ALU.mult))
            tt(Xs[:, 1, :, 1:BLOCKS], j3(t2[:, 0, :]), j3(t2[:, 1, :]), ALU.add).then_inc(S("states"), 1)
            dve.wait_ge(S("y_loaded"), 16)
            for n in range(KT):
                dve.scalar_tensor_tensor(out=yT[:, n, :], in0=uT[:, n, :], scalar=pc("s5_d", n), in1=yT[:, n, :],
                                         op0=ALU.mult, op1=ALU.add).then_inc(S("y_skipped"), 1)
            for c in range(4):
                dve.wait_ge(*was_read(f"gate{c}"))
                link(tt(sg[c % 2], sg[c % 2], bank(f"val{c}")[:, :], ALU.mult))
                v = x[:, 2 * c:2 * c + 2, :].rearrange("p n (j s) -> p n j s", s=TAU)
                dve.tensor_tensor(v, v, sg[c % 2].rearrange("p (n s j) -> p n j s", n=2, s=TAU), ALU.add).then_inc(S("x_written"), 1)
                x_written[0] += 1
                dve.wait_ge(S("x_written"), x_written[0])
                dve.sem_inc(read(f"val{c}"), 1)
            cross_attention(1)

            norm_of_x("norm_ffn1", "ffn1")
            dve.wait_ge(*is_filled("logits"))
            dve.tensor_copy(lgt, bank("logits")[:, 0:16].rearrange("p (c e) -> p c e", c=2)).then_inc(read("logits"), 1)
            dve.wait_ge(*was_read("logits"))
            wide = [P, 2, EXPERTS, EXPERTS]
            mine, other = lgt.unsqueeze(3).broadcast_to(wide), lgt.unsqueeze(2).broadcast_to(wide)
            number = con[:, CONST_COLS["slots"], 0:EXPERTS]
            sq8 = [P, EXPERTS, EXPERTS]
            link(tt(cmpA[:, 0], number.unsqueeze(2).broadcast_to(sq8), number.unsqueeze(1).broadcast_to(sq8), ALU.is_gt))
            link(tt(cmpB, other, mine, ALU.is_equal))
            link(tt(cmpB, cmpB, cmpA[:, 0:1].broadcast_to(wide), ALU.mult))
            link(tt(cmpA, other, mine, ALU.is_gt))
            link(tt(cmpA, cmpA, cmpB, ALU.add))
            link(dve.tensor_reduce(sel, cmpA, AX.X, ALU.add))
            dve.tensor_reduce(gm[:, 0:2], lgt, AX.X, ALU.max)
            dve.tensor_scalar(sel, sel, 1.5, None, ALU.is_lt).then_inc(S("selected"), 1)
            dve.wait_ge(S("selected"), 1)
            dve.tensor_tensor(lgt, lgt, gm[:, 0:2].unsqueeze(2).broadcast_to([P, 2, EXPERTS]), ALU.subtract).then_inc(S("logits_less_max"), 1)
            dve.wait_ge(S("gate_exp"), 1)
            link(tt(gw, gw, sel, ALU.mult))
            link(dve.tensor_reduce(gm[:, 0:2], gw, AX.X, ALU.add))
            link(dve.reciprocal(gm[:, 2:4], gm[:, 0:2]))
            link(dve.memset(PG, -FAR))
            tt(PG[:, :, 1, 0:EXPERTS], gw, gm[:, 2:4].unsqueeze(2).broadcast_to([P, 2, EXPERTS]), ALU.mult)
            dve.wait_ge(*is_filled("places"))
            dve.tensor_reduce(cnt[:, 8:9], bank("places")[:, 16:24], AX.X, ALU.max)
            link(dve.tensor_copy(PG[:, :, 0, 0:EXPERTS], bank("places")[:, 0:16].rearrange("p (c e) -> p c e", c=2)))
            dve.tensor_copy(flag[0:1, 0:1], cnt[0:1, 8:9]).then_inc(read("places"), 1)
            dve.wait_ge(*was_read("places"))
            dve.sem_inc(S("flag_ready"), 1)
            pl = PG[:, :, 0, 0:EXPERTS]
            link(ts(pl, pl, FAR, None, ALU.add))
            link(tt(pl, pl, sel, ALU.mult))
            link(ts(pl, pl, -FAR, None, ALU.add))
            slots = con[:, CONST_COLS["slots"], :]

            def take_slots(e, i):
                dve.tensor_copy(pick, PG[:, :, :, bass.ds(e, 1)].rearrange("p c w o -> p c (w o)")).then_inc(S("picked"), 1)
                dve.wait_ge(S("picked"), i + 1)
                for c in range(2):
                    dve.tensor_scalar(Gs[:, c, :], slots, pick[:, c, 0:1], None, ALU.is_equal)
                    last = dve.tensor_scalar(Gg[:, c, :], slots, pick[:, c, 0:1], pick[:, c, 1:2], ALU.is_equal, ALU.mult)
                last.then_inc(S("slots_ready"), 1)

            def expert(e, i, rnd):
                for step in range(STEPS):
                    dve.wait_ge(S("moe_gated"), i * STEPS + step + 1)
                    dve.wait_ge(S("hidden_turned"), (i + 1) * STEPS + step - 1)
                    dve.tensor_tensor(hid[step % 2], sil[step % 2], ps[step % 2][:, STEP:2 * STEP], ALU.mult).then_inc(S("moe_hidden"), 1)
                dve.wait_ge(S("gates_turned"), i + 1)
                dve.wait_ge(S("slots_ready"), i + 1 + rnd)
                take_slots(e + 1, i + 1 + 2 * rnd)
                for m in range(4):
                    dve.wait_ge(S("scattered"), i * 4 + m + 1)
                    v = flat(x[:, 2 * m:2 * m + 2, :])
                    dve.wait_ge(S("moe_added"), i * 4 + m + 4)
                    dve.tensor_tensor(v, v, ps[6 + m % 2][:, :], ALU.add).then_inc(S("moe_added"), 1)

            take_slots(0, 0)
            with dve.Fori(0, EXPERTS) as e:
                expert(e, e, 0)
            busiest = dve.value_load(flag[0:1, 0:1], min_val=0, max_val=T)
            with dve.If(busiest > P):
                dve.wait_ge(S("slots_ready"), EXPERTS + 1)
                dve.tensor_scalar(pl, pl, -float(P), None, ALU.add).then_inc(S("picked"), 1)
                dve.wait_ge(S("picked"), EXPERTS + 2)
                take_slots(0, EXPERTS + 2)
                with dve.Fori(0, EXPERTS) as e:
                    expert(e, e + EXPERTS, 1)
                dve.wait_ge(S("moe_added"), 8 * EXPERTS + 4)
            dve.wait_ge(S("moe_added"), 4 * EXPERTS + 4)
            dve.sem_inc(S("x_written"), 4)
            norm_of_x("norm_fin", "fin")
            dve.wait_ge(S("norm_scaled"), norms[0])
            dve.sem_inc(S("final_ready"), KT)


def channel_major(a):
    return np.ascontiguousarray(a.T.reshape(-1, P, a.shape[0]).transpose(1, 0, 2))


def column_chunks(w, width=512):
    k, n = w.shape
    return w.reshape(k // P, P, n // width, width).transpose(2, 1, 0, 3).reshape(n // width, P, k // P * width)


def step_chunks(w13, w2):
    w13 = w13.reshape(KT, P, 2, STEPS, STEP).transpose(3, 1, 0, 2, 4).reshape(STEPS, P, DENSE)
    w2 = w2.reshape(STEPS, 2, P, D).transpose(0, 2, 1, 3).reshape(STEPS, P, SLOT - DENSE)
    return np.concatenate([w13, w2], 2)


def param_table(a):
    out = np.zeros((P, N_PARAM), np.float32)

    def put(name, v, rows=P):
        c0, w = PARAM_COLS[name]
        out[0:rows, c0:c0 + w] = np.asarray(v).reshape(w, rows).T

    for i in range(2):
        put(f"mix{i}", a["mix_norm_g"][i])
        put(f"xat{i}", a["xattn_norm_g"][i])
        put(f"ffn{i}", a["ffn_norm_g"][i])
    put("memg", a["mem_norm_g"])
    put("fin", a["final_norm_g"])
    put("s5_d", a["s5_d"][0])
    mu = a["rw_mu"][0]
    for i, name in enumerate(("mu_r", "mu_k", "mu_v")):
        put(name, mu[512 * i:512 * (i + 1)])
    put("mu_wd", mu[1536:1568], 32)
    put("mu_ad", mu[1568:1600], 32)
    put("mu_gd", mu[1600:1696], 96)
    for name in ("w0", "a0", "k_k", "k_a", "gn_g", "gn_b", "r_k"):
        put(name, a["rw_" + name][0].reshape(-1))
    put("onorm", a["hg_onorm_g"][0])
    put("lb", a["hg_lb_logits"][0])
    return out


def host_arrays(a):
    a = {k: np.asarray(v) for k, v in a.items()}
    w_in = a["ab_w_in"][0]
    hgrn, rwkv = w_in[:, :2048], w_in[:, 2048:]
    kv0 = a["xa_wkv"][0]
    glu = a["c_w_glu"][0]
    glu = np.concatenate([glu[:, :D].reshape(D, 4, 256), glu[:, D:].reshape(D, 4, 256)], 2).reshape(D, 2 * D)
    kv1 = a["xa_wkv"][1]
    dense = [rwkv[:, :1536], hgrn, kv0, a["ab_w_out"][0], a["xa_wq"][0], a["xa_wo"][0], a["c_w_in"][0], kv1, glu,
             a["xa_wq"][1], a["xa_wo"][1]]
    dense = [column_chunks(w) for w in dense]
    s5 = lambda name: a["s5_" + name][0].reshape((PAIRS, P) + a["s5_" + name][0].shape[2:])
    s5a = np.stack([s5("a_re").T, s5("a_im").T, np.repeat(a["s5_log_dt"][0].reshape(PAIRS, 2), S5_P, 1).T], 1)
    c_by_state = lambda name: a["s5_" + name][0].transpose(0, 2, 1).reshape(PAIRS, P, S5_M)
    s5bc = np.stack([v.transpose(1, 0, 2) for v in (s5("b_re"), s5("b_im"), c_by_state("c_re"), c_by_state("c_im"))], 1)
    small = np.zeros((P, 3, 512), np.float32)
    small[:32, 0], small[:32, 1], small[:96, 2] = a["rw_w2"][0], a["rw_a2"][0], a["rw_g2"][0]
    return {
        "x": channel_major(a["x"][0]), "mem": channel_major(a["mem"][0]), "con": shape_constants(), "par": param_table(a),
        "lora": column_chunks(rwkv[:, 1536:], 160)[0], "dense": np.concatenate(dense), "smallw": small.reshape(P, -1),
        "ffn": step_chunks(a["ffn_w13"][0], a["ffn_w2"][0]),
        "moe": np.stack([step_chunks(w13, w2) for w13, w2 in zip(a["moe_w13"][0], a["moe_w2"][0])]),
        "s5a": s5a.reshape(P, -1), "s5bc": s5bc.reshape(P, -1),
        "router": a["moe_router"][0].reshape(KT, P, EXPERTS).transpose(1, 0, 2).reshape(P, -1),
    }


def kernel(**inputs):
    import concourse.bacc as bacc
    from concourse.bass_utils import run_bass_kernel_spmd

    nc = bacc.Bacc("TRN2", target_bir_lowering=False, num_devices=1)
    arrays = {name: np.ascontiguousarray(v) for name, v in host_arrays(inputs).items()}
    aps = {name: nc.dram_tensor(name + "_dram", v.shape, mybir.dt.from_np(v.dtype), kind="ExternalInput").ap()
           for name, v in arrays.items()}
    out = nc.dram_tensor("out_dram", (P, KT, T), F32, kind="ExternalOutput").ap()
    build_trunk(nc, aps, out)
    r = run_bass_kernel_spmd(nc, [{name + "_dram": v for name, v in arrays.items()}], core_ids=[0])
    y = r.results[0]["out_dram"]
    return np.ascontiguousarray(y.transpose(2, 1, 0).reshape(1, T, D))
```

```python
from contextlib import ExitStack

import numpy as np

import concourse.bass as bass
from concourse import mybir

F32 = mybir.dt.float32
ALU = mybir.AluOpType
ACT = mybir.ActivationFunctionType
AX = mybir.AxisListType

P = 128
T = 256
D = 1024
KT = D // P
C = 128
LEVELS = 7
RW_N = 64
EPS = 1e-6
GN_EPS = 64e-5
RING = 4
SLOT = 6144
DENSE = 4096
D_FF = 2816
STEP = 256
STEPS = D_FF // STEP
EXPERTS = 8
TAU = 8
BLOCKS = T // TAU
S5_M = 16
S5_P = 64
PAIRS = 32
PIECE = 4
PIECES = PAIRS // PIECE
GRANULE = 2048
GRANULES = [g for n in range(STEPS + 2) for g in ([(n, 0), (n, 1)] if n < STEPS else []) + ([(n - 2, 2)] if n >= 2 else [])]
N_GRANULES = len(GRANULES)
FFN_GRANULE = GRANULE // 2
FFN_GRANULES = [g for n in range(STEPS + 1) for g in ([(n, p) for p in range(4)] if n < STEPS else []) +
                ([(n - 1, 4), (n - 1, 5)] if n else [])]
XA_HEADS = 4
TWO_PI = 6.283185307179586
TWO_PI_HI = 6.28125
PI_BELOW = 3.1415925
ROUNDER = 12582912.0
FAR = 1048576.0
XA_SCALE = float(D // XA_HEADS) ** -0.5

ARENA = 13568

PARAM_COLS = {}
_n = 0
for _name, _w in (("mix0", 8), ("mix1", 8), ("xat0", 8), ("xat1", 8), ("ffn0", 8), ("ffn1", 8), ("memg", 8),
                  ("fin", 8), ("s5_d", 8), ("mu_r", 4), ("mu_k", 4), ("mu_v", 4), ("mu_wd", 1), ("mu_ad", 1),
                  ("mu_gd", 1), ("w0", 4), ("a0", 4), ("k_k", 4), ("k_a", 4), ("r_k", 4), ("gn_g", 4),
                  ("gn_b", 4), ("onorm", 1), ("lb", 4)):
    PARAM_COLS[_name] = (_n, _w)
    _n += _w
N_PARAM = _n
MU0, MU1 = PARAM_COLS["mu_r"][0], PARAM_COLS["mu_gd"][0] + 1

CONST_COLS = {"ident": 0, "lev": 1, "incl0": 8, "strict": 9, "incl1": 10, "head_ones": 11, "ones": 12,
              "slots": 14}
N_CONST = 15


def shape_constants():
    s = np.arange(P)[:, None]
    t = np.arange(P)[None, :]
    out = np.zeros((N_CONST, P, P), np.float32)
    out[0] = s == t
    for i in range(LEVELS):
        h = 1 << i
        out[1 + i] = (s // (2 * h) == t // (2 * h)) & (s % (2 * h) < h) & (t % (2 * h) >= h)
    out[8] = out[10] = s <= t
    out[9] = s < t
    out[11] = s // RW_N == t // RW_N
    out[12] = out[13] = 1.0
    out[14] = t
    return np.ascontiguousarray(out.transpose(1, 0, 2).reshape(P, N_CONST * P))


def build_trunk(nc, A, out):
    ctx = ExitStack()
    with ctx:
        def sb(name, shape):
            return ctx.enter_context(nc.sbuf_tensor(name, shape, F32))

        def sb_two_lives(name, shape, pieces=1):
            with ExitStack() as second_life:
                piece = [shape[0]] + [shape[1] // pieces] + shape[2:]
                rounded = [second_life.enter_context(nc.sbuf_tensor(f"{name}_rounded{i}", piece, mybir.dt.float32r))
                           for i in range(pieces)]
            return sb(name, shape), (rounded if pieces > 1 else rounded[0])

        sems = {}

        def S(name):
            if name not in sems:
                sems[name] = ctx.enter_context(nc.semaphore(name))
            return sems[name]

        x = sb("x", [P, KT, T])
        h, h_rounded = sb_two_lives("h", [P, KT, T])
        sq, sq_rounded = sb_two_lives("sq", [P, KT, T])
        memn, memn_rounded = sb_two_lives("memn", [P, KT, T])
        kT, kT_rounded = sb_two_lives("kT", [P, KT, T])
        vN, vN_rounded = sb_two_lives("vN", [P, 2, D])
        con = sb("con", [P, N_CONST, P])
        par = sb("par", [P, N_PARAM])
        omu = sb("omu", [P, MU1 - MU0])
        lbs = sb("lbs", [P, 4, 4])
        rstd = sb("rstd", [P, T])
        nrm = sb("nrm", [P, T])
        small = sb("small", [P, 16])
        ring, ring_rounded = sb_two_lives("ring", [P, RING, SLOT], RING)
        arena, arena_rounded = sb_two_lives("arena", [P, ARENA])
        ps = [ctx.enter_context(nc.psum_tensor(f"ps{i}", [P, 512], F32)) for i in range(8)]

        def pc(name, i=0, rows=P, n=1):
            c0 = PARAM_COLS[name][0] + i
            return par[0:rows, c0:c0 + n]

        def om(name, i=0, rows=P):
            c0 = PARAM_COLS[name][0] + i - MU0
            return omu[0:rows, c0:c0 + 1]

        def cc(name, n=1):
            c0 = CONST_COLS[name]
            return con[:, c0:c0 + n, :]

        ident = con[:, 0, :]
        head_ones = con[:, CONST_COLS["head_ones"], :]
        ones = con[:, CONST_COLS["ones"], :]
        ring_flat = ring[:, :, :].rearrange("p s w -> p (s w)")

        def ar(at, words):
            assert at + words <= ARENA
            return arena[:, at:at + words]

        def rounded_ar(at, words):
            return arena_rounded[:, at:at + words]

        def spare(at, words):
            assert at + words <= 2 * SLOT
            return ring_flat[:, 2 * SLOT + at:2 * SLOT + at + words]

        def tiles4(a):
            return a.rearrange("p (n t) -> p n t", t=T)

        def flat(a):
            return a.rearrange("p n t -> p (n t)")

        def stack(a, n=8):
            return a.rearrange("p (n t) -> p n t", n=n)

        hq, hL, hk, hg = (tiles4(ar(1024 * i, 1024)) for i in range(4))
        hi = ar(4096, 1024).rearrange("p (c v) -> p c v", c=2)
        rr, rk, rv, rg = (tiles4(ar(5120 + 1024 * i, 1024)) for i in range(4))
        lw, la, lg = (ar(9216 + 256 * i, 256) for i in range(3))
        vn = ar(9984, 1024).rearrange("p (c v) -> p c v", c=2)
        F = [ar(11008 + 1024 * i, 1024) for i in range(2)]
        M0 = ar(13056, 512).rearrange("p (n two v) -> p n two v", n=4, two=2)
        smallw = spare(0, 1536).rearrange("p (m n) -> p m n", m=3)
        ld, cL, ra, kk = (tiles4(spare(1536 + 1024 * i, 1024)) for i in range(4))
        AR = spare(5632, 2048).rearrange("p (n c two t) -> p n c two t", n=4, c=2, two=2)
        bt = tiles4(spare(7680, 1024))
        kt = tiles4(spare(8704, 1024))
        att = [spare(9728 + 512 * i, 512) for i in range(2)]
        R = stack(spare(10752, 512))
        U = stack(spare(11264, 512))
        bonus = tiles4(flat(sq[:, 0:4, :]))
        tA = tiles4(spare(9728, 1024))
        tB = tiles4(spare(10752, 1024))
        tC = tiles4(flat(sq[:, 4:8, :]))
        SC = spare(2560, 3072).rearrange("p (h m t) -> p h m t", h=8, m=3)
        Am = stack(spare(1536, 1024))
        X = stack(ar(5120, 1024))
        Y = stack(ar(6144, 1024))
        V = stack(spare(0, 1024))
        bkn = flat(sq[:, 4:8, :]).rearrange("p (two v) -> p two v", two=2)
        ro = tiles4(ar(7168, 1024))
        ho = hq

        qT = ar(0, 2048).rearrange("p (n t) -> p n t", t=T)
        prob = ar(2048, 2048).rearrange("p (h s m) -> p h s m", h=4, s=2)
        pT = ar(4096, 2048).rearrange("p (h m t) -> p h m t", h=4, m=2)
        smax = small[:, 0:8]
        ssum = small[:, 8:16]
        fg = [nrm[:, :], rstd[:, :]]
        fh_high, fh_low = ([sq_rounded[:, 4 * part + 2 * i:4 * part + 2 * i + 2, :] for i in range(2)] for part in range(2))
        h_high = rounded_ar(11168, 2048).rearrange("p (n t) -> p n t", t=T)
        dense_high = [rounded_ar(6144 + FFN_GRANULE * i, FFN_GRANULE).rearrange("p (k n) -> p k n", k=KT) for i in range(4)]
        ffn_high = [flat(v[:, 4 * i:4 * i + 4, :]) for v in (kT_rounded, vN_rounded.rearrange("p c (n t) -> p (c n) t", t=T))
                    for i in range(2)]
        sa = ar(0, 96).rearrange("p (w g) -> p w g", w=3)
        sw = ar(96, 1024).rearrange("p (w g) -> p w g", g=PAIRS)
        sbc = ar(1120, 2048).rearrange("p (w g m) -> p w g m", w=4, g=PAIRS)
        sbb = ar(3168, 1024).rearrange("p (w g m) -> p w g m", w=2, g=PAIRS)
        spw = ar(4192, 576).rearrange("p (w k g) -> p w k g", w=2, k=TAU + 1)
        sCW = ar(4768, 1152).rearrange("p (g w k m) -> p g w k m", g=PIECE, w=2, k=TAU + 1)
        sW1T = ar(5920, 1024).rearrange("p (w g k m) -> p w g k m", w=2, g=PIECE, k=TAU)
        st = [ar(6944 + 576 * i, 576) for i in range(2)]
        sW1 = ar(8096, 1024).rearrange("p (g w c) -> p g w c", g=PIECE, w=2)
        sK = ar(9120, 2048).rearrange("p (g k m) -> p g k m", g=2 * PIECE, k=2 * TAU)[0:S5_M, :, :, :]
        s5rot = ar(ARENA - 128, 96).rearrange("p (w g) -> p w g", w=3)
        uT = ar(0, 2048).rearrange("p (n t) -> p n t", t=T)
        Ub = ar(2048, 2048).rearrange("p (g j) -> p g j", j=BLOCKS)
        Z = ar(4096, 2048).rearrange("p (w g) -> p w g", w=2)
        rot = ar(6144, 2048).rearrange("p (w g j) -> p w g j", w=2, g=PAIRS)
        rho = ar(8192, 1024).rearrange("p (g j) -> p g j", g=PAIRS)
        t2 = ar(9216, 2048).rearrange("p (w g) -> p w g", w=2)
        Xs = [v[:, :, :].rearrange("p n t -> p (n t)").rearrange("p (g two j) -> p g two j", g=PAIRS, two=2) for v in (sq, h)]
        Yb = ar(9216, 2048).rearrange("p (g j) -> p g j", j=BLOCKS)
        yT = ar(4096, 2048).rearrange("p (n t) -> p n t", t=T)
        sg = [ar(2048 + 512 * i, 512) for i in range(2)]
        hN = ar(0, 2048).rearrange("p (c d) -> p c d", c=2)
        Gs = ar(2048, 256).rearrange("p (c s) -> p c s", c=2)
        Gg = ar(2304, 256).rearrange("p (c s) -> p c s", c=2)
        GT = ar(2560, 256)
        hc = rounded_ar(2816, 1024).rearrange("p (k c) -> p k c", k=KT)
        sil = [ar(3840 + 256 * i, 256) for i in range(2)]
        hid = [ar(4352 + 256 * i, 256) for i in range(2)]
        hidT = [rounded_ar(4864 + 256 * i, 256).rearrange("p (j c) -> p j c", j=2) for i in range(2)]
        yc = ar(5376, 1024)
        spent = flat(memn_rounded[:, :, :])
        hc_low = spent[:, 0:1024].rearrange("p (k c) -> p k c", k=KT)
        hidT_low = [spent[:, 1024 + 256 * i:1280 + 256 * i].rearrange("p (j c) -> p j c", j=2) for i in range(2)]
        high = ([rounded_ar(6880 + GRANULE * i, GRANULE) for i in range(3)]
                + [flat(v[:, :, :]) for v in (kT_rounded, vN_rounded, sq_rounded)])
        router_flat = sb("router", [P, KT * EXPERTS])
        router = router_flat[:, :].rearrange("p (k e) -> p k e", k=KT)
        lgt = ar(6464, 16).rearrange("p (c e) -> p c e", c=2)
        cmpA = ar(6480, 128).rearrange("p (c e f) -> p c e f", c=2, e=EXPERTS)
        cmpB = ar(6608, 128).rearrange("p (c e f) -> p c e f", c=2, e=EXPERTS)
        sel = ar(6736, 16).rearrange("p (c e) -> p c e", c=2)
        gw = ar(6752, 16).rearrange("p (c e) -> p c e", c=2)
        gm = ar(6768, 4)
        PG = ar(6776, 40).rearrange("p (c w e) -> p c w e", c=2, w=2)
        pick = ar(6816, 4).rearrange("p (c w) -> p c w", c=2)
        cnt = ar(6820, 9)
        flag = ctx.enter_context(nc.sbuf_tensor("flag", [1, 1], mybir.dt.int32))
        dW1 = nc.dram_tensor("s5_w1", [2, P, 4096], F32, kind="Internal").ap()
        dW2 = nc.dram_tensor("s5_w2", [2, P, 4096], F32, kind="Internal").ap()
        dK = nc.dram_tensor("s5_k", [S5_M, 2 * PAIRS, 2 * TAU * S5_M], F32, kind="Internal").ap()
        dU = nc.dram_tensor("s5_u", [D, T], F32, kind="Internal").ap()
        dY = nc.dram_tensor("s5_y", [D, T], F32, kind="Internal").ap()

        bank_count = [[0, 0] for _ in range(8)]
        uses = {}

        def use_bank(name, bank, reads=1, fills=1):
            fills_before, before = bank_count[bank]
            uses[name] = (bank, fills_before + fills, before, before + reads)
            bank_count[bank] = [fills_before + fills, before + reads]

        def bank(name):
            return ps[uses[name][0]]

        def wait_bank_free(pe, name):
            b, _, before, _ = uses[name]
            if before:
                pe.wait_ge(S(f"bank{b}_read"), before)

        def filled(name):
            return S(f"bank{uses[name][0]}_filled")

        def is_filled(name):
            return S(f"bank{uses[name][0]}_filled"), uses[name][1]

        def read(name):
            return S(f"bank{uses[name][0]}_read")

        def was_read(name):
            return S(f"bank{uses[name][0]}_read"), uses[name][3]

        use_bank("norm_mix0", 6)
        use_bank("norm_mem", 7)
        use_bank("wd_ad", 0, 2)
        use_bank("gd", 1)
        turn = [2]

        def next_bank(name):
            use_bank(name, turn[0] % 6)
            turn[0] += 1

        for name in ("r", "k", "z", "a", "rg", "v", "kk", "q", "f", "i", "g", "bonus", "vn", "kv_0"):
            for half in range(2):
                next_bank(f"{name}{half}")
        order = []
        levels = [("level", i) for i in range(LEVELS + 2)]
        for c in range(2):
            order.append(("scores", c))
            for l in range(LEVELS):
                order.append(("invert", c, l))
                if levels:
                    order.append(levels.pop(0))
                if l == 3 and c == 0:
                    order.append(("kv", 1))
            order.append(("solve", c))
        assert not levels
        for step in order:
            if step[0] == "scores":
                for head in range(8):
                    use_bank(f"sc{step[1]}_{head}", head % 4)
                if step[1] == 0:
                    for m in range(2):
                        use_bank(f"bkn{m}", 4 + m)
            elif step[0] == "invert":
                c, l = step[1:]
                for g in range(2):
                    use_bank(f"V{c}_{l}_{g}", g)
                for g in range(2):
                    if l < LEVELS - 1:
                        use_bank(f"dX{c}_{l}_{g}", 2)
                    use_bank(f"dY{c}_{l}_{g}", 3)
            elif step[0] == "level":
                for b in range(2 if step[1] <= LEVELS else 1):
                    use_bank(f"att{step[1]}_{b}", 4 + b)
                if step[1] == LEVELS + 1:
                    for b in range(2):
                        use_bank(f"ho{b}", 6 + b)
            elif step[0] == "kv":
                for half in range(2):
                    use_bank(f"kv_{step[1]}{half}", 4 + half)
            elif step[0] == "solve":
                c = step[1]
                use_bank(f"R{c}", 0)
                use_bank(f"U{c}", 1)
                if c == 0:
                    use_bank("M0", 2)
                use_bank(f"ro{c}", 3)
        for b in range(2):
            use_bank(f"mean{b}", b)
        for b in range(2):
            use_bank(f"hsum{b}", 4 + b)
        use_bank("kv_20", 6)
        for b in range(2):
            use_bank(f"var{b}", b)
        use_bank("kv_21", 7)
        for half in range(2):
            use_bank(f"kv_3{half}", 4 + half)

        def xattn_uses(l):
            use_bank(f"norm_xat{l}", 7)
            for c in range(2):
                for half in range(2):
                    use_bank(f"q{l}_{c}{half}", 2 * c + half)
            for head in range(4):
                use_bank(f"s{l}_{head}", 4 + head % 2)
            for head in range(4):
                use_bank(f"pt{l}_{head}", head)
                use_bank(f"pv{l}_{head}", 6 + head % 2)
            for c in range(2):
                for half in range(2):
                    use_bank(f"xo{l}_{c}{half}", 2 * c + half)

        for c in range(2):
            for half in range(2):
                use_bank(f"out_{c}{half}", 2 + 2 * c + half)
        xattn_uses(0)
        use_bank("norm_ffn0", 7)
        for step in range(STEPS):
            for j in range(2):
                use_bank(f"f{step}_{j}", (2 * step + j) % 3, fills=0)
        for piece in range(PIECES):
            for what in ("re", "im", "k0", "k1"):
                use_bank(f"{what}_{piece}", 3)
        for b in range(4):
            use_bank(f"fo{b}", 4 + b)
        use_bank("norm_mix1", 0)
        for c in range(2):
            for half in range(2):
                use_bank(f"u_{c}{half}", 1 + 2 * c + half)
        for c in range(2):
            for half in range(2):
                use_bank(f"kv1_{c}{half}", (5 + 2 * c + half) % 4)
        for w_ in range(2):
            for half in range(2):
                use_bank(f"Z{w_}{half}", 4 + 2 * w_ + half)
        for quarter in range(4):
            use_bank(f"Y{quarter}", quarter)
        for c in range(2, 4):
            for half in range(2):
                use_bank(f"kv1_{c}{half}", 2 * c + half - 4)
        for c in range(4):
            use_bank(f"val{c}", 4 + (2 * c) % 4)
            use_bank(f"gate{c}", 4 + (2 * c + 1) % 4)
        xattn_uses(1)
        use_bank("norm_ffn1", 0)
        use_bank("logits", 1)
        for m in range(4):
            use_bank(f"hN{m}", 2 + m)
        use_bank("places", 6)

        use_bank("norm_fin", 0)
        x_writes, squares_before = {}, {}
        for i, name in enumerate(("norm_xat0", "norm_ffn0", "norm_mix1", "norm_xat1", "norm_ffn1", "norm_fin")):
            x_writes[name] = 4 * i
            squares_before[name] = 8 + 4 * i

        stream = []
        slot_uses = [0] * RING
        in_slot = [None, None, ("yb_ready", 1), ("yb_ready", 1)]
        place = {}

        def chunk(name, slot, src, last_bank=None, freed=None):
            stream.append((name, slot, src, in_slot[slot]))
            place[name] = (slot, slot_uses[slot])
            slot_uses[slot] += 1
            in_slot[slot] = freed or ("bank", last_bank)

        first = [("w_lora", "gd"), ("w_r", "r1"), ("w_k", "k1"), ("w_v", "v1"), ("w_q", "q1"), ("w_f", "f1"),
                 ("w_i", "i1"), ("w_g", "g1"), ("kv0_0", "kv_01"), ("kv0_1", "kv_11"), ("kv0_2", "kv_21"),
                 ("kv0_3", "kv_31"), ("wout0", "out_01"), ("wout1", "out_11"), ("wq0_0", "q0_01"),
                 ("wq0_1", "q0_11"), ("wo0_0", "xo0_01"), ("wo0_1", "xo0_11")]
        for n, (name, last) in enumerate(first):
            chunk(name, n % (2 if n < 14 else 4), A["dense"][n - 1] if n else A["lora"], last)
        turn_slot = len(first)
        n_dense = len(first) - 1
        for i in range(STEPS):
            chunk(f"ffn{i}", turn_slot % RING, A["ffn"][i], freed=("ffn_used", FFN_GRANULES.index((i, 5)) + 1) if i < STEPS - 1 else ("bank", "fo3"))
            turn_slot += 1
        second = [("cw0", "u_01"), ("cw1", "u_11"), ("kv1_0", "kv1_01"), ("kv1_1", "kv1_11"), ("s5_W1_0", None),
                  ("s5_W1_1", None), ("s5_T_0", None), ("s5_T_1", None), ("s5_W2_0", None), ("s5_W2_1", None),
                  ("kv1_2", "kv1_21"), ("kv1_3", "kv1_31"), ("glu0", "gate0"), ("glu1", "gate1"), ("glu2", "gate2"),
                  ("glu3", "gate3"), ("wq1_0", "q1_01"), ("wq1_1", "q1_11"), ("wo1_0", "xo1_01"), ("wo1_1", "xo1_11")]
        turn_slot += -(turn_slot + len(second)) % RING
        for name, last in second:
            if name.startswith("s5_"):
                i = int(name[-1])
                src = {"W1": dW1[i], "T_": i, "W2": dW2[i]}[name[3:5]]
                freed = {"s5_W1_0": ("bank", "Z10"), "s5_W1_1": ("bank", "Z11"), "s5_T_0": ("T_used", 1), "s5_T_1": ("T_used", 2),
                         "s5_W2_0": ("bank", "Y1"), "s5_W2_1": ("bank", "kv1_21")}[name]
                chunk(name, turn_slot % RING, src, freed=freed)
            else:
                chunk(name, turn_slot % RING, A["dense"][n_dense], last)
                n_dense += 1
            turn_slot += 1
        first_use = list(slot_uses)
        per_expert = [len(range(i, STEPS, RING)) for i in range(RING)]

        def weights(name, words=DENSE):
            return ring[:, place[name][0], 0:words].rearrange("p (k n) -> p k n", k=KT)

        def arrived(name):
            slot, use = place[name]
            return S(f"slot{slot}_filled"), 16 * (use + 1)

        def freed_by(what):
            return is_filled(what[1]) if what[0] == "bank" else (S(what[0]), what[1])

        def ffn_granule(n):
            step, part = FFN_GRANULES[n]
            slot = place[f"ffn{step}"][0]
            cols = slice(FFN_GRANULE * part, FFN_GRANULE * (part + 1))
            return ffn_high[n % len(ffn_high)], ring[:, slot, cols], ring_rounded[slot][:, 0, cols]

        ffn_order, n_split = [], len(ffn_high)

        def split_until(last):
            count = max(0, min(last + len(ffn_high), len(FFN_GRANULES) - 1) + 1 - n_split)
            return [("split", n_split + i) for i in range(count)]

        for step in range(STEPS + 1):
            if step < STEPS:
                for j in range(2):
                    splits = split_until(FFN_GRANULES.index((step, 2 * j + 1)))
                    n_split += len(splits)
                    ffn_order += [("hidden", step, j)] + splits[:1] + [("split_hidden", step, j)] + splits[1:]
            if step:
                splits = split_until(FFN_GRANULES.index((step - 1, 5)))
                n_split += len(splits)
                ffn_order += splits
            if step < STEPS:
                ffn_order.append(("tables", step))
        assert n_split == len(FFN_GRANULES)

        split_groups = [(["wq0_0", "wq0_1", "wo0_0", "wo0_1"], [f"{w}0_{c}{half}" for w in ("q", "xo") for c in range(2) for half in range(2)]),
                        ([f"glu{c}" for c in range(4)] + ["wq1_0", "wq1_1", "wo1_0", "wo1_1"],
                         [f"{w}{c}" for c in range(4) for w in ("val", "gate")] +
                         [f"{w}1_{c}{half}" for w in ("q", "xo") for c in range(2) for half in range(2)])]
        dense_granules, served = [], {}
        for chunks, banks in split_groups:
            first = len(dense_granules)
            for n in range(4 * len(chunks)):
                dense_granules.append((chunks[n // 4], n % 4, banks[n // 2 - 2] if n >= 4 else None))
            for n, name in enumerate(banks):
                served[name] = range(first + min(2 * n + 4, 4 * len(chunks)), first + min(2 * n + 6, 4 * len(chunks)))
        group_start = {"wq0_0": range(4), "glu0": range(16, 20)}

        def dense_granule(n):
            name, block_, _ = dense_granules[n]
            slot = place[name][0]
            at = lambda a: a.rearrange("p (k n) -> p k n", k=KT)[:, :, block_ * P:(block_ + 1) * P]
            return dense_high[n % 4], at(ring[:, slot, 0:DENSE]), at(ring_rounded[slot][:, 0, 0:DENSE])

        h_high_before = {"xat0": 0, "pv0": 4, "ffn0": 8, "glu": 12, "xat1": 20, "pv1": 24}
        h_low_before = {"xat0": 0, "ffn0": 4, "glu": 8, "xat1": 16}
        norms_before = {"xat0": 2, "ffn0": 3, "xat1": 5}

        def in_float32(a):
            return a.bitcast(F32)

        def split_ahead(n):
            done = lambda m: 6 if m < 0 else min(N_GRANULES, GRANULES.index((m, 1)) + 1 + len(high))
            return range(done(n - 1), done(n)) if n < STEPS else range(0)

        def granule(step, part):
            n = GRANULES.index((step, part))
            cols = slice(GRANULE * part, GRANULE * (part + 1))
            return n, high[n % len(high)], ring[:, step % RING, cols], ring_rounded[step % RING][:, 0, cols]

        block = ctx.enter_context(nc.Block())

        @block.sync
        def _(sp):
            sp.wait_ge(S("x_loaded"), 16)
            for name, slot, src, freed in stream:
                if freed:
                    sp.wait_ge(*freed_by(freed))
                if name.startswith("s5_"):
                    sp.wait_ge(S({"W1": "W1_stored", "T_": "K_stored", "W2": "W2_stored"}[name[3:5]]), 16 * PIECES)
                if name.startswith("s5_T"):
                    for kappa in range(TAU):
                        row, sigma = S5_M * kappa, TAU - 1 - kappa
                        sp.dma_start(ring[row:row + S5_M, slot, 0:DENSE].rearrange("p (g c) -> p g c", g=PAIRS),
                                     dK[:, PAIRS * src:PAIRS * (src + 1), (TAU - sigma) * S5_M:(2 * TAU - sigma) * S5_M])\
                          .then_inc(S("s5_T_filled"), 16)
                    sp.wait_ge(S("s5_T_filled"), 16 * TAU * (src + 1))
                    sp.sem_inc(S(f"slot{slot}_filled"), 16)
                    continue
                sp.dma_start(ring[:, slot, 0:src.shape[-1]], src).then_inc(S(f"slot{slot}_filled"), 16)

            def expert_weights(e, i):
                def load(step, sem, at, words, part):
                    slot = step % RING
                    if step < RING:
                        sp.wait_ge(S("granules_used"), i * N_GRANULES + GRANULES.index((max(range(slot, STEPS, RING)), part)) + 1)
                    else:
                        sp.wait_ge(S("granules_used"), (i + 1) * N_GRANULES + GRANULES.index((step - RING, part)) + 1)
                    sp.dma_start(ring[:, slot, at:at + words], A["moe"][bass.ds(e, 1), step, :, at:at + words].rearrange("o p w -> p (o w)"))\
                      .then_inc(S(f"{sem}{slot}_filled"), 16)

                for n in range(STEPS + 2):
                    if n < STEPS:
                        load(n, "slot", 0, DENSE, 1)
                    if n >= 2:
                        load(n - 2, "w2_", DENSE, SLOT - DENSE, 2)

            with sp.Fori(0, EXPERTS) as e:
                expert_weights(e, e)
            sp.wait_ge(S("flag_ready"), 1)
            busiest = sp.value_load(flag[0:1, 0:1], min_val=0, max_val=T)
            with sp.If(busiest > P):
                with sp.Fori(0, EXPERTS) as e:
                    expert_weights(e, e + EXPERTS)
            for b in range(4):
                sp.wait_ge(S("norm_scaled"), KT * 7 + 2 * b + 2)
                sp.dma_start(out[:, 2 * b:2 * b + 2, :], h[:, 2 * b:2 * b + 2, :]).then_inc(S("stored"), 16)
            sp.wait_ge(S("stored"), 64)

        @block.gpsimd
        def _(pool):
            pool.wait_ge(*is_filled("xo0_11"))
            pool.memset(ar(9120, 2048)[0:S5_M, :], 0.0).then_inc(S("s5_zeros"), 1)
            for p in range(PIECES):
                pool.wait_ge(S("s5_cw"), p + 1)
                cols = slice((p % 4) * 1024, (p % 4 + 1) * 1024)
                pool.dma_start(dW2[p // 4][:, cols].rearrange("p (g w c) -> p g w c", g=PIECE, w=2),
                               sCW[:, :, :, 1:TAU + 1, :].rearrange("p g w k m -> p g w (k m)")).then_inc(S("W2_stored"), 16)
                pool.wait_ge(*was_read(f"im_{p}"))
                pool.wait_ge(*was_read(f"k1_{p}"))
                pool.dma_start(dW1[p // 4][:, cols], ar(8096, 1024)).then_inc(S("W1_stored"), 16)
                pool.dma_start(dK[:, 8 * p:8 * p + 8, :], sK.rearrange("p g k m -> p g (k m)")).then_inc(S("K_stored"), 16)
            pool.wait_ge(*is_filled("norm_mix1"))
            pool.memset(sq[:, :, :], 0.0).then_inc(S("states_zero"), 1)
            pool.wait_ge(*is_filled("u_11"))
            pool.memset(h[:, :, :], 0.0).then_inc(S("states_zero"), 1)

        @block.scalar
        def _(act):
            act.dma_start(x[:, :, :], A["x"]).then_inc(S("x_loaded"), 16)
            act.dma_start(con[:, :, :].rearrange("p n c -> p (n c)"), A["con"]).then_inc(S("con_loaded"), 16)
            act.dma_start(par[:, :], A["par"]).then_inc(S("parityloaded"), 16)
            act.dma_start(memn[:, :, :], A["mem"]).then_inc(S("mem_loaded"), 16)
            act.dma_start(spare(0, 1536), A["smallw"]).then_inc(S("smallw_loaded"), 16)
            act.dma_start(router_flat[:, :], A["router"]).then_inc(S("router_loaded"), 16)

            linked = [0]

            def link(ins):
                linked[0] += 1
                ins.then_inc(S("act_link"), 1)
                act.wait_ge(S("act_link"), linked[0])

            def squares(src):
                for b in range(4):
                    act.activation(sq[:, 2 * b:2 * b + 2, :], src[:, 2 * b:2 * b + 2, :], ACT.Square).then_inc(S("squares"), 1)

            def root(name):
                act.wait_ge(*is_filled(name))
                act.activation(nrm[:, :], bank(name)[:, 0:T], ACT.Sqrt, bias=EPS, scale=1.0 / D).then_inc(read(name), 1)

            def copy_bank(name, dst):
                act.wait_ge(*is_filled(name))
                act.activation(dst, bank(name)[:, :], ACT.Copy).then_inc(read(name), 1)

            act.wait_ge(S("x_loaded"), 16)
            squares(x)
            root("norm_mix0")
            act.wait_ge(S("mem_loaded"), 16)
            squares(memn)
            act.wait_ge(S("norm_scaled"), 1)
            root("norm_mem")
            act.wait_ge(S("lb_shifted"), 1)
            act.activation(lbs[:, 1, :], lbs[:, 0, :], ACT.Exp).then_inc(S("lb_exp"), 1)

            act.wait_ge(S("omu_ready"), 1)
            act.wait_ge(*is_filled("wd_ad"))
            act.activation(lw[0:32, :], bank("wd_ad")[0:32, 0:T], ACT.Copy, scale=om("mu_wd", 0, 32)).then_inc(S("own_part"), 1)
            act.activation(la[0:32, :], bank("wd_ad")[0:32, T:2 * T], ACT.Copy, scale=om("mu_ad", 0, 32)).then_inc(S("own_part"), 1)
            act.wait_ge(*is_filled("gd"))
            act.activation(lg[0:96, :], bank("gd")[0:96, 0:T], ACT.Copy, scale=om("mu_gd", 0, 96)).then_inc(S("own_part"), 1)

            def own_part(name, dst):
                for half in range(2):
                    act.wait_ge(*is_filled(f"{name}{half}"))
                    for i in range(2):
                        act.activation(dst[:, 2 * half + i, :], bank(f"{name}{half}")[:, i * T:(i + 1) * T], ACT.Copy,
                                       scale=om("mu_" + name, 2 * half + i)).then_inc(S("own_part"), 1)

            own_part("r", rr)
            act.wait_ge(*was_read("wd_ad"))
            act.wait_ge(*was_read("gd"))
            act.activation(lw[0:32, :], lw[0:32, :], ACT.Tanh).then_inc(S("low_rank_in"), 1)
            act.activation(lg[0:96, :], lg[0:96, :], ACT.Sigmoid).then_inc(S("low_rank_in"), 1)
            own_part("k", rk)
            for name, bias, dst in (("z", "w0", ld), ("a", "a0", ra)):
                for half in range(2):
                    act.wait_ge(*is_filled(f"{name}{half}"))
                    for i in range(2):
                        last = act.activation(dst[:, 2 * half + i, :], bank(f"{name}{half}")[:, i * T:(i + 1) * T],
                                              ACT.Sigmoid, bias=pc(bias, 2 * half + i))
                    last.then_inc(read(f"{name}{half}"), 1)
            for half in range(2):
                copy_bank(f"rg{half}", flat(rg[:, 2 * half:2 * half + 2, :]))
            own_part("v", rv)
            act.wait_ge(*was_read("k1"))
            for n in range(4):
                last = act.activation(kk[:, n, :], rk[:, n, :], ACT.Copy, scale=pc("k_k", n))
            link(last)
            act.activation(tC, kk, ACT.Square).then_inc(S("kk_squared"), 1)
            act.wait_ge(*was_read("kk0"))
            act.wait_ge(*was_read("kk1"))
            act.activation(tC, tC, ACT.Sqrt).then_inc(S("kk_root"), 1)
            for half in range(2):
                act.wait_ge(*is_filled(f"q{half}"))
                act.activation(flat(hq[:, 2 * half:2 * half + 2, :]), bank(f"q{half}")[:, :], ACT.Sigmoid).then_inc(S("q_sigmoid"), 1)
            for half in range(2):
                act.wait_ge(*is_filled(f"f{half}"))
                act.activation(F[0][:, half * 512:(half + 1) * 512], bank(f"f{half}")[:, :], ACT.Abs)
                act.activation(flat(hk[:, 2 * half:2 * half + 2, :]), bank(f"f{half}")[:, :], ACT.Sigmoid, scale=-1.0).then_inc(S("f_sigmoid"), 1)
            for half in range(2):
                copy_bank(f"i{half}", hi[:, half, :])
            for half in range(2):
                act.wait_ge(*is_filled(f"g{half}"))
                act.activation(flat(hg[:, 2 * half:2 * half + 2, :]), bank(f"g{half}")[:, :], ACT.Sigmoid).then_inc(S("g_sigmoid"), 1)
            act.wait_ge(*was_read("f0"))
            act.wait_ge(*was_read("f1"))
            act.activation(F[0], F[0], ACT.Exp, scale=-1.0)
            link(act.activation(F[1], F[1], ACT.Exp))
            act.wait_ge(S("decays_in"), 1)
            act.activation(small[:, 0:4], small[:, 0:4], ACT.Exp)
            act.activation(tA, cL, ACT.Exp, scale=-1.0)
            act.activation(tB, ld, ACT.Exp).then_inc(S("decays_out"), 1)
            act.activation(cL, cL, ACT.Exp).then_inc(S("decays_out"), 1)
            act.activation(F[0], F[0], ACT.Ln, bias=1.0)
            act.wait_ge(S("lb_ready"), 1)
            for n in range(4):
                last = act.activation(F[1][:, n * T:(n + 1) * T], F[1][:, n * T:(n + 1) * T], ACT.Ln, bias=1.0, scale=lbs[:, 2, n:n + 1])
            last.then_inc(S("f_logs"), 1)
            for c in range(2):
                copy_bank(f"vn{c}", vn[:, c, :])
            for half in range(2):
                copy_bank(f"kv_0{half}", flat(kT[:, 2 * half:2 * half + 2, :]))
            def level(i):
                if i > LEVELS + 1:
                    return
                act.wait_ge(S("distances"), i)
                act.activation(F[i % 2], F[i % 2], ACT.Exp).then_inc(S("level_decays"), 1)

            for step in order:
                if step[0] == "scores":
                    c = step[1]
                    if c == 1:
                        act.wait_ge(*is_filled(f"V0_{LEVELS - 1}_1"))
                    for head in range(8):
                        act.wait_ge(*is_filled(f"sc{c}_{head}"))
                        act.activation(Am[:, head, :], bank(f"sc{c}_{head}")[:, 0:P], ACT.Copy).then_inc(S("A_copied"), 1)
                    if c == 0:
                        for m in range(2):
                            copy_bank(f"bkn{m}", bkn[:, m, :])
                elif step[0] == "level":
                    level(step[1] + 1)
                elif step[0] == "kv":
                    for half in range(2):
                        copy_bank(f"kv_1{half}", flat(kT[:, 4 + 2 * half:6 + 2 * half, :]))
                elif step[0] == "solve":
                    c = step[1]
                    copy_bank(f"R{c}", flat(R))
                    copy_bank(f"U{c}", flat(U))
                    act.wait_ge(*is_filled(f"ro{c}"))
                    act.activation(ro[:, :, c * C:(c + 1) * C], stack(bank(f"ro{c}")[:, :], 4), ACT.Copy).then_inc(read(f"ro{c}"), 1)
            for b in range(2):
                copy_bank(f"ho{b}", flat(ho[:, 2 * b:2 * b + 2, :]))
            act.wait_ge(*was_read("ho0"))
            act.wait_ge(*was_read("ho1"))
            act.activation(F[0], flat(ho), ACT.Square).then_inc(S("ho_squared"), 1)
            for b in range(2):
                act.wait_ge(*was_read(f"mean{b}"))
            act.activation(tA, ro, ACT.Square).then_inc(S("ro_squared"), 1)
            for b in range(2):
                act.wait_ge(*is_filled(f"hsum{b}"))
                act.activation(F[1][:, b * 512:(b + 1) * 512], bank(f"hsum{b}")[:, :], ACT.Sqrt, bias=EPS, scale=1.0 / P).then_inc(read(f"hsum{b}"), 1)
            copy_bank("kv_20", vN[:, 0, 0:512])
            for b in range(2):
                act.wait_ge(*is_filled(f"var{b}"))
                act.activation(flat(tB[:, 2 * b:2 * b + 2, :]), bank(f"var{b}")[:, :], ACT.Sqrt, bias=GN_EPS, scale=1.0 / RW_N).then_inc(read(f"var{b}"), 1)
            copy_bank("kv_21", vN[:, 1, 0:512])
            for half in range(2):
                copy_bank(f"kv_3{half}", vN[:, half, 512:1024])

            norms = [2]

            def norm_of_x(name):
                for b in range(4):
                    act.wait_ge(S("x_written"), x_writes[name] + b + 1)
                    act.activation(sq[:, 2 * b:2 * b + 2, :], x[:, 2 * b:2 * b + 2, :], ACT.Square).then_inc(S("squares"), 1)
                act.wait_ge(S("norm_scaled"), KT * (norms[0] - 1) + 1)
                norms[0] += 1
                root(name)

            def round_dense_weights(granules):
                for n in granules:
                    high_part, words, _ = dense_granule(n)
                    name, part, before = dense_granules[n]
                    if part == 0:
                        act.wait_ge(*arrived(name))
                    if before:
                        act.wait_ge(*is_filled(before))
                    act.activation(high_part, words, ACT.Copy).then_inc(S("dense_high"), 1)

            def round_normed(name):
                for b in range(4):
                    blocks = slice(2 * b, 2 * b + 2)
                    act.wait_ge(S("norm_scaled"), norms_before[name] * KT + 2 * b + 2)
                    act.activation(h_high[:, blocks, :], h[:, blocks, :], ACT.Copy).then_inc(S("h_high"), 1)

            def cross_attention(l):
                norm_of_x(f"norm_xat{l}")
                round_normed(f"xat{l}")
                for c in range(2):
                    for half in range(2):
                        name = f"q{l}_{c}{half}"
                        copy_bank(name, flat(qT[:, 4 * c + 2 * half:4 * c + 2 * half + 2, :]))
                        round_dense_weights(served[name])
                for head in range(4):
                    act.wait_ge(S("score_max"), 4 * l + head + 1)
                    for b in range(2):
                        last = act.activation(prob[:, head, b, :], bank(f"s{l}_{head}")[:, b * T:(b + 1) * T], ACT.Exp, scale=XA_SCALE,
                                              bias=smax[:, 2 * head + b:2 * head + b + 1], accum_out=ssum[:, 2 * head + b:2 * head + b + 1])
                    last.then_inc(read(f"s{l}_{head}"), 1)
                for head in range(4):
                    copy_bank(f"pt{l}_{head}", pT[:, head, :, :].rearrange("p m t -> p (m t)"))
                    act.wait_ge(*is_filled(f"pv{l}_{head}"))
                    act.activation(flat(h_high[:, 2 * head:2 * head + 2, :]), bank(f"pv{l}_{head}")[:, :], ACT.Copy).then_inc(S("h_high"), 1)
                for c in range(2):
                    for half in range(2):
                        round_dense_weights(served[f"xo{l}_{c}{half}"])

            def round_ffn_weights(n):
                high_part, words, _ = ffn_granule(n)
                step, part = FFN_GRANULES[n]
                if part == 0:
                    act.wait_ge(*arrived(f"ffn{step}"))
                if n >= len(ffn_high):
                    act.wait_ge(S("ffn_used"), n - len(ffn_high) + 1)
                act.activation(high_part, words, ACT.Copy).then_inc(S("ffn_high"), 1)

            act.wait_ge(S("yb_ready"), 1)
            round_dense_weights(group_start["wq0_0"])
            cross_attention(0)
            for n in range(len(ffn_high)):
                round_ffn_weights(n)
            norm_of_x("norm_ffn0")
            round_normed("ffn0")

            act.dma_start(ar(0, 96), A["s5a"]).then_inc(S("s5_a_loaded"), 16)
            act.dma_start(ar(1120, 2048), A["s5bc"]).then_inc(S("s5_bc_loaded"), 16)

            def s5_base():
                act.wait_ge(S("s5_a_loaded"), 16)
                act.activation(sw[:, 0, :], sa[:, 2, :], ACT.Exp).then_inc(S("s5_dt"), 1)
                act.wait_ge(S("s5_angles"), 1)
                act.activation(sw[:, 3, :], sw[:, 1, :], ACT.Exp)
                act.activation(s5rot[:, 2, :], sw[:, 1, :], ACT.Exp, scale=float(TAU))
                act.activation(sw[:, 4, :], sw[:, 5, :], ACT.Sin)
                act.activation(sw[:, 6, :], sw[:, 7, :], ACT.Sin).then_inc(S("s5_sines"), 1)

            def s5_piece(p):
                if p:
                    act.wait_ge(S("W1_stored"), 16 * p)
                for w, name in enumerate(("re", "im")):
                    act.wait_ge(*is_filled(f"{name}_{p}"))
                    act.activation(sW1[:, :, w, :], stack(bank(f"{name}_{p}")[:, :], PIECE), ACT.Copy).then_inc(read(f"{name}_{p}"), 1)
                if p == 0:
                    act.wait_ge(S("s5_zeros"), 1)
                else:
                    act.wait_ge(S("K_stored"), 16 * p)
                for parity in range(2):
                    name = f"k{parity}_{p}"
                    act.wait_ge(*is_filled(name))
                    act.activation(sK.rearrange("p (g two) k m -> p g two (k m)", two=2)[:, :, parity, P:2 * P],
                                   stack(bank(name)[0:S5_M, :], PIECE), ACT.Copy).then_inc(read(name), 1)

            for what, n, *rest in ffn_order:
                if what == "split":
                    round_ffn_weights(n)
                elif what == "hidden":
                    name, count = f"f{n}_{rest[0]}", 2 * n + rest[0]
                    act.wait_ge(S("ffn_used"), FFN_GRANULES.index((n, 2 * rest[0] + 1)) + 1)
                    if count >= 2:
                        act.wait_ge(S("hidden_low"), count - 1)
                    act.activation(fg[rest[0]], bank(name)[:, 0:T], ACT.Silu).then_inc(S("gated"), 1)
                elif what == "split_hidden":
                    act.wait_ge(S("hidden"), 2 * n + rest[0] + 1)
                    if n >= 2:
                        act.wait_ge(S("ffn_used"), FFN_GRANULES.index((n - 2, 5)) + 1)
                    act.activation(fh_high[n % 2][:, rest[0], :], fg[rest[0]], ACT.Copy).then_inc(S("hidden_high"), 1)
                elif n == 0:
                    s5_base()
                elif n >= 3:
                    s5_piece(n - 3)

            act.wait_ge(*is_filled("fo3"))
            norm_of_x("norm_mix1")
            for c in range(2):
                for half in range(2):
                    copy_bank(f"u_{c}{half}", flat(uT[:, 4 * c + 2 * half:4 * c + 2 * half + 2, :]))
            act.wait_ge(*was_read("u_11"))
            by_channel = lambda a: a.rearrange("(n p) t -> p n t", p=P)
            by_group = lambda a: a.rearrange("(g m) (s j) -> m g s j", m=S5_M, j=BLOCKS)
            act.dma_start(by_channel(dU), uT).then_inc(S("u_stored"), 16)
            act.wait_ge(S("u_stored"), 16)
            for kappa in range(TAU):
                act.dma_start(Ub[S5_M * kappa:S5_M * (kappa + 1), :, :], by_group(dU)[:, :, TAU - 1 - kappa, :]).then_inc(S("u_blocks"), 16)
            for c in range(2):
                for half in range(2):
                    copy_bank(f"kv1_{c}{half}", flat(kT[:, 4 * c + 2 * half:4 * c + 2 * half + 2, :]))
            for w in range(2):
                for half in range(2):
                    copy_bank(f"Z{w}{half}", Z[:, w, half * 512:(half + 1) * 512])
            act.wait_ge(S("states"), 1)
            for half in range(2):
                for quarter in (2 * half, 2 * half + 1):
                    copy_bank(f"Y{quarter}", Yb[:, 16 * quarter:16 * quarter + 16, :].rearrange("p g j -> p (g j)"))
                for quarter in (2 * half, 2 * half + 1):
                    act.wait_ge(*was_read(f"Y{quarter}"))
                groups = slice(PAIRS * half, PAIRS * half + PAIRS)
                for tau in range(TAU):
                    act.dma_start(by_group(dY)[:, groups, tau, :], Yb[S5_M * tau:S5_M * (tau + 1), groups, :]).then_inc(S(f"y_stored{half}"), 16)
            for half in range(2):
                blocks = slice(4 * half, 4 * half + 4)
                act.wait_ge(S(f"y_stored{half}"), 16 * TAU)
                act.dma_start(yT[:, blocks, :], by_channel(dY)[:, blocks, :]).then_inc(S(f"y_loaded{half}"), 16)
            round_dense_weights(group_start["glu0"])
            for half in range(2):
                copy_bank(f"kv1_2{half}", vN[:, half, 0:512])
            for n in range(KT):
                act.wait_ge(S("y_skipped"), n + 1)
                act.activation(h[:, n, :], yT[:, n, :], ACT.Gelu_apprx_tanh).then_inc(S("gelu"), 1)
                act.wait_ge(S("gelu"), n + 1)
                act.activation(h_high[:, n, :], h[:, n, :], ACT.Copy).then_inc(S("h_high"), 1)
            for half in range(2):
                copy_bank(f"kv1_3{half}", vN[:, half, 512:1024])
            for c in range(4):
                round_dense_weights(served[f"val{c}"])
                act.wait_ge(*is_filled(f"gate{c}"))
                if c >= 2:
                    act.wait_ge(S("x_written"), x_writes["norm_xat1"] + c - 1)
                act.activation(sg[c % 2], bank(f"gate{c}")[:, :], ACT.Sigmoid).then_inc(read(f"gate{c}"), 1)
                round_dense_weights(served[f"gate{c}"])
            cross_attention(1)

            def round_weights(i, n):
                step, part = GRANULES[n]
                _, high_part, words, _ = granule(step, part)
                slot = step % RING
                if part == 0:
                    act.wait_ge(S(f"slot{slot}_filled"), i * (16 * per_expert[slot]) + 16 * (first_use[slot] + step // RING + 1))
                if part == 2:
                    act.wait_ge(S(f"w2_{slot}_filled"), i * (16 * per_expert[slot]) + 16 * (step // RING + 1))
                if n >= len(high):
                    act.wait_ge(S("granules_used"), (i + 1) * N_GRANULES + n - len(high) + 1)
                else:
                    act.wait_ge(S("granules_used"), i * N_GRANULES + max(range(n, N_GRANULES, len(high))) + 1)
                act.activation(high_part, words, ACT.Copy).then_inc(S("weights_high"), 1)

            norm_of_x("norm_ffn1")
            for n in range(3):
                round_weights(0, n)
            act.wait_ge(S("logits_less_max"), 1)
            act.activation(gw, lgt, ACT.Exp).then_inc(S("gate_exp"), 1)
            for m in range(4):
                copy_bank(f"hN{m}", hN[:, m // 2, (m % 2) * 512:(m % 2 + 1) * 512])

            def round_rows(i):
                for b in range(2):
                    act.wait_ge(S("gathered"), 2 * i + b + 1)
                    act.activation(hc[:, 4 * b:4 * b + 4, :].rearrange("p k c -> p (k c)"), ps[6 + b][:, :], ACT.Copy)\
                       .then_inc(S("gather_copied"), 1)

            def copy_gates(i):
                act.wait_ge(S("gates_turned"), i + 1)
                act.activation(GT, ps[3][:, 0:T], ACT.Copy).then_inc(S("gates_copied"), 1)

            def begin(i):
                if i:
                    for n in range(3):
                        round_weights(i, n)
                round_rows(i)
                copy_gates(i)

            def expert(i, last=False):
                for n in range(3, 6):
                    round_weights(i, n)
                for n in range(STEPS + 1):
                    ahead = list(split_ahead(n))
                    if n < STEPS:
                        act.wait_ge(S("granules_used"), (i + 1) * N_GRANULES + GRANULES.index((n, 1)) + 1)
                        act.wait_ge(S("moe_hidden"), (i + 1) * STEPS + n - 1)
                        act.activation(sil[n % 2], ps[n % 2][:, 0:STEP], ACT.Silu).then_inc(S("moe_gated"), 1)
                    for q in ahead[:2]:
                        round_weights(i, q)
                    if n == STEPS and not last:
                        round_weights(i + 1, 0)
                    if n >= 1:
                        act.wait_ge(S("hidden_turned"), (i + 1) * STEPS + n)
                        if n >= 3:
                            act.wait_ge(S("granules_used"), (i + 1) * N_GRANULES + GRANULES.index((n - 3, 2)) + 1)
                        act.activation(hidT[(n - 1) % 2].rearrange("p j c -> p (j c)"), ps[2][:, 0:T], ACT.Copy)\
                           .then_inc(S("hidden_copied"), 1)
                    for q in ahead[2:]:
                        round_weights(i, q)
                if not last:
                    round_rows(i + 1)
                    round_weights(i + 1, 1)
                act.wait_ge(S("granules_used"), (i + 2) * N_GRANULES)
                for b in range(2):
                    act.activation(yc[:, b * 512:(b + 1) * 512], ps[4 + b][:, :], ACT.Copy).then_inc(S("y_copied"), 1)
                if not last:
                    round_weights(i + 1, 2)
                    copy_gates(i + 1)

            def experts(first):
                begin(first)
                with act.Fori(0, EXPERTS - 1) as e:
                    expert(e + first if first else e)
                expert(first + EXPERTS - 1, last=True)

            experts(0)
            act.wait_ge(S("flag_ready"), 1)
            busiest = act.value_load(flag[0:1, 0:1], min_val=0, max_val=T)
            with act.If(busiest > P):
                experts(EXPERTS)
            norm_of_x("norm_fin")

        @block.tensor
        def _(pe):
            def norm_sum(name, before):
                for k in range(KT):
                    pe.wait_ge(S("squares"), before + k // 2 + 1)
                    last = pe.matmul(bank(name)[:, 0:T], ones, sq[:, k, :], start=(k == 0), stop=(k == KT - 1))
                last.then_inc(filled(name), 1)

            def three_products(out, rows, rest_of_rows, high_part, low_part, start, stop):
                pe.matmul(out, rows, high_part, start=start, stop=False, skip_group_check=True)
                pe.matmul(out, rows, low_part, start=False, stop=False, skip_group_check=True)
                return pe.matmul(out, rest_of_rows, high_part, start=False, stop=stop, skip_group_check=True)

            def project(w, names, rhs, fresh=False):
                pe.wait_ge(*arrived(w))
                for half in range(2):
                    name = f"{names}{half}"
                    wait_bank_free(pe, name)
                    for i in range(2):
                        n = 2 * half + i
                        for k in range(KT):
                            if fresh and n == 0:
                                wait_normed(k)
                            last = pe.matmul(bank(name)[:, i * T:(i + 1) * T], weights(w)[:, k, n * P:(n + 1) * P],
                                             rhs[:, k, :], start=(k == 0), stop=(k == KT - 1))
                    last.then_inc(filled(name), 1)

            def project_tokens(w, names, lhs, halves=(0, 1)):
                pe.wait_ge(*arrived(w))
                for half in halves:
                    name = f"{names}{half}"
                    wait_bank_free(pe, name)
                    for k in range(KT):
                        last = pe.matmul(bank(name)[:, :], lhs[:, k, half * P:(half + 1) * P], weights(w)[:, k, :],
                                         start=(k == 0), stop=(k == KT - 1))
                    last.then_inc(filled(name), 1)

            def low_rank(names, m, rows, rhs):
                for half in range(2):
                    name = f"{names}{half}"
                    wait_bank_free(pe, name)
                    for i in range(2):
                        n = 2 * half + i
                        last = pe.matmul(bank(name)[:, i * T:(i + 1) * T], smallw[0:rows, m, n * P:(n + 1) * P], rhs[0:rows, :],
                                         start=True, stop=True)
                    last.then_inc(filled(name), 1)

            def head_sums(names, src, matrix=head_ones):
                for half in range(2):
                    name = f"{names}{half}"
                    wait_bank_free(pe, name)
                    for i in range(2):
                        last = pe.matmul(bank(name)[:, i * T:(i + 1) * T], matrix, src[:, 2 * half + i, :], start=True, stop=True)
                    last.then_inc(filled(name), 1)

            pe.sem_inc(S("y_copied"), 2)
            pe.sem_inc(S("moe_added"), 4)
            pe.sem_inc(S("moe_hidden"), STEPS)
            pe.sem_inc(S("hidden_split"), STEPS)
            pe.sem_inc(S("hidden_turned"), STEPS)
            pe.wait_ge(S("con_loaded"), 16)
            norm_sum("norm_mix0", 0)
            norm_sum("norm_mem", 4)
            pe.wait_ge(S("norm_scaled"), KT)
            w = ring[:, place["w_lora"][0], 0:KT * 160].rearrange("p (k n) -> p k n", k=KT)
            pe.wait_ge(*arrived("w_lora"))
            for name, i, c0, c1 in (("wd_ad", 0, 0, 32), ("wd_ad", 1, 32, 64), ("gd", 0, 64, 160)):
                for k in range(KT):
                    last = pe.matmul(bank(name)[0:c1 - c0, i * T:(i + 1) * T], w[:, k, c0:c1], h[:, k, :], start=(k == 0), stop=(k == KT - 1))
                if (name, i) != ("wd_ad", 0):
                    last.then_inc(filled(name), 1)
            project("w_r", "r", h)
            project("w_k", "k", h)
            pe.wait_ge(S("smallw_loaded"), 16)
            pe.wait_ge(S("low_rank_in"), 1)
            low_rank("z", 0, 32, lw)
            low_rank("a", 1, 32, la)
            pe.wait_ge(S("low_rank_in"), 2)
            low_rank("rg", 2, 96, lg)
            project("w_v", "v", h)
            pe.wait_ge(S("kk_squared"), 1)
            head_sums("kk", tC)
            project("w_q", "q", h)
            project("w_f", "f", h)
            project_tokens("w_i", "i", h)
            project("w_g", "g", h)
            pe.wait_ge(S("bonus_in"), 4)
            head_sums("bonus", tC)
            for c in range(2):
                wait_bank_free(pe, f"vn{c}")
                pe.wait_ge(*was_read("v1"))
                for n in range(4):
                    last = pe.transpose(bank(f"vn{c}")[:, n * P:(n + 1) * P], rv[:, n, c * C:(c + 1) * C], ident)
                last.then_inc(filled(f"vn{c}"), 1)
            pe.wait_ge(S("norm_scaled"), 2 * KT)
            project("kv0_0", "kv_0", memn)

            def head_rows(head):
                return slice(RW_N * (head % 2), RW_N * (head % 2) + RW_N)

            def scores(c):
                for head in range(8):
                    n, rows, name = head // 2, head_rows(head), f"sc{c}_{head}"
                    if head == 0:
                        pe.wait_ge(S("tildes"), 1)
                    wait_bank_free(pe, name)
                    pb = bank(name)
                    pe.matmul(pb[:, 0:P], AR[rows, n, c, 0, :], bt[rows, n, c * C:(c + 1) * C], start=True, stop=True)
                    pe.matmul(pb[:, P:2 * P], bt[rows, n, c * C:(c + 1) * C], AR[rows, n, c, 1, :], start=True, stop=True)
                    pe.matmul(pb[:, 2 * P:4 * P], kt[rows, n, c * C:(c + 1) * C], AR[rows, n, c, :, :].rearrange("p two t -> p (two t)"),
                              start=True, stop=True).then_inc(filled(name), 1)
                if c == 0:
                    for m, src in ((0, bt), (1, kt)):
                        name = f"bkn{m}"
                        wait_bank_free(pe, name)
                        for n in range(4):
                            last = pe.transpose(bank(name)[:, n * P:(n + 1) * P], src[:, n, 0:C], ident)
                        last.then_inc(filled(name), 1)

            def invert(c, l):
                if l == 0:
                    pe.wait_ge(S("A_copied"), 8 * (c + 1))
                    pe.wait_ge(S("XY_ready"), c + 1)
                for g in range(2):
                    name = f"V{c}_{l}_{g}"
                    wait_bank_free(pe, name)
                    if l:
                        pe.wait_ge(*was_read(f"dY{c}_{l - 1}_{g}"))
                    for i in range(4):
                        last = pe.matmul(bank(name)[:, i * P:(i + 1) * P], Am[:, 4 * g + i, :], Y[:, 4 * g + i, :], start=True, stop=True)
                    last.then_inc(filled(name), 1)
                for g in range(2):
                    pe.wait_ge(*was_read(f"V{c}_{l}_{g}"))
                    if l < LEVELS - 1:
                        name = f"dX{c}_{l}_{g}"
                        wait_bank_free(pe, name)
                        for i in range(4):
                            last = pe.matmul(bank(name)[:, i * P:(i + 1) * P], V[:, 4 * g + i, :], X[:, 4 * g + i, :], start=True, stop=True)
                        last.then_inc(filled(name), 1)
                    name = f"dY{c}_{l}_{g}"
                    wait_bank_free(pe, name)
                    for i in range(4):
                        last = pe.matmul(bank(name)[:, i * P:(i + 1) * P], X[:, 4 * g + i, :], V[:, 4 * g + i, :], start=True, stop=True)
                    last.then_inc(filled(name), 1)

            def head_cols(head):
                return slice(RW_N * head, RW_N * head + RW_N)

            def solve(c):
                name = f"R{c}"
                wait_bank_free(pe, name)
                pe.wait_ge(*was_read(f"sc{c}_7"))
                for c_ in range(2):
                    pe.wait_ge(*was_read(f"vn{c_}"))
                if c == 1:
                    pe.wait_ge(*was_read("M0"))
                for n in range(4):
                    if c == 1:
                        pe.matmul(bank(name)[:, n * P:(n + 1) * P], AR[:, n, c, 0, :], M0[:, n, :, :].rearrange("p two v -> p (two v)"),
                                  start=True, stop=False, skip_group_check=True)
                    for head in (2 * n, 2 * n + 1):
                        last = pe.matmul(bank(name)[:, head_cols(head)], SC[:, head, 1, :], vn[:, c, head_cols(head)],
                                         start=(c == 0), stop=True, skip_group_check=True)
                last.then_inc(filled(name), 1)
                for g in range(2):
                    pe.wait_ge(*was_read(f"dY{c}_{LEVELS - 1}_{g}"))
                pe.wait_ge(*was_read(name))
                name = f"U{c}"
                wait_bank_free(pe, name)
                for head in range(8):
                    last = pe.matmul(bank(name)[:, head_cols(head)], Y[:, head, :], flat(R)[:, head_cols(head)], start=True, stop=True)
                last.then_inc(filled(name), 1)
                pe.wait_ge(*was_read(name))
                if c == 0:
                    wait_bank_free(pe, "M0")
                    for m in range(2):
                        pe.wait_ge(*was_read(f"bkn{m}"))
                    for head in range(8):
                        pb = bank("M0")[head_rows(head), head_cols(head // 2)]
                        pe.matmul(pb, bkn[:, 0, head_cols(head)], flat(U)[:, head_cols(head)], start=True, stop=False)
                        last = pe.matmul(pb, bkn[:, 1, head_cols(head)], vn[:, 0, head_cols(head)], start=False, stop=True)
                    last.then_inc(filled("M0"), 1)
                name = f"ro{c}"
                wait_bank_free(pe, name)
                for n in range(4):
                    if c == 1:
                        pe.matmul(bank(name)[:, n * P:(n + 1) * P], M0[:, n, :, :].rearrange("p two v -> p (two v)"), AR[:, n, c, 1, :],
                                  start=True, stop=False, skip_group_check=True)
                    for head in (2 * n, 2 * n + 1):
                        pb = bank(name)[head_rows(head), n * P:(n + 1) * P]
                        pe.matmul(pb, flat(U)[:, head_cols(head)], SC[:, head, 0, :], start=(c == 0), stop=False, skip_group_check=True)
                        last = pe.matmul(pb, vn[:, c, head_cols(head)], SC[:, head, 2, :], start=False, stop=True, skip_group_check=True)
                last.then_inc(filled(name), 1)

            def level(i):
                if i == 0:
                    for b in range(2):
                        wait_bank_free(pe, f"ho{b}")
                if i <= LEVELS:
                    for b in range(2):
                        name = f"att{i}_{b}"
                        wait_bank_free(pe, name)
                        if i == 0:
                            for half in range(2):
                                pe.wait_ge(*was_read(f"q{half}"))
                                pe.wait_ge(*was_read(f"f{half}"))
                            left, right = hk, hq
                        else:
                            pe.wait_ge(S("level_ready"), i)
                            left = right = tiles4(F[i % 2])
                        for j in range(4):
                            head, c = 2 * b + j // 2, j % 2
                            last = pe.matmul(bank(name)[:, j * P:(j + 1) * P], left[:, head, c * C:(c + 1) * C],
                                             right[:, head, c * C:(c + 1) * C], start=True, stop=True)
                        last.then_inc(filled(name), 1)
                    for b in range(2):
                        name = f"att{i}_{b}"
                        pe.wait_ge(*was_read(name))
                        if i == 0:
                            for half in range(2):
                                pe.wait_ge(*was_read(f"i{half}"))
                        for j in range(4):
                            head, c = 2 * b + j // 2, j % 2
                            last = pe.matmul(ps[6 + b][:, j * P:(j + 1) * P], hi[:, c, head * P:(head + 1) * P],
                                             att[b][:, j * P:(j + 1) * P], start=(i == 0 and j == 0), stop=False, skip_group_check=True)
                        last.then_inc(S("att_used"), 1)
                else:
                    name = f"att{i}_0"
                    wait_bank_free(pe, name)
                    pe.wait_ge(S("level_ready"), i)
                    f = tiles4(F[i % 2])
                    for head in range(4):
                        last = pe.matmul(bank(name)[:, head * P:(head + 1) * P], f[:, head, 0:C], f[:, head, C:T], start=True, stop=True)
                    last.then_inc(filled(name), 1)
                    pe.wait_ge(*was_read(name))
                    for head in range(4):
                        b, j = head // 2, 2 * (head % 2) + 1
                        last = pe.matmul(ps[6 + b][:, j * P:(j + 1) * P], hi[:, 0, head * P:(head + 1) * P],
                                         att[0][:, head * P:(head + 1) * P], start=False, stop=True, skip_group_check=True)
                        if head % 2:
                            last.then_inc(filled(f"ho{b}"), 1)

            for step in order:
                if step[0] == "scores":
                    scores(step[1])
                elif step[0] == "invert":
                    invert(*step[1:])
                elif step[0] == "level":
                    level(step[1])
                elif step[0] == "kv":
                    project("kv0_1", "kv_1", memn)
                elif step[0] == "solve":
                    solve(step[1])
            for c in range(2):
                pe.wait_ge(*was_read(f"ro{c}"))
            head_sums("mean", ro)
            pe.wait_ge(S("ho_squared"), 1)
            head_sums("hsum", tiles4(F[0]), ones)
            project_tokens("kv0_2", "kv_2", memn, [0])
            pe.wait_ge(S("ro_squared"), 1)
            head_sums("var", tA)
            project_tokens("kv0_2", "kv_2", memn, [1])
            project_tokens("kv0_3", "kv_3", memn)

            pe.wait_ge(S("ya_ready"), 1)
            pe.wait_ge(S("yb_ready"), 1)
            project("wout0", "out_0", h)
            project("wout1", "out_1", h)
            norm_done = [2]

            def sum_squares(name):
                wait_bank_free(pe, name)
                n = squares_before[name]
                for b in range(4):
                    pe.wait_ge(S("squares"), n + b + 1)
                    for k in (2 * b, 2 * b + 1):
                        last = pe.matmul(bank(name)[:, 0:T], ones, sq[:, k, :], start=(k == 0), stop=(k == KT - 1))
                last.then_inc(filled(name), 1)
                norm_done[0] += 1

            def wait_normed(k):
                pe.wait_ge(S("norm_scaled"), KT * (norm_done[0] - 1) + k + 1)

            def project_in_three(chunk_, names, ready=None):
                for block_ in range(4):
                    n = [g[:2] for g in dense_granules].index((chunk_, block_))
                    name = names[block_ // 2]
                    if block_ % 2 == 0:
                        wait_bank_free(pe, name)
                    pe.wait_ge(S("dense_low"), n + 1)
                    high_part, _, low_part = dense_granule(n)
                    i = block_ % 2
                    for k in range(KT):
                        if ready and block_ == 0:
                            pe.wait_ge(S("h_low"), ready(k))
                        last = three_products(bank(name)[:, i * T:(i + 1) * T], high_part[:, k, :], low_part[:, k, :],
                                              h_high[:, k, :], h_rounded[:, k, :], start=(k == 0), stop=(k == KT - 1))
                    if i:
                        last.then_inc(filled(name), 1)

            left = [GRANULES.index((STEPS - 3 + i, 1)) + 1 for i in range(3)] + [N_GRANULES]

            def leave_slot(name):
                pe.wait_ge(*is_filled(name))
                pe.sem_inc(S("granules_used"), left[0] - before_expert[0])
                before_expert[0] = left.pop(0)

            before_expert = [0]

            def cross_attention(l):
                sum_squares(f"norm_xat{l}")
                for c in range(2):
                    project_in_three(f"wq{l}_{c}", [f"q{l}_{c}0", f"q{l}_{c}1"],
                                     None if c else lambda k: h_low_before[f"xat{l}"] + k // 2 + 1)
                    if l == 1:
                        leave_slot(f"q{l}_{c}1")
                if l == 1:
                    for c in range(4):
                        pe.wait_ge(*was_read(f"kv1_{c}1"))
                for head in range(4):
                    name = f"s{l}_{head}"
                    wait_bank_free(pe, name)
                    pe.wait_ge(*was_read(f"q{l}_{head // 2}{head % 2}"))
                    for b in range(2):
                        for k in (2 * head, 2 * head + 1):
                            last = pe.matmul(bank(name)[:, b * T:(b + 1) * T], qT[:, k, b * P:(b + 1) * P], kT[:, k, :],
                                             start=(k == 2 * head), stop=(k == 2 * head + 1))
                    last.then_inc(filled(name), 1)
                for head in range(4):
                    name = f"pt{l}_{head}"
                    wait_bank_free(pe, name)
                    pe.wait_ge(S("prob_normed"), 4 * l + head + 1)
                    for m in range(2):
                        for b in range(2):
                            last = pe.transpose(bank(name)[:, m * T + b * P:m * T + (b + 1) * P], prob[:, head, b, m * P:(m + 1) * P], ident)
                    last.then_inc(filled(name), 1)
                    pe.wait_ge(*was_read(name))
                    name = f"pv{l}_{head}"
                    wait_bank_free(pe, name)
                    for i in range(2):
                        for m in range(2):
                            last = pe.matmul(bank(name)[:, i * T:(i + 1) * T], vN[:, m, (2 * head + i) * P:(2 * head + i + 1) * P],
                                             pT[:, head, m, :], start=(m == 0), stop=(m == 1))
                    last.then_inc(filled(name), 1)
                for head in range(4):
                    pe.wait_ge(*was_read(f"pv{l}_{head}"))
                for c in range(2):
                    project_in_three(f"wo{l}_{c}", [f"xo{l}_{c}0", f"xo{l}_{c}1"])
                    if l == 1:
                        leave_slot(f"xo{l}_{c}1")

            cross_attention(0)

            sum_squares("norm_ffn0")

            def step_up(step):
                for part in range(4):
                    n = FFN_GRANULES.index((step, part))
                    name, i = f"f{step}_{part // 2}", part % 2
                    if i == 0:
                        wait_bank_free(pe, name)
                    pe.wait_ge(S("ffn_low"), n + 1)
                    high_part, _, low_part = ffn_granule(n)
                    for k in range(KT):
                        if n == 0:
                            pe.wait_ge(S("h_low"), h_low_before["ffn0"] + k // 2 + 1)
                        cols = slice(k * P, (k + 1) * P)
                        last = three_products(bank(name)[:, i * T:(i + 1) * T], high_part[:, cols], low_part[:, cols],
                                              h_high[:, k, :], h_rounded[:, k, :], start=(k == 0), stop=(k == KT - 1))
                    last.then_inc(S("ffn_used"), 1)
            def step_down(step):
                pe.wait_ge(S("hidden_low"), 2 * step + 2)
                for j in range(2):
                    count = FFN_GRANULES.index((step, 4 + j))
                    pe.wait_ge(S("ffn_low"), count + 1)
                    high_part, _, low_part = ffn_granule(count)
                    for n in range(KT):
                        if step == j == 0 and n % 2 == 0:
                            wait_bank_free(pe, f"fo{n // 2}")
                        cols = slice(n * P, (n + 1) * P)
                        last = three_products(ps[4 + n // 2][:, (n % 2) * T:(n % 2 + 1) * T], high_part[:, cols], low_part[:, cols],
                                              fh_high[step % 2][:, j, :], fh_low[step % 2][:, j, :],
                                              start=(step == 0 and j == 0 and n % 2 == 0), stop=(step == STEPS - 1 and j == 1))
                        if step == STEPS - 1 and j == 1 and n % 2:
                            last.then_inc(filled(f"fo{n // 2}"), 1)
                    if (step, j) != (STEPS - 1, 1):
                        last.then_inc(S("ffn_used"), 1)

            def s5_piece(p):
                pe.wait_ge(S("s5_w1t"), p + 1)
                for w, name in enumerate(("re", "im")):
                    name = f"{name}_{p}"
                    wait_bank_free(pe, name)
                    for g in range(PIECE):
                        last = pe.transpose(bank(name)[:, g * P:(g + 1) * P], sW1T[:, w, g, :, :].rearrange("p k m -> p (k m)"), ident)
                    last.then_inc(filled(name), 1)
                pe.wait_ge(S("s5_cw"), p + 1)
                for parity in range(2):
                    name = f"k{parity}_{p}"
                    wait_bank_free(pe, name)
                    rows = slice(S5_P * parity, S5_P * (parity + 1))
                    for g in range(PIECE):
                        for w in range(2):
                            last = pe.matmul(bank(name)[0:S5_M, g * P:(g + 1) * P], sbb[rows, w, PIECE * p + g, :],
                                             sCW[rows, g, w, 0:TAU, :].rearrange("p k m -> p (k m)"), start=(w == 0), stop=(w == 1))
                    last.then_inc(filled(name), 1)

            for step in range(STEPS):
                step_up(step)
                if step:
                    step_down(step - 1)
                if step >= 3:
                    s5_piece(step - 3)
            step_down(STEPS - 1)

            sum_squares("norm_mix1")
            project("cw0", "u_0", h, fresh=True)
            project("cw1", "u_1", h)
            project("kv1_0", "kv1_0", memn)
            project("kv1_1", "kv1_1", memn)
            pe.wait_ge(S("u_blocks"), 16 * TAU)
            table = lambda name: ring[:, place[name][0], 0:DENSE]
            for half in range(2):
                pe.wait_ge(*arrived(f"s5_W1_{half}"))
                for w in range(2):
                    wait_bank_free(pe, f"Z{w}{half}")
                w1 = table(f"s5_W1_{half}").rearrange("p (g w c) -> p g w c", g=PAIRS // 2, w=2)
                for w in range(2):
                    for g in range(PAIRS // 2):
                        for parity in range(2):
                            rows = slice(S5_P * parity, S5_P * (parity + 1))
                            last = pe.matmul(bank(f"Z{w}{half}")[rows, g * BLOCKS:(g + 1) * BLOCKS], w1[:, g, w, rows],
                                             Ub[:, PAIRS * half + 2 * g + parity, :], start=True, stop=True)
                    last.then_inc(filled(f"Z{w}{half}"), 1)
            for half in range(2):
                pe.wait_ge(*arrived(f"s5_T_{half}"))
                within = table(f"s5_T_{half}").rearrange("p (g c) -> p g c", g=PAIRS)
                for quarter in (2 * half, 2 * half + 1):
                    wait_bank_free(pe, f"Y{quarter}")
                    for group in range(16 * quarter, 16 * quarter + 16):
                        first = group % 16 == 0
                        last = pe.matmul(bank(f"Y{quarter}")[:, group % 16 * BLOCKS:(group % 16 + 1) * BLOCKS], within[:, group - PAIRS * half, :],
                                         Ub[:, group, :], start=first, stop=False, skip_group_check=True)
                last.then_inc(S("T_used"), 1)
            pe.wait_ge(S("states"), 1)
            for half in range(2):
                pe.wait_ge(*arrived(f"s5_W2_{half}"))
                from_state = table(f"s5_W2_{half}").rearrange("p (g w c) -> p g w c", g=PAIRS // 2, w=2)
                for quarter in (2 * half, 2 * half + 1):
                    for w in range(2):
                        for pair in range(8 * quarter, 8 * quarter + 8):
                            i = pair % 8
                            last = pe.matmul(bank(f"Y{quarter}")[:, i * 2 * BLOCKS:(i + 1) * 2 * BLOCKS], from_state[:, pair - 16 * half, w, :],
                                             Xs[w][:, pair, :, :].rearrange("p two j -> p (two j)"),
                                             start=False, stop=(w == 1 and i == 7), skip_group_check=True)
                    last.then_inc(filled(f"Y{quarter}"), 1)
            project_tokens("kv1_2", "kv1_2", memn)
            project_tokens("kv1_3", "kv1_3", memn)
            for c in range(4):
                project_in_three(f"glu{c}", [f"val{c}", f"gate{c}"], None if c else lambda k: h_low_before["glu"] + k + 1)
            cross_attention(1)

            sum_squares("norm_ffn1")
            pe.wait_ge(S("router_loaded"), 16)
            wait_bank_free(pe, "logits")
            for b in range(2):
                for k in range(KT):
                    if b == 0:
                        wait_normed(k)
                    last = pe.matmul(bank("logits")[:, b * EXPERTS:(b + 1) * EXPERTS], h[:, k, b * P:(b + 1) * P], router[:, k, :],
                                     start=(k == 0), stop=(k == KT - 1))
            last.then_inc(filled("logits"), 1)
            for m in range(4):
                name = f"hN{m}"
                wait_bank_free(pe, name)
                for i in range(4):
                    k = 4 * (m % 2) + i
                    last = pe.transpose(bank(name)[:, i * P:(i + 1) * P], h[:, k, (m // 2) * P:(m // 2 + 1) * P], ident)
                last.then_inc(filled(name), 1)
            pe.wait_ge(S("selected"), 1)
            wait_bank_free(pe, "places")
            strict = con[:, CONST_COLS["strict"], :]
            pb = bank("places")
            pe.matmul(pb[:, 0:8], strict, sel[:, 0, :], start=True, stop=True)
            pe.matmul(pb[:, 8:16], strict, sel[:, 1, :], start=True, stop=False)
            pe.matmul(pb[:, 8:16], ones, sel[:, 0, :], start=False, stop=True)
            pe.matmul(pb[:, 16:24], ones, sel[:, 0, :], start=True, stop=False)
            pe.matmul(pb[:, 16:24], ones, sel[:, 1, :], start=False, stop=True).then_inc(filled("places"), 1)
            for m in range(4):
                pe.wait_ge(*was_read(f"hN{m}"))

            def gather(i, after_another=True):
                pe.wait_ge(S("slots_ready"), i + 1)
                if after_another:
                    pe.wait_ge(S("moe_added"), i * 4)
                for b in range(2):
                    for k in range(4):
                        for c in range(2):
                            last = pe.matmul(ps[6 + b][:, k * P:(k + 1) * P], hN[:, c, (4 * b + k) * P:(4 * b + k + 1) * P], Gs[:, c, :],
                                             start=(c == 0), stop=(c == 1))
                    last.then_inc(S("gathered"), 1)

            def turn_gates():
                for c in range(2):
                    last = pe.transpose(ps[3][:, c * P:(c + 1) * P], Gg[:, c, :], ident)
                last.then_inc(S("gates_turned"), 1)

            def expert(i, last_one=False):
                pe.wait_ge(S("gather_split"), 2 * i + 2)

                def up(step):
                    pe.wait_ge(S("moe_hidden"), (i + 1) * STEPS + max(step - 1, 0))
                    for part in range(2):
                        n, high_part, _, low_part = granule(step, part)
                        pe.wait_ge(S("weights_low"), i * N_GRANULES + n + 1)
                        for k in range(KT // 2):
                            cols = slice(k * 2 * STEP, (k + 1) * 2 * STEP)
                            kk_ = KT // 2 * part + k
                            last = three_products(ps[step % 2][:, :], hc[:, kk_, :], hc_low[:, kk_, :], high_part[:, cols], low_part[:, cols],
                                                  start=(kk_ == 0), stop=(kk_ == KT - 1))
                        last.then_inc(S("granules_used"), 1)

                def turn(step):
                    pe.wait_ge(S("moe_hidden"), (i + 1) * STEPS + step + 1)
                    pe.wait_ge(S("hidden_split"), (i + 1) * STEPS + step)
                    for j in range(2):
                        last = pe.transpose(ps[2][:, j * P:(j + 1) * P], hid[step % 2][:, j * P:(j + 1) * P], ident)
                    last.then_inc(S("hidden_turned"), 1)

                def down(step):
                    pe.wait_ge(S("hidden_split"), (i + 1) * STEPS + step + 1)
                    if step == 0:
                        pe.wait_ge(S("y_copied"), 2 * i + 2)
                    n, high_part, _, low_part = granule(step, 2)
                    pe.wait_ge(S("weights_low"), i * N_GRANULES + n + 1)
                    for j in range(2):
                        for b in range(2):
                            cols = slice(j * D + b * 512, j * D + (b + 1) * 512)
                            last = three_products(ps[4 + b][:, :], hidT[step % 2][:, j, :], hidT_low[step % 2][:, j, :],
                                                  high_part[:, cols], low_part[:, cols],
                                                  start=(step == 0 and j == 0), stop=(step == STEPS - 1 and j == 1))
                    last.then_inc(S("granules_used"), 1)

                for step in range(STEPS):
                    up(step)
                    if step >= 2:
                        down(step - 2)
                    if step >= 1:
                        turn(step - 1)
                down(STEPS - 2)
                turn(STEPS - 1)
                if not last_one:
                    gather(i + 1)
                down(STEPS - 1)
                pe.wait_ge(S("y_copied"), 2 * i + 4)
                pe.wait_ge(S("gates_copied"), i + 1)
                if not last_one:
                    pe.wait_ge(S("gather_split"), 2 * i + 4)
                for m in range(4):
                    pe.wait_ge(S("moe_added"), i * 4 + max(m - 1, 0) + 4)
                    for j in range(2):
                        n = 2 * m + j
                        last = pe.matmul(ps[6 + m % 2][:, j * T:(j + 1) * T], yc[:, n * P:(n + 1) * P], GT, start=True, stop=True)
                    last.then_inc(S("scattered"), 1)

                if not last_one:
                    turn_gates()

            def experts(first):
                gather(first, after_another=first > 0)
                turn_gates()
                with pe.Fori(0, EXPERTS - 1) as e:
                    expert(e + first if first else e)
                expert(first + EXPERTS - 1, last_one=True)

            experts(0)
            pe.wait_ge(S("flag_ready"), 1)
            busiest = pe.value_load(flag[0:1, 0:1], min_val=0, max_val=T)
            with pe.If(busiest > P):
                experts(EXPERTS)
            sum_squares("norm_fin")

        @block.vector
        def _(dve):
            linked = [0]

            def link(ins):
                linked[0] += 1
                ins.then_inc(S("dve_link"), 1)
                dve.wait_ge(S("dve_link"), linked[0])

            norms = [0]

            def normalise(name, src, gain, dst):
                dve.wait_ge(*was_read(name))
                if norms[0]:
                    dve.wait_ge(S("norm_scaled"), norms[0])
                norms[0] += KT
                link(dve.reciprocal(rstd[:, :], nrm[:, :]))
                for k in range(KT):
                    dve.scalar_tensor_tensor(out=dst[:, k, :], in0=src[:, k, :], scalar=pc(gain, k), in1=rstd[:, :],
                                             op0=ALU.mult, op1=ALU.mult).then_inc(S("norm_scaled"), 1)

            dve.wait_ge(S("parityloaded"), 16)
            dve.tensor_scalar(omu[:, :], par[:, MU0:MU1], -1.0, 1.0, ALU.mult, ALU.add).then_inc(S("omu_ready"), 1)
            lb = pc("lb", 0, P, 4)
            dve.tensor_tensor(lbs[:, 0, :], lb, lb, ALU.subtract).then_inc(S("lb_shifted"), 1)
            dve.wait_ge(S("x_loaded"), 16)
            normalise("norm_mix0", x, "mix0", h)
            dve.wait_ge(S("mem_loaded"), 16)
            normalise("norm_mem", memn, "memg", memn)
            dve.wait_ge(S("lb_exp"), 1)
            link(dve.reciprocal(lbs[:, 0, :], lbs[:, 1, :]))
            link(dve.tensor_tensor(lbs[:, 0, :], lbs[:, 0, :], lbs[:, 1, :], ALU.mult))
            link(dve.tensor_tensor(lbs[:, 2, :], lbs[:, 0, :], lbs[:, 0, :], ALU.subtract))
            dve.tensor_scalar(lbs[:, 3, :], lbs[:, 2, :], -1.0, 1.0, ALU.mult, ALU.add).then_inc(S("lb_ready"), 1)

            def shifted(dst, src, mu, own):
                dve.wait_ge(S("own_part"), own)
                return dve.scalar_tensor_tensor(out=dst[:, 1:T], in0=src[:, 0:T - 1], scalar=mu, in1=dst[:, 1:T],
                                                op0=ALU.mult, op1=ALU.add)

            shifted(lw[0:32, :], bank("wd_ad")[0:32, 0:T], pc("mu_wd", 0, 32), 2).then_inc(read("wd_ad"), 1)
            shifted(la[0:32, :], bank("wd_ad")[0:32, T:2 * T], pc("mu_ad", 0, 32), 2).then_inc(read("wd_ad"), 1)
            shifted(lg[0:96, :], bank("gd")[0:96, 0:T], pc("mu_gd", 0, 96), 3).then_inc(read("gd"), 1)

            def shift(name, dst, own):
                for half in range(2):
                    for i in range(2):
                        n = 2 * half + i
                        last = shifted(dst[:, n, :], bank(f"{name}{half}")[:, i * T:(i + 1) * T], pc("mu_" + name, n), own + 2 * half + 2)
                    last.then_inc(read(f"{name}{half}"), 1)

            shift("r", rr, 3)
            shift("k", rk, 7)
            for half in range(2):
                dve.wait_ge(*was_read(f"z{half}"))
            link(dve.tensor_scalar(ld, ld, -float(np.exp(-0.5)), None, ALU.mult))
            for n in range(4):
                for c in range(2):
                    last = dve.tensor_tensor_scan(cL[:, n, c * C:(c + 1) * C], ones, ld[:, n, c * C:(c + 1) * C], 0.0, ALU.mult, ALU.add)
            link(last)
            shift("v", rv, 11)
            for half in range(2):
                dve.wait_ge(*is_filled(f"kk{half}"))
                dve.tensor_scalar(flat(tC[:, 2 * half:2 * half + 2, :]), bank(f"kk{half}")[:, :], 1e-24, None, ALU.max).then_inc(read(f"kk{half}"), 1)
            dve.wait_ge(S("kk_root"), 1)
            link(dve.reciprocal(tC, tC))
            link(dve.tensor_tensor(kk, kk, tC, ALU.mult))
            for half in range(2):
                dve.wait_ge(*was_read(f"a{half}"))
            for n in range(4):
                last = dve.tensor_scalar(tC[:, n, :], ra[:, n, :], -1.0, pc("k_a", n), ALU.add, ALU.mult)
            link(last)
            link(dve.scalar_tensor_tensor(out=rk, in0=tC, scalar=1.0, in1=rk, op0=ALU.add, op1=ALU.mult))
            dve.tensor_tensor(ra, ra, kk, ALU.mult)
            for n in range(4):
                dve.scalar_tensor_tensor(out=tC[:, n, :], in0=rr[:, n, :], scalar=pc("r_k", n), in1=rk[:, n, :],
                                         op0=ALU.mult, op1=ALU.mult).then_inc(S("bonus_in"), 1)
            mid = small[:, 4:12].rearrange("p (n c) -> p n c", n=4)
            cL8 = flat(cL).rearrange("p (m t) -> p m t", t=C)
            link(dve.tensor_copy(small[:, 4:12], cL8[:, :, C // 2 - 1]))
            dve.tensor_copy(small[:, 0:4], mid[:, :, 1])
            link(dve.tensor_tensor(cL8, cL8, small[:, 4:12].rearrange("p (m o) -> p m o", o=1).broadcast_to([P, 8, C]), ALU.subtract))
            dve.tensor_tensor(ld, cL, ld, ALU.subtract).then_inc(S("decays_in"), 1)

            for half in range(2):
                dve.wait_ge(S("q_sigmoid"), half + 1)
                v = flat(hq[:, 2 * half:2 * half + 2, :])
                dve.tensor_tensor(v, v, bank(f"q{half}")[:, :], ALU.mult).then_inc(read(f"q{half}"), 1)
            for half in range(2):
                dve.wait_ge(S("f_sigmoid"), half + 1)
                for i in range(2):
                    n = 2 * half + i
                    dve.tensor_scalar(hk[:, n, :], hk[:, n, :], lbs[:, 3, n:n + 1], None, ALU.mult)
                pb = bank(f"f{half}")[:, :]
                sl = slice(half * 512, (half + 1) * 512)
                dve.tensor_scalar(flat(hL)[:, sl], pb, 0.0, None, ALU.min)
                dve.tensor_scalar(F[1][:, sl], pb, -1.0, 60.0, ALU.mult, ALU.min).then_inc(read(f"f{half}"), 1)
            for half in range(2):
                dve.wait_ge(S("g_sigmoid"), half + 1)
                v = flat(hg[:, 2 * half:2 * half + 2, :])
                dve.tensor_tensor(v, v, bank(f"g{half}")[:, :], ALU.mult).then_inc(read(f"g{half}"), 1)
            dve.wait_ge(S("decays_out"), 2)
            v4 = lambda a: a.rearrange("p n (c t) -> p n c t", c=2)
            for n in range(4):
                a, b = v4(kk)[:, n], v4(tB)[:, n]
                dve.scalar_tensor_tensor(out=AR[:, n, :, 0, :], in0=a, scalar=-1.0, in1=b, op0=ALU.mult, op1=ALU.mult)
                last = dve.tensor_tensor(AR[:, n, :, 1, :], v4(rr)[:, n], v4(cL)[:, n], ALU.mult)
            dve.tensor_tensor(bt, ra, tA, ALU.mult)
            dve.tensor_tensor(kt, rk, tA, ALU.mult)
            dve.tensor_tensor(small[:, 0:4], small[:, 0:4], cL[:, :, C - 1], ALU.mult).then_inc(S("tildes"), 1)
            for half in range(2):
                dve.wait_ge(*is_filled(f"bonus{half}"))
                dve.tensor_tensor(flat(bonus[:, 2 * half:2 * half + 2, :]), bank(f"bonus{half}")[:, :],
                                  flat(rv[:, 2 * half:2 * half + 2, :]), ALU.mult).then_inc(read(f"bonus{half}"), 1)
            dve.wait_ge(S("f_logs"), 1)
            link(dve.tensor_tensor(flat(hL), flat(hL), F[0], ALU.subtract))
            link(dve.tensor_tensor(F[0], flat(hL), F[1], ALU.add))
            for n in range(4):
                last = dve.tensor_tensor_scan(hL[:, n, :], flat(cc("ones", 2)),
                                              F[0][:, n * T:(n + 1) * T], 0.0, ALU.mult, ALU.add)
            link(last)

            def distances(i):
                if i == 0 or i > LEVELS + 1:
                    return
                w = 1 << (i - 1)
                L = flat(hL).rearrange("p (b u) -> p b u", u=2 * w)
                f = F[i % 2].rearrange("p (b u) -> p b u", u=2 * w)
                edge = L[:, :, w - 1:w].broadcast_to([P, 1024 // (2 * w), w])
                if i > 2:
                    dve.wait_ge(*is_filled(f"att{i - 2}_1"))
                dve.tensor_tensor(f[:, :, 0:w], edge, L[:, :, 0:w], ALU.subtract)
                dve.tensor_tensor(f[:, :, w:2 * w], L[:, :, w:2 * w], edge, ALU.subtract).then_inc(S("distances"), 1)

            def factors(i):
                if i == 0 or i > LEVELS + 1:
                    return
                w = 1 << (i - 1)
                f = F[i % 2].rearrange("p (b u) -> p b u", u=2 * w)
                dve.wait_ge(S("level_decays"), i)
                k = flat(hk).rearrange("p (b u) -> p b u", u=2 * w)
                q = flat(hq).rearrange("p (b u) -> p b u", u=2 * w)
                dve.tensor_tensor(f[:, :, 0:w], f[:, :, 0:w], k[:, :, 0:w], ALU.mult)
                dve.tensor_tensor(f[:, :, w:2 * w], f[:, :, w:2 * w], q[:, :, w:2 * w], ALU.mult).then_inc(S("level_ready"), 1)

            def level(i):
                distances(i + 1)
                for b in range(2 if i <= LEVELS else 1):
                    name = f"att{i}_{b}"
                    dve.wait_ge(*is_filled(name))
                    if i:
                        dve.wait_ge(S("att_used"), 2 * (i - 1) + b + 1)
                    if i <= LEVELS:
                        mask = con[:, i:i + 1, :].broadcast_to([P, 4, P])
                        dve.tensor_tensor(stack(att[b], 4), stack(bank(name)[:, :], 4), mask, ALU.mult).then_inc(read(name), 1)
                    else:
                        dve.tensor_copy(att[0], bank(name)[:, :]).then_inc(read(name), 1)
                factors(i + 1)

            def scores(c):
                if c == 0:
                    link(dve.memset(M0, 0.0))
                else:
                    dve.wait_ge(*is_filled("ro0"))
                for head in range(8):
                    name = f"sc{c}_{head}"
                    dve.wait_ge(*is_filled(name))
                    dve.wait_ge(S("A_copied"), 8 * c + head + 1)
                    dve.tensor_tensor(SC[:, head, :, :], bank(name)[:, P:4 * P].rearrange("p (m t) -> p m t", m=3),
                                      cc("incl0", 3), ALU.mult).then_inc(read(name), 1)
                one = con[:, 0:1, :].broadcast_to([P, 8, P])
                dve.tensor_copy(X, one)
                dve.tensor_copy(Y, one).then_inc(S("XY_ready"), 1)

            def invert(c, l):
                half = lambda a, g: a[:, 4 * g:4 * g + 4, :]
                mask = con[:, 1 + l:2 + l, :].broadcast_to([P, 4, P])
                for g in range(2):
                    name = f"V{c}_{l}_{g}"
                    dve.wait_ge(*is_filled(name))
                    if c or l:
                        before = f"dY{c}_{l - 1}_{g}" if l else f"dY{c - 1}_{LEVELS - 1}_{g}"
                        dve.wait_ge(*is_filled(before))
                    dve.tensor_tensor(half(V, g), stack(bank(name)[:, :], 4), mask, ALU.mult).then_inc(read(name), 1)
                for g in range(2):
                    dve.wait_ge(*is_filled(f"dY{c}_{l}_{g}"))
                    if l < LEVELS - 1:
                        dve.wait_ge(*is_filled(f"dX{c}_{l}_{g}"))
                        dve.tensor_tensor(half(X, g), half(X, g), stack(bank(f"dX{c}_{l}_{g}")[:, :], 4), ALU.add).then_inc(read(f"dX{c}_{l}_{g}"), 1)
                    dve.tensor_tensor(half(Y, g), half(Y, g), stack(bank(f"dY{c}_{l}_{g}")[:, :], 4), ALU.add).then_inc(read(f"dY{c}_{l}_{g}"), 1)

            for step in order:
                if step[0] == "scores":
                    scores(step[1])
                elif step[0] == "invert":
                    invert(*step[1:])
                elif step[0] == "level":
                    level(step[1])
                elif step == ("solve", 0):
                    dve.wait_ge(*is_filled("M0"))
                    for n in range(4):
                        for two in range(2):
                            rows = slice(RW_N * two, RW_N * two + RW_N)
                            last = dve.tensor_scalar(M0[rows, n, two, :], bank("M0")[rows, n * RW_N:(n + 1) * RW_N], small[rows, n:n + 1], None, ALU.mult)
                    last.then_inc(read("M0"), 1)
            for b in range(2):
                name = f"mean{b}"
                dve.wait_ge(*is_filled(name))
                v = flat(ro[:, 2 * b:2 * b + 2, :])
                dve.scalar_tensor_tensor(out=v, in0=bank(name)[:, :], scalar=-1.0 / RW_N, in1=v, op0=ALU.mult, op1=ALU.add).then_inc(read(name), 1)
            for b in range(2):
                dve.wait_ge(*was_read(f"hsum{b}"))
            link(dve.reciprocal(F[1], F[1]))
            link(dve.scalar_tensor_tensor(out=flat(ho), in0=flat(ho), scalar=pc("onorm"), in1=F[1], op0=ALU.mult, op1=ALU.mult))
            for b in range(2):
                dve.wait_ge(*was_read(f"g{b}"))
            dve.tensor_tensor(h[:, 0:4, :], ho, hg, ALU.mult).then_inc(S("ya_ready"), 1)
            for b in range(2):
                dve.wait_ge(*was_read(f"var{b}"))
            link(dve.reciprocal(tB, tB))
            link(dve.tensor_tensor(ro, ro, tB, ALU.mult))
            for n in range(4):
                last = dve.tensor_scalar(ro[:, n, :], ro[:, n, :], pc("gn_g", n), pc("gn_b", n), ALU.mult, ALU.add)
            link(last)
            for b in range(2):
                dve.wait_ge(*was_read(f"bonus{b}"))
                dve.wait_ge(*was_read(f"rg{b}"))
            link(dve.tensor_tensor(ro, ro, bonus, ALU.add))
            dve.tensor_tensor(h[:, 4:8, :], ro, rg, ALU.mult).then_inc(S("yb_ready"), 1)

            def add_to_x(name, b):
                dve.wait_ge(*is_filled(name))
                v = flat(x[:, 2 * b:2 * b + 2, :])
                dve.tensor_tensor(v, v, bank(name)[:, :], ALU.add).then_inc(S("x_written"), 1)
                x_written[0] += 1
                dve.wait_ge(S("x_written"), x_written[0])
                dve.sem_inc(read(name), 1)

            x_written = [0]

            def rest_of_h(name, size, pieces):
                for b in pieces:
                    blocks = slice(size * b, size * b + size)
                    dve.wait_ge(S("h_high"), h_high_before[name] + b + 1)
                    dve.tensor_tensor(h_rounded[:, blocks, :], h[:, blocks, :], in_float32(h_high[:, blocks, :]), ALU.subtract)\
                       .then_inc(S("h_low"), 1)

            def norm_of_x(name, gain, permuted=False, split=None):
                dve.wait_ge(*was_read(name))
                dve.wait_ge(S("norm_scaled"), norms[0])
                norms[0] += KT
                link(dve.reciprocal(rstd[:, :], nrm[:, :]))
                v = (lambda a: a.rearrange("p (j s) -> p s j", s=TAU)) if permuted else (lambda a: a)
                o = (lambda a: a.rearrange("p (s j) -> p s j", s=TAU)) if permuted else (lambda a: a)
                for k in range(KT):
                    dve.scalar_tensor_tensor(out=o(h[:, k, :]), in0=v(x[:, k, :]), scalar=pc(gain, k), in1=v(rstd[:, :]),
                                             op0=ALU.mult, op1=ALU.mult).then_inc(S("norm_scaled"), 1)
                    if split and k >= 3 and k % 2:
                        rest_of_h(split, 2, [k // 2 - 1])
                if split:
                    rest_of_h(split, 2, [KT // 2 - 1])

            def dense_weights_rest(granules):
                for n in granules:
                    high_part, words, low_part = dense_granule(n)
                    dve.wait_ge(S("dense_high"), n + 1)
                    dve.tensor_tensor(low_part, words, in_float32(high_part), ALU.subtract).then_inc(S("dense_low"), 1)

            def ffn_weights_rest(n):
                high_part, words, low_part = ffn_granule(n)
                dve.wait_ge(S("ffn_high"), n + 1)
                dve.tensor_tensor(low_part, words, in_float32(high_part), ALU.subtract).then_inc(S("ffn_low"), 1)

            def cross_attention(l):
                norm_of_x(f"norm_xat{l}", f"xat{l}", split=f"xat{l}")
                for c in range(2):
                    for half in range(2):
                        dense_weights_rest(served[f"q{l}_{c}{half}"])
                for head in range(4):
                    dve.wait_ge(*is_filled(f"s{l}_{head}"))
                    m = smax[:, 2 * head:2 * head + 2]
                    link(dve.tensor_reduce(m, bank(f"s{l}_{head}")[:, :].rearrange("p (b m) -> p b m", b=2), AX.X, ALU.max))
                    dve.tensor_scalar(m, m, -XA_SCALE, None, ALU.mult).then_inc(S("score_max"), 1)
                for head in range(4):
                    dve.wait_ge(*was_read(f"s{l}_{head}"))
                    m = ssum[:, 2 * head:2 * head + 2]
                    link(dve.reciprocal(m, m))
                    for b in range(2):
                        last = dve.tensor_scalar(prob[:, head, b, :], prob[:, head, b, :], ssum[:, 2 * head + b:2 * head + b + 1], None, ALU.mult)
                    last.then_inc(S("prob_normed"), 1)
                for head in range(4):
                    dve.wait_ge(S("h_high"), h_high_before[f"pv{l}"] + head + 1)
                    name, blocks = f"pv{l}_{head}", slice(2 * head, 2 * head + 2)
                    dve.tensor_tensor(flat(h_rounded[:, blocks, :]), bank(name)[:, :], in_float32(flat(h_high[:, blocks, :])), ALU.subtract)\
                       .then_inc(read(name), 1)
                for c in range(2):
                    for half in range(2):
                        name = f"xo{l}_{c}{half}"
                        dense_weights_rest(served[name])
                        if l == c == 0 and half == 1:
                            add_to_x(name, 1)
                            for n in range(len(ffn_high)):
                                ffn_weights_rest(n)
                        else:
                            add_to_x(name, 2 * c + half)

            dense_weights_rest(group_start["wq0_0"])
            for c in range(2):
                for half in range(2):
                    add_to_x(f"out_{c}{half}", 2 * c + half)
            cross_attention(0)
            norm_of_x("norm_ffn0", "ffn0", split="ffn0")

            def w_(i):
                return sw[:, i, :]

            def tt(o, a, b, op):
                return dve.tensor_tensor(o, a, b, op)

            def ts(o, a, s1, s2, op0, op1=None):
                return dve.tensor_scalar(o, a, s1, s2, op0, op1) if op1 is not None else dve.tensor_scalar(o, a, s1, s2, op0)

            def product(o_re, o_im, a_re, a_im, b_re, b_im, work, conjugate=False):
                t0, t1, t2_, t3 = work
                tt(t0, a_re, b_re, ALU.mult)
                tt(t1, a_im, b_im, ALU.mult)
                tt(t2_, a_re, b_im, ALU.mult)
                link(tt(t3, a_im, b_re, ALU.mult))
                tt(o_re, t0, t1, ALU.add if conjugate else ALU.subtract)
                link(tt(o_im, t3, t2_, ALU.subtract if conjugate else ALU.add))

            def s5_angles():
                dve.wait_ge(S("s5_a_loaded"), 16)
                dve.wait_ge(S("s5_dt"), 1)
                link(ts(w_(9), sa[:, 0, :], -1e-4, None, ALU.min))
                tt(w_(1), w_(9), w_(0), ALU.mult)
                link(tt(w_(2), sa[:, 1, :], w_(0), ALU.mult))
                for dst, turn in ((5, 0.0), (7, 0.25)):
                    if turn:
                        link(ts(w_(8), w_(2), 1 / TWO_PI, turn, ALU.mult, ALU.add))
                    else:
                        link(ts(w_(8), w_(2), 1 / TWO_PI, None, ALU.mult))
                    link(ts(w_(8), w_(8), ROUNDER, None, ALU.add))
                    link(ts(w_(8), w_(8), ROUNDER, None, ALU.subtract))
                    link(dve.scalar_tensor_tensor(out=w_(dst), in0=w_(8), scalar=-TWO_PI_HI, in1=w_(2), op0=ALU.mult, op1=ALU.add))
                    link(dve.scalar_tensor_tensor(out=w_(dst), in0=w_(8), scalar=-(TWO_PI - TWO_PI_HI), in1=w_(dst), op0=ALU.mult, op1=ALU.add))
                    if turn:
                        link(ts(w_(dst), w_(dst), TWO_PI * turn, None, ALU.add))
                    link(ts(w_(dst), w_(dst), PI_BELOW, -PI_BELOW, ALU.min, ALU.max))
                dve.tensor_copy(w_(10), w_(2)).then_inc(S("s5_angles"), 1)

            def s5_powers():
                dve.wait_ge(S("s5_sines"), 1)
                pw = lambda w, k: spw[:, w, k, :]
                dve.memset(pw(0, 0), 1.0)
                dve.memset(pw(1, 0), 0.0)
                tt(pw(0, 1), w_(3), w_(6), ALU.mult)
                link(tt(pw(1, 1), w_(3), w_(4), ALU.mult))
                for k in range(2, TAU + 1):
                    product(pw(0, k), pw(1, k), pw(0, k - 1), pw(1, k - 1), pw(0, 1), pw(1, 1), [w_(12 + i) for i in range(4)])

            def s5_input_map():
                pw = lambda w, k: spw[:, w, k, :]
                tt(w_(12), w_(9), w_(9), ALU.mult)
                tt(w_(13), sa[:, 1, :], sa[:, 1, :], ALU.mult)
                link(ts(w_(11), pw(0, 1), -1.0, None, ALU.add))
                link(tt(w_(12), w_(12), w_(13), ALU.add))
                link(dve.reciprocal(w_(10), w_(12)))
                product(w_(16), w_(17), w_(11), pw(1, 1), w_(9), sa[:, 1, :], [w_(12 + i) for i in range(4)], conjugate=True)
                tt(w_(16), w_(16), w_(10), ALU.mult)
                link(tt(w_(17), w_(17), w_(10), ALU.mult))
                dve.wait_ge(S("s5_bc_loaded"), 16)
                wide = lambda v: v.rearrange("p (g o) -> p g o", o=1).broadcast_to([P, PAIRS, S5_M])
                q = [sCW_flat(i) for i in range(2)]
                c_re, c_im, b_re, b_im = wide(w_(16)), wide(w_(17)), sbc[:, 0, :, :], sbc[:, 1, :, :]
                g3 = lambda a: a.rearrange("p (g m) -> p g m", g=PAIRS)
                tt(g3(q[0]), c_re, b_re, ALU.mult)
                link(tt(g3(q[1]), c_im, b_im, ALU.mult))
                link(tt(sbb[:, 0, :, :], g3(q[0]), g3(q[1]), ALU.subtract))
                tt(g3(q[0]), c_re, b_im, ALU.mult)
                link(tt(g3(q[1]), c_im, b_re, ALU.mult))
                link(tt(sbb[:, 1, :, :], g3(q[0]), g3(q[1]), ALU.add))
                rc, rs = s5rot[:, 0, :], s5rot[:, 1, :]
                wk = [w_(12 + i) for i in range(4)]
                product(rc, rs, w_(6), w_(4), w_(6), w_(4), wk)
                product(rc, rs, rc, rs, rc, rs, wk)
                product(rc, rs, rc, rs, rc, rs, wk)
                tt(w_(12), rc, rc, ALU.mult)
                link(tt(w_(13), rs, rs, ALU.mult))
                link(tt(w_(12), w_(12), w_(13), ALU.add))
                link(ts(w_(12), w_(12), -0.5, 1.5, ALU.mult, ALU.add))
                tt(rc, rc, w_(12), ALU.mult)
                link(tt(rs, rs, w_(12), ALU.mult))

            def sCW_flat(i):
                return ar(4768 + 576 * i, 512)

            def s5_piece(p):
                pairs = slice(PIECE * p, PIECE * (p + 1))
                if p:
                    dve.wait_ge(S("W2_stored"), 16 * p)
                    dve.wait_ge(*is_filled(f"k1_{p - 1}"))
                def power(w, n, m):
                    a = spw[:, w, 0:n, pairs].rearrange("p k g -> p g k")
                    return a.unsqueeze(3).broadcast_to([P, PIECE, n, m])
                def channel(a, n):
                    return a.unsqueeze(2).broadcast_to([P, PIECE, n, S5_M])
                v = [st[i].rearrange("p (g k m) -> p g k m", g=PIECE, k=TAU + 1) for i in range(2)]
                c_re, c_im = channel(sbc[:, 2, pairs, :], TAU + 1), channel(sbc[:, 3, pairs, :], TAU + 1)
                p_re, p_im = power(0, TAU + 1, S5_M), power(1, TAU + 1, S5_M)
                tt(v[0], c_re, p_re, ALU.mult)
                link(tt(v[1], c_im, p_im, ALU.mult))
                link(tt(sCW[:, :, 0, :, :], v[0], v[1], ALU.subtract))
                tt(v[0], c_re, p_im, ALU.mult)
                link(tt(v[1], c_im, p_re, ALU.mult))
                dve.scalar_tensor_tensor(out=sCW[:, :, 1, :, :], in0=v[0], scalar=-1.0, in1=v[1], op0=ALU.mult, op1=ALU.subtract)\
                   .then_inc(S("s5_cw"), 1)
                dve.wait_ge(S("s5_cw"), p + 1)
                v = [st[i][:, 0:512].rearrange("p (g k m) -> p g k m", g=PIECE, k=TAU) for i in range(2)]
                b_re, b_im = channel(sbb[:, 0, pairs, :], TAU), channel(sbb[:, 1, pairs, :], TAU)
                p_re, p_im = power(0, TAU, S5_M), power(1, TAU, S5_M)
                tt(v[0], b_re, p_re, ALU.mult)
                link(tt(v[1], b_im, p_im, ALU.mult))
                link(tt(sW1T[:, 0, :, :, :], v[0], v[1], ALU.subtract))
                tt(v[0], b_re, p_im, ALU.mult)
                link(tt(v[1], b_im, p_re, ALU.mult))
                tt(sW1T[:, 1, :, :, :], v[0], v[1], ALU.add).then_inc(S("s5_w1t"), 1)
                dve.wait_ge(S("s5_w1t"), p + 1)

            for what, n, *rest in ffn_order:
                if what == "split":
                    ffn_weights_rest(n)
                elif what == "hidden":
                    name, count = f"f{n}_{rest[0]}", 2 * n + rest[0]
                    dve.wait_ge(S("gated"), count + 1)
                    dve.tensor_tensor(fg[rest[0]], fg[rest[0]], bank(name)[:, T:2 * T], ALU.mult).then_inc(S("hidden"), 1)
                    dve.wait_ge(S("hidden"), count + 1)
                    dve.sem_inc(read(name), 1)
                elif what == "split_hidden":
                    dve.wait_ge(S("hidden_high"), 2 * n + rest[0] + 1)
                    dve.tensor_tensor(fh_low[n % 2][:, rest[0], :], fg[rest[0]], in_float32(fh_high[n % 2][:, rest[0], :]), ALU.subtract)\
                       .then_inc(S("hidden_low"), 1)
                elif n == 0:
                    s5_angles()
                    s5_powers()
                elif n == 1:
                    s5_input_map()
                elif n < PIECES + 2:
                    s5_piece(n - 2)
            for b in range(4):
                add_to_x(f"fo{b}", b)

            norm_of_x("norm_mix1", "mix1", permuted=True)
            for table in ("W1", "W2", "K"):
                dve.wait_ge(S(f"{table}_stored"), 16 * PIECES)
            cos_, sin_ = rot[:, 0, :, :], rot[:, 1, :, :]
            dve.memset(cos_[:, :, 0:1], 1.0)
            link(dve.memset(sin_[:, :, 0:1], 0.0))
            e_re, e_im = ar(11264, 32), ar(11296, 32)
            link(dve.tensor_copy(ar(11264, 64), ar(ARENA - 128, 64)))
            n = 1
            while n < BLOCKS:
                bro = lambda v: v.rearrange("p (g o) -> p g o", o=1).broadcast_to([P, PAIRS, n])
                tmp = [ar(9216 + 512 * i, PAIRS * n).rearrange("p (g j) -> p g j", g=PAIRS) for i in range(4)]
                product(cos_[:, :, n:2 * n], sin_[:, :, n:2 * n], cos_[:, :, 0:n], sin_[:, :, 0:n], bro(e_re), bro(e_im), tmp)
                product(e_re, e_im, e_re, e_im, e_re, e_im, [ar(11328 + 32 * i, 32) for i in range(4)])
                n *= 2
            link(dve.tensor_copy(rho, s5rot[:, 2, :].rearrange("p (g o) -> p g o", o=1).broadcast_to([P, PAIRS, BLOCKS])))
            link(dve.memset(rho[:, :, 0:1], 0.0))
            for w in range(2):
                for half in range(2):
                    dve.wait_ge(*was_read(f"Z{w}{half}"))
            c1, s1 = cos_.rearrange("p g j -> p (g j)"), sin_.rearrange("p g j -> p (g j)")
            flat_x = ar(11264, 2048).rearrange("p (w g) -> p w g", w=2)
            tt(t2[:, 0, :], Z[:, 0, :], c1, ALU.mult)
            tt(t2[:, 1, :], Z[:, 1, :], c1, ALU.mult)
            tt(flat_x[:, 0, :], Z[:, 1, :], s1, ALU.mult)
            link(tt(flat_x[:, 1, :], Z[:, 0, :], s1, ALU.mult))
            tt(t2[:, 0, :], t2[:, 0, :], flat_x[:, 0, :], ALU.add)
            link(tt(t2[:, 1, :], t2[:, 1, :], flat_x[:, 1, :], ALU.subtract))
            r1 = rho.rearrange("p g j -> p (g j)")
            dve.tensor_tensor_scan(Z[:, 0, :], r1, t2[:, 0, :], 0.0, ALU.mult, ALU.add)
            link(dve.tensor_tensor_scan(Z[:, 1, :], r1, t2[:, 1, :], 0.0, ALU.mult, ALU.add))
            j3 = lambda a: a.rearrange("p (g j) -> p g j", j=BLOCKS)[:, :, 0:BLOCKS - 1]
            tt(t2[:, 0, :], Z[:, 0, :], c1, ALU.mult)
            link(tt(t2[:, 1, :], Z[:, 1, :], s1, ALU.mult))
            dve.wait_ge(S("states_zero"), 2)

            def states(w, op):
                for group in range(2):
                    rows = slice(S5_P * group, S5_P * (group + 1))
                    last = tt(Xs[w][rows, :, group, 1:BLOCKS], j3(t2[rows, 0, :]), j3(t2[rows, 1, :]), op)
                return last

            link(states(0, ALU.subtract))
            tt(t2[:, 0, :], Z[:, 0, :], s1, ALU.mult)
            link(tt(t2[:, 1, :], Z[:, 1, :], c1, ALU.mult))
            states(1, ALU.add).then_inc(S("states"), 1)
            dense_weights_rest(group_start["glu0"])
            for n in range(KT):
                if n % 4 == 0:
                    dve.wait_ge(S(f"y_loaded{n // 4}"), 16)
                dve.scalar_tensor_tensor(out=yT[:, n, :], in0=uT[:, n, :], scalar=pc("s5_d", n), in1=yT[:, n, :],
                                         op0=ALU.mult, op1=ALU.add).then_inc(S("y_skipped"), 1)
            rest_of_h("glu", 1, range(KT))
            for c in range(4):
                dense_weights_rest(served[f"val{c}"])
                dense_weights_rest(served[f"gate{c}"])
                dve.wait_ge(*was_read(f"gate{c}"))
                link(tt(sg[c % 2], sg[c % 2], bank(f"val{c}")[:, :], ALU.mult))
                v = x[:, 2 * c:2 * c + 2, :].rearrange("p n (j s) -> p n j s", s=TAU)
                dve.tensor_tensor(v, v, sg[c % 2].rearrange("p (n s j) -> p n j s", n=2, s=TAU), ALU.add).then_inc(S("x_written"), 1)
                x_written[0] += 1
                dve.wait_ge(S("x_written"), x_written[0])
                dve.sem_inc(read(f"val{c}"), 1)
            cross_attention(1)

            def weights_rest(i, n):
                _, high_part, words, rest = granule(*GRANULES[n])
                dve.wait_ge(S("weights_high"), i * N_GRANULES + n + 1)
                dve.tensor_tensor(rest, words, in_float32(high_part), ALU.subtract).then_inc(S("weights_low"), 1)

            norm_of_x("norm_ffn1", "ffn1")
            for n in range(3):
                weights_rest(0, n)
            dve.wait_ge(*is_filled("logits"))
            dve.tensor_copy(lgt, bank("logits")[:, 0:16].rearrange("p (c e) -> p c e", c=2)).then_inc(read("logits"), 1)
            dve.wait_ge(*was_read("logits"))
            wide = [P, 2, EXPERTS, EXPERTS]
            mine, other = lgt.unsqueeze(3).broadcast_to(wide), lgt.unsqueeze(2).broadcast_to(wide)
            number = con[:, CONST_COLS["slots"], 0:EXPERTS]
            sq8 = [P, EXPERTS, EXPERTS]
            link(tt(cmpA[:, 0], number.unsqueeze(2).broadcast_to(sq8), number.unsqueeze(1).broadcast_to(sq8), ALU.is_gt))
            link(tt(cmpB, other, mine, ALU.is_equal))
            link(tt(cmpB, cmpB, cmpA[:, 0:1].broadcast_to(wide), ALU.mult))
            link(tt(cmpA, other, mine, ALU.is_gt))
            link(tt(cmpA, cmpA, cmpB, ALU.add))
            link(dve.tensor_reduce(sel, cmpA, AX.X, ALU.add))
            dve.tensor_reduce(gm[:, 0:2], lgt, AX.X, ALU.max)
            dve.tensor_scalar(sel, sel, 1.5, None, ALU.is_lt).then_inc(S("selected"), 1)
            dve.wait_ge(S("selected"), 1)
            dve.tensor_tensor(lgt, lgt, gm[:, 0:2].unsqueeze(2).broadcast_to([P, 2, EXPERTS]), ALU.subtract).then_inc(S("logits_less_max"), 1)
            dve.wait_ge(S("gate_exp"), 1)
            link(tt(gw, gw, sel, ALU.mult))
            link(dve.tensor_reduce(gm[:, 0:2], gw, AX.X, ALU.add))
            link(dve.reciprocal(gm[:, 2:4], gm[:, 0:2]))
            link(dve.memset(PG, -FAR))
            tt(PG[:, :, 1, 0:EXPERTS], gw, gm[:, 2:4].unsqueeze(2).broadcast_to([P, 2, EXPERTS]), ALU.mult)
            dve.wait_ge(*is_filled("places"))
            dve.tensor_reduce(cnt[:, 8:9], bank("places")[:, 16:24], AX.X, ALU.max)
            link(dve.tensor_copy(PG[:, :, 0, 0:EXPERTS], bank("places")[:, 0:16].rearrange("p (c e) -> p c e", c=2)))
            dve.tensor_copy(flag[0:1, 0:1], cnt[0:1, 8:9]).then_inc(read("places"), 1)
            dve.wait_ge(*was_read("places"))
            dve.sem_inc(S("flag_ready"), 1)
            pl = PG[:, :, 0, 0:EXPERTS]
            link(ts(pl, pl, FAR, None, ALU.add))
            link(tt(pl, pl, sel, ALU.mult))
            link(ts(pl, pl, -FAR, None, ALU.add))
            slots = con[:, CONST_COLS["slots"], :]

            def take_slots(e, i):
                dve.tensor_copy(pick, PG[:, :, :, bass.ds(e, 1)].rearrange("p c w o -> p c (w o)")).then_inc(S("picked"), 1)
                dve.wait_ge(S("picked"), i + 1)
                for c in range(2):
                    dve.tensor_scalar(Gs[:, c, :], slots, pick[:, c, 0:1], None, ALU.is_equal)
                    last = dve.tensor_scalar(Gg[:, c, :], slots, pick[:, c, 0:1], pick[:, c, 1:2], ALU.is_equal, ALU.mult)
                last.then_inc(S("slots_ready"), 1)

            def rows_rest(i):
                for b in range(2):
                    v = slice(4 * b, 4 * b + 4)
                    dve.wait_ge(S("gather_copied"), 2 * i + b + 1)
                    dve.tensor_tensor(hc_low[:, v, :], ps[6 + b][:, :].rearrange("p (k c) -> p k c", k=4), in_float32(hc[:, v, :]), ALU.subtract)\
                       .then_inc(S("gather_split"), 1)

            def expert(e, i, rnd, last=False):
                for n in range(3, 6):
                    weights_rest(i, n)
                for n in range(STEPS + 1):
                    ahead = list(split_ahead(n))
                    if n < STEPS:
                        dve.wait_ge(S("moe_gated"), i * STEPS + n + 1)
                        dve.wait_ge(S("hidden_turned"), (i + 1) * STEPS + n - 1)
                        dve.tensor_tensor(hid[n % 2], sil[n % 2], ps[n % 2][:, STEP:2 * STEP], ALU.mult).then_inc(S("moe_hidden"), 1)
                    for q in ahead[:2]:
                        weights_rest(i, q)
                    if n == STEPS and not last:
                        weights_rest(i + 1, 0)
                    if n >= 1:
                        dve.wait_ge(S("hidden_copied"), i * STEPS + n)
                        b = (n - 1) % 2
                        dve.tensor_tensor(hidT_low[b], ps[2][:, 0:T].rearrange("p (j c) -> p j c", j=2), in_float32(hidT[b]), ALU.subtract)\
                           .then_inc(S("hidden_split"), 1)
                    for q in ahead[2:]:
                        weights_rest(i, q)
                    if n == 2 and not last:
                        dve.wait_ge(S("gates_turned"), i + 1)
                        take_slots(e + 1, i + 1 + rnd)
                if not last:
                    rows_rest(i + 1)
                    weights_rest(i + 1, 1)
                for m in range(4):
                    dve.wait_ge(S("scattered"), i * 4 + m + 1)
                    v = flat(x[:, 2 * m:2 * m + 2, :])
                    dve.wait_ge(S("moe_added"), i * 4 + m + 4)
                    dve.tensor_tensor(v, v, ps[6 + m % 2][:, :], ALU.add).then_inc(S("moe_added"), 1)
                if not last:
                    weights_rest(i + 1, 2)

            def experts(rnd):
                first = EXPERTS * rnd
                take_slots(0, first + rnd)
                if first:
                    for n in range(3):
                        weights_rest(first, n)
                rows_rest(first)
                with dve.Fori(0, EXPERTS - 1) as e:
                    expert(e, e + first if first else e, rnd)
                expert(EXPERTS - 1, first + EXPERTS - 1, rnd, last=True)

            experts(0)
            busiest = dve.value_load(flag[0:1, 0:1], min_val=0, max_val=T)
            with dve.If(busiest > P):
                dve.wait_ge(S("slots_ready"), EXPERTS)
                dve.tensor_scalar(pl, pl, -float(P), None, ALU.add).then_inc(S("picked"), 1)
                dve.wait_ge(S("picked"), EXPERTS + 1)
                experts(1)
                dve.wait_ge(S("moe_added"), 8 * EXPERTS + 4)
            dve.wait_ge(S("moe_added"), 4 * EXPERTS + 4)
            dve.sem_inc(S("x_written"), 4)
            norm_of_x("norm_fin", "fin")


def channel_major(a):
    return np.ascontiguousarray(a.T.reshape(-1, P, a.shape[0]).transpose(1, 0, 2))


def column_chunks(w, width=512):
    k, n = w.shape
    return w.reshape(k // P, P, n // width, width).transpose(2, 1, 0, 3).reshape(n // width, P, k // P * width)


def step_chunks(w13, w2, by_granule=False):
    if by_granule:
        w13 = w13.reshape(KT, P, 2, STEPS, 2, P).transpose(3, 1, 4, 2, 0, 5).reshape(STEPS, P, DENSE)
    else:
        w13 = w13.reshape(KT, P, 2, STEPS, STEP).transpose(3, 1, 0, 2, 4).reshape(STEPS, P, DENSE)
    w2 = w2.reshape(STEPS, 2, P, D).transpose(0, 2, 1, 3).reshape(STEPS, P, SLOT - DENSE)
    return np.concatenate([w13, w2], 2)


def param_table(a):
    out = np.zeros((P, N_PARAM), np.float32)

    def put(name, v, rows=P):
        c0, w = PARAM_COLS[name]
        out[0:rows, c0:c0 + w] = np.asarray(v).reshape(w, rows).T

    for i in range(2):
        put(f"mix{i}", a["mix_norm_g"][i])
        put(f"xat{i}", a["xattn_norm_g"][i])
        put(f"ffn{i}", a["ffn_norm_g"][i])
    put("memg", a["mem_norm_g"])
    put("fin", a["final_norm_g"])
    put("s5_d", a["s5_d"][0])
    mu = a["rw_mu"][0]
    for i, name in enumerate(("mu_r", "mu_k", "mu_v")):
        put(name, mu[512 * i:512 * (i + 1)])
    put("mu_wd", mu[1536:1568], 32)
    put("mu_ad", mu[1568:1600], 32)
    put("mu_gd", mu[1600:1696], 96)
    for name in ("w0", "a0", "k_k", "k_a", "gn_g", "gn_b", "r_k"):
        put(name, a["rw_" + name][0].reshape(-1))
    put("onorm", a["hg_onorm_g"][0])
    put("lb", a["hg_lb_logits"][0])
    return out


def host_arrays(a):
    a = {k: np.asarray(v) for k, v in a.items()}
    w_in = a["ab_w_in"][0]
    hgrn, rwkv = w_in[:, :2048], w_in[:, 2048:]
    kv0 = a["xa_wkv"][0]
    glu = a["c_w_glu"][0]
    glu = np.concatenate([glu[:, :D].reshape(D, 4, 256), glu[:, D:].reshape(D, 4, 256)], 2).reshape(D, 2 * D)
    kv1 = a["xa_wkv"][1]
    dense = [rwkv[:, :1536], hgrn, kv0, a["ab_w_out"][0], a["xa_wq"][0], a["xa_wo"][0], a["c_w_in"][0], kv1, glu,
             a["xa_wq"][1], a["xa_wo"][1]]
    dense = [column_chunks(w) for w in dense]
    s5 = lambda name: a["s5_" + name][0].reshape((PAIRS, P) + a["s5_" + name][0].shape[2:])
    s5a = np.stack([s5("a_re").T, s5("a_im").T, np.repeat(a["s5_log_dt"][0].reshape(PAIRS, 2), S5_P, 1).T], 1)
    c_by_state = lambda name: a["s5_" + name][0].transpose(0, 2, 1).reshape(PAIRS, P, S5_M)
    s5bc = np.stack([v.transpose(1, 0, 2) for v in (s5("b_re"), s5("b_im"), c_by_state("c_re"), c_by_state("c_im"))], 1)
    small = np.zeros((P, 3, 512), np.float32)
    small[:32, 0], small[:32, 1], small[:96, 2] = a["rw_w2"][0], a["rw_a2"][0], a["rw_g2"][0]
    return {
        "x": channel_major(a["x"][0]), "mem": channel_major(a["mem"][0]), "con": shape_constants(), "par": param_table(a),
        "lora": column_chunks(rwkv[:, 1536:], 160)[0], "dense": np.concatenate(dense), "smallw": small.reshape(P, -1),
        "ffn": step_chunks(a["ffn_w13"][0], a["ffn_w2"][0], by_granule=True),
        "moe": np.stack([step_chunks(w13, w2) for w13, w2 in zip(a["moe_w13"][0], a["moe_w2"][0])]),
        "s5a": s5a.reshape(P, -1), "s5bc": s5bc.reshape(P, -1),
        "router": a["moe_router"][0].reshape(KT, P, EXPERTS).transpose(1, 0, 2).reshape(P, -1),
    }


def kernel(**inputs):
    import concourse.bacc as bacc
    from concourse.bass_utils import run_bass_kernel_spmd

    nc = bacc.Bacc("TRN2", target_bir_lowering=False, num_devices=1)
    arrays = {name: np.ascontiguousarray(v) for name, v in host_arrays(inputs).items()}
    aps = {name: nc.dram_tensor(name + "_dram", v.shape, mybir.dt.from_np(v.dtype), kind="ExternalInput").ap()
           for name, v in arrays.items()}
    out = nc.dram_tensor("out_dram", (P, KT, T), F32, kind="ExternalOutput").ap()
    build_trunk(nc, aps, out)
    r = run_bass_kernel_spmd(nc, [{name + "_dram": v for name, v in arrays.items()}], core_ids=[0])
    y = r.results[0]["out_dram"]
    return np.ascontiguousarray(y.transpose(2, 1, 0).reshape(1, T, D))
```
